# Optimizing a Trainium2 kernel written in Bass

```python
import math
import jax, jax.numpy as jnp
from jax import lax
import numpy as np

D_MODEL = 1024
BATCH = 1
SEQ = 512
DEPTH = 1

N_META = 16
ATT_HEADS = 4
ATT_HEAD_DIM = 64
ATT_V_DIM = 2 * ATT_HEAD_DIM
REC_HEADS = 4
REC_DK = 128
REC_DV = 128
ATT_WIDTH = ATT_HEADS * ATT_V_DIM
REC_WIDTH = REC_HEADS * REC_DV
MIX_WIDTH = ATT_WIDTH + REC_WIDTH
COL_SIZES = (
    ATT_HEADS * 2 * ATT_HEAD_DIM,
    ATT_HEADS * 2 * ATT_HEAD_DIM,
    ATT_WIDTH,
    REC_HEADS * REC_DK,
    REC_HEADS * REC_DK,
    REC_WIDTH,
    REC_WIDTH,
)
IN_COLS = sum(COL_SIZES)
SPLIT_POINTS = tuple(int(v) for v in np.cumsum(COL_SIZES)[:-1])
Q_BLOCK = 128
REC_CHUNK = 64
ROPE_THETA = 10000.0
PEER_HEADS = 8
PEER_QUERY_DIM = 256
N_KEYS = 128
N_EXPERTS = N_KEYS * N_KEYS
PEER_TOPK = 16
PEER_BLOCK = 128
EPS = 1e-6


def rmsnorm(x, w):
    xf = x.astype(jnp.float32)
    y = xf * lax.rsqrt(jnp.mean(xf * xf, axis=-1, keepdims=True) + EPS)
    return (y * w.astype(jnp.float32)).astype(x.dtype)

def rope_tables(T, d):
    inv_freq = ROPE_THETA ** (-jnp.arange(0, d, 2, dtype=jnp.float32) / d)
    ang = jnp.arange(T, dtype=jnp.float32)[:, None] * inv_freq[None, :]
    ang = jnp.concatenate([ang, ang], axis=-1)
    return jnp.cos(ang), jnp.sin(ang)

def apply_rope(z, cos, sin):
    half = z.shape[-1] // 2
    rot = jnp.concatenate([-z[..., half:], z[..., :half]], axis=-1)
    return (z * cos.astype(z.dtype) + rot * sin.astype(z.dtype)).astype(z.dtype)

def lambda_init(layer_idx):
    return 0.8 - 0.6 * math.exp(-0.3 * layer_idx)

def diff_attention(aq, ak, av, lq1, lk1, lq2, lk2, subln_w, lam_init, cos, sin):
    B, T, _ = aq.shape
    q = apply_rope(aq.reshape(B, T, ATT_HEADS, 2, ATT_HEAD_DIM).transpose(3, 0, 2, 1, 4), cos, sin)
    k = apply_rope(ak.reshape(B, T, ATT_HEADS, 2, ATT_HEAD_DIM).transpose(3, 0, 2, 1, 4), cos, sin)
    v = av.reshape(B, T, ATT_HEADS, ATT_V_DIM).transpose(0, 2, 1, 3)
    q = q * (ATT_HEAD_DIM ** -0.5)
    lam = (jnp.exp(jnp.sum(lq1.astype(jnp.float32) * lk1.astype(jnp.float32)))
           - jnp.exp(jnp.sum(lq2.astype(jnp.float32) * lk2.astype(jnp.float32))) + lam_init)
    neg = jnp.finfo(jnp.float32).min

    def block(q_blk, k_blk, v_blk, q_start):
        nq, nk = q_blk.shape[-2], k_blk.shape[-2]
        mask = jnp.arange(nk)[None, :] <= (q_start + jnp.arange(nq))[:, None]
        s = jnp.einsum('pbhqd,pbhkd->pbhqk', q_blk, k_blk).astype(jnp.float32)
        p = jax.nn.softmax(jnp.where(mask, s, neg), axis=-1)
        w = p[0] - lam * p[1]
        return jnp.einsum('bhqk,bhkv->bhqv', w.astype(v_blk.dtype), v_blk)

    outs = [block(q[..., :N_META, :], k[..., :N_META, :], v[:, :, :N_META], 0)]
    for i in range((T - N_META) // Q_BLOCK):
        s0 = N_META + i * Q_BLOCK
        e0 = s0 + Q_BLOCK
        outs.append(block(q[..., s0:e0, :], k[..., :e0, :], v[:, :, :e0], s0))
    o = jnp.concatenate(outs, axis=2)
    o = rmsnorm(o, subln_w) * (1.0 - lam_init)
    return o.transpose(0, 2, 1, 3).reshape(B, T, ATT_WIDTH)

def gla_chunk(S, q, k, v, g):
    C = q.shape[2]
    cum = jnp.cumsum(g, axis=2)
    inter = jnp.einsum('bhtc,bhcv->bhtv', q * jnp.exp(cum), S)
    causal = jnp.tril(jnp.ones((C, C), dtype=bool))[:, :, None]
    diff = cum[:, :, :, None, :] - cum[:, :, None, :, :]
    decay = jnp.where(causal, jnp.exp(jnp.where(causal, diff, 0.0)), 0.0)
    A = jnp.einsum('bhtc,bhsc,bhtsc->bhts', q, k, decay)
    intra = jnp.einsum('bhts,bhsv->bhtv', A, v)
    last = cum[:, :, -1]
    S_new = (jnp.exp(last)[..., None] * S
             + jnp.einsum('bhsc,bhsv->bhcv', k * jnp.exp(last[:, :, None, :] - cum), v))
    return S_new, inter + intra

def hgrn2(rq, rf, ri, rg, lb, norm_w):
    B, T, _ = rq.shape

    def heads(z, d):
        return z.reshape(B, T, REC_HEADS, d).transpose(0, 2, 1, 3).astype(jnp.float32)

    q = jax.nn.silu(heads(rq, REC_DK))
    lbh = lb.reshape(REC_HEADS, 1, REC_DK)
    f = lbh + (1.0 - lbh) * jax.nn.sigmoid(heads(rf, REC_DK))
    k = 1.0 - f
    g = jnp.log(f)
    v = heads(ri, REC_DV)
    S0 = jnp.zeros((B, REC_HEADS, REC_DK, REC_DV), jnp.float32)
    S_meta, o_meta = gla_chunk(S0, q[:, :, :N_META], k[:, :, :N_META], v[:, :, :N_META], g[:, :, :N_META])
    n_chunks = (T - N_META) // REC_CHUNK

    def to_chunks(z):
        z = z[:, :, N_META:].reshape(B, REC_HEADS, n_chunks, REC_CHUNK, z.shape[-1])
        return z.transpose(2, 0, 1, 3, 4)

    _, o_real = lax.scan(lambda S, xs: gla_chunk(S, *xs), S_meta,
                         (to_chunks(q), to_chunks(k), to_chunks(v), to_chunks(g)))
    o_real = o_real.transpose(1, 2, 0, 3, 4).reshape(B, REC_HEADS, T - N_META, REC_DV)
    o = jnp.concatenate([o_meta, o_real], axis=2)
    o = rmsnorm(o, norm_w[:, None, :])
    o = o.transpose(0, 2, 1, 3).reshape(B, T, REC_WIDTH) * jax.nn.silu(rg.astype(jnp.float32))
    return o.astype(rq.dtype)

def token_mix(a, w_in, lb, rec_norm_w, lq1, lk1, lq2, lk2, subln_w, w_out, lam_init, cos, sin):
    proj = jnp.einsum('btd,dc->btc', a, w_in)
    aq, ak, av, rq, rf, ri, rg = jnp.split(proj, SPLIT_POINTS, axis=-1)
    att = diff_attention(aq, ak, av, lq1, lk1, lq2, lk2, subln_w, lam_init, cos, sin)
    rec = hgrn2(rq, rf, ri, rg, lb, rec_norm_w)
    mixed = jnp.concatenate([att, rec.astype(att.dtype)], axis=-1)
    return jnp.einsum('btc,cd->btd', mixed, w_out)

def peer_ffn(h, w_query, subkeys, u_table, v_table):
    B, T, D = h.shape
    n = B * T
    pad = (-n) % PEER_BLOCK
    blocks = jnp.pad(h.reshape(n, D), ((0, pad), (0, 0))).reshape(-1, PEER_BLOCK, D)

    def one_block(xb):
        q = jnp.einsum('nd,dc->nc', xb, w_query).reshape(PEER_BLOCK, PEER_HEADS, 2, PEER_QUERY_DIM // 2)
        s = jnp.einsum('nhpc,hpkc->nhpk', q, subkeys).astype(jnp.float32)
        sv, si = lax.top_k(s, PEER_TOPK)
        cand_s = (sv[:, :, 0, :, None] + sv[:, :, 1, None, :]).reshape(PEER_BLOCK, PEER_HEADS, PEER_TOPK * PEER_TOPK)
        cand_i = (si[:, :, 0, :, None] * N_KEYS + si[:, :, 1, None, :]).reshape(PEER_BLOCK, PEER_HEADS, PEER_TOPK * PEER_TOPK)
        top_s, pos = lax.top_k(cand_s, PEER_TOPK)
        experts = jnp.take_along_axis(cand_i, pos, axis=-1).reshape(PEER_BLOCK, PEER_HEADS * PEER_TOPK)
        gates = jax.nn.softmax(top_s, axis=-1).reshape(PEER_BLOCK, PEER_HEADS * PEER_TOPK)
        u = u_table[experts]
        hid = jax.nn.gelu(jnp.einsum('nkd,nd->nk', u, xb).astype(jnp.float32), approximate=False) * gates
        return jnp.einsum('nk,nkd->nd', hid.astype(xb.dtype), v_table[experts])

    y = lax.map(one_block, blocks).reshape(-1, D)[:n]
    return y.reshape(B, T, D)

def first_inputs(seed: int = 0) -> dict:
    key = jax.random.key(seed)
    ks = jax.random.split(key, 18)
    nrm = jax.random.normal
    f32 = jnp.float32
    return {
        "x": nrm(ks[0], (BATCH, SEQ, D_MODEL), f32),
        "meta_tokens": nrm(ks[1], (N_META, D_MODEL), f32),
        "mix_norm_w": 1.0 + 0.02 * nrm(ks[2], (DEPTH, D_MODEL), f32),
        "w_in": nrm(ks[3], (DEPTH, D_MODEL, IN_COLS), f32) * D_MODEL ** -0.5,
        "rec_lb_logits": 0.5 * nrm(ks[4], (DEPTH + 1, REC_HEADS * REC_DK), f32),
        "rec_norm_w": 1.0 + 0.02 * nrm(ks[5], (DEPTH, REC_HEADS, REC_DV), f32),
        "diff_lambda_q1": 0.1 * nrm(ks[6], (DEPTH, ATT_HEAD_DIM), f32),
        "diff_lambda_k1": 0.1 * nrm(ks[7], (DEPTH, ATT_HEAD_DIM), f32),
        "diff_lambda_q2": 0.1 * nrm(ks[8], (DEPTH, ATT_HEAD_DIM), f32),
        "diff_lambda_k2": 0.1 * nrm(ks[9], (DEPTH, ATT_HEAD_DIM), f32),
        "diff_subln_w": 1.0 + 0.02 * nrm(ks[10], (DEPTH, ATT_V_DIM), f32),
        "w_out": nrm(ks[11], (DEPTH, MIX_WIDTH, D_MODEL), f32) * MIX_WIDTH ** -0.5,
        "ffn_norm_w": 1.0 + 0.02 * nrm(ks[12], (DEPTH, D_MODEL), f32),
        "peer_w_query": nrm(ks[13], (DEPTH, D_MODEL, PEER_HEADS * PEER_QUERY_DIM), f32) * D_MODEL ** -0.5,
        "peer_subkeys": nrm(ks[14], (DEPTH, PEER_HEADS, 2, N_KEYS, PEER_QUERY_DIM // 2), f32) * (PEER_QUERY_DIM // 2) ** -0.5,
        "peer_u": nrm(ks[15], (DEPTH, N_EXPERTS, D_MODEL), f32) * D_MODEL ** -0.5,
        "peer_v": nrm(ks[16], (DEPTH, N_EXPERTS, D_MODEL), f32) * PEER_HEADS ** -0.5,
        "final_norm_w": 1.0 + 0.02 * nrm(ks[17], (D_MODEL,), f32),
    }

def first_block(x, meta_tokens, mix_norm_w, w_in, rec_lb_logits, rec_norm_w,
              diff_lambda_q1, diff_lambda_k1, diff_lambda_q2, diff_lambda_k2,
              diff_subln_w, w_out, ffn_norm_w, peer_w_query, peer_subkeys,
              peer_u, peer_v, final_norm_w):
    B = x.shape[0]
    T = N_META + x.shape[1]
    meta = jnp.broadcast_to(meta_tokens[None].astype(x.dtype), (B, N_META, D_MODEL))
    h = jnp.concatenate([meta, x], axis=1)
    cos, sin = rope_tables(T, ATT_HEAD_DIM)
    lb_all = jnp.cumsum(jax.nn.softmax(rec_lb_logits.astype(jnp.float32), axis=0), axis=0)
    for l in range(DEPTH):
        a = rmsnorm(h, mix_norm_w[l])
        h = h + token_mix(a, w_in[l], lb_all[l], rec_norm_w[l],
                          diff_lambda_q1[l], diff_lambda_k1[l], diff_lambda_q2[l], diff_lambda_k2[l],
                          diff_subln_w[l], w_out[l], lambda_init(l), cos, sin).astype(h.dtype)
        if l == DEPTH - 1:
            h = h[:, N_META:]
        h = h + peer_ffn(rmsnorm(h, ffn_norm_w[l]), peer_w_query[l], peer_subkeys[l],
                         peer_u[l], peer_v[l]).astype(h.dtype)
    return rmsnorm(h, final_norm_w)


CHUNK = 64
N_HEADS_SB = 8
HEAD_DIM_SB = 64
D_SB = N_HEADS_SB * HEAD_DIM_SB
N_GROUPS_SGU = 8
GROUP_DIM_SGU = 64
D_SGU = N_GROUPS_SGU * GROUP_DIM_SGU
SGU_CHUNK = 128
IN_WIDTHS = (D_SB, D_SB, D_SB, D_SB, D_SGU, D_SGU, D_SGU, D_MODEL, D_MODEL)
D_IN = 4 * D_SB + 3 * D_SGU + 2 * D_MODEL


def rmsnorm_2(x, g):
    xf = x.astype(jnp.float32)
    y = xf * lax.rsqrt(jnp.mean(xf * xf, axis=-1, keepdims=True) + EPS)
    return (y * g.astype(jnp.float32)).astype(x.dtype)

def split_points():
    pts, acc = [], 0
    for w in IN_WIDTHS[:-1]:
        acc += w
        pts.append(acc)
    return pts

def stick_breaking_attention(q, k, v):
    b, s, h, dh = q.shape
    scale = dh ** -0.5
    qf = q.astype(jnp.float32).transpose(0, 2, 1, 3) * scale
    kf = k.astype(jnp.float32).transpose(0, 2, 1, 3)
    vf = v.astype(jnp.float32).transpose(0, 2, 1, 3)
    outs = []
    for start in range(0, s, Q_BLOCK):
        end = start + Q_BLOCK
        qb = qf[:, :, start:end]
        kb = kf[:, :, :end]
        vb = vf[:, :, :end]
        z = jnp.einsum('bhqd,bhkd->bhqk', qb, kb)
        t_idx = start + jnp.arange(Q_BLOCK)[:, None]
        s_idx = jnp.arange(end)[None, :]
        before = s_idx < t_idx
        log_keep = jnp.where(before, jax.nn.log_sigmoid(-z), 0.0)
        log_stick = lax.cumsum(log_keep, axis=3, reverse=True) - log_keep
        log_w = jax.nn.log_sigmoid(z) + log_stick
        w = jnp.where(before, jnp.exp(log_w), 0.0)
        outs.append(jnp.einsum('bhqk,bhkd->bhqd', w, vb))
    o = jnp.concatenate(outs, axis=2)
    return o.transpose(0, 2, 1, 3).astype(q.dtype)

def spatial_gating(u, v, ln_g, ln_b, w_s, b_s):
    b, s, g, c = v.shape
    vf = v.astype(jnp.float32)
    mu = jnp.mean(vf, axis=-1, keepdims=True)
    var = jnp.mean(jnp.square(vf - mu), axis=-1, keepdims=True)
    vn = (vf - mu) * lax.rsqrt(var + EPS) * ln_g.astype(jnp.float32) + ln_b.astype(jnp.float32)
    vn = vn.reshape(b, s // SGU_CHUNK, SGU_CHUNK, g, c)
    pos = jnp.arange(SGU_CHUNK)
    mask = (pos[None, :] // CHUNK) <= (pos[:, None] // CHUNK)
    w = jnp.where(mask[None], w_s.astype(jnp.float32), 0.0)
    mixed = jnp.einsum('gts,bnsgc->bntgc', w, vn) + b_s.astype(jnp.float32).T[None, None, :, :, None]
    return u * mixed.reshape(b, s, g, c).astype(u.dtype)

def second_inputs(seed: int = 0) -> dict:
    key = jax.random.key(seed)
    ks = jax.random.split(key, 13)
    f32 = jnp.float32
    x = jax.random.normal(ks[0], (BATCH, SEQ, D_MODEL), f32)
    norm_g = 1.0 + 0.1 * jax.random.normal(ks[1], (DEPTH, D_MODEL), f32)
    w_in = jax.random.normal(ks[2], (DEPTH, D_MODEL, D_IN), f32) * D_MODEL ** -0.5
    sgu_ln_g = 1.0 + 0.1 * jax.random.normal(ks[3], (DEPTH, N_GROUPS_SGU, GROUP_DIM_SGU), f32)
    sgu_ln_b = 0.1 * jax.random.normal(ks[4], (DEPTH, N_GROUPS_SGU, GROUP_DIM_SGU), f32)
    w_spatial = jax.random.normal(ks[5], (DEPTH, N_GROUPS_SGU, SGU_CHUNK, SGU_CHUNK), f32) * SGU_CHUNK ** -0.5
    b_spatial = 1.0 + 0.1 * jax.random.normal(ks[6], (DEPTH, N_GROUPS_SGU, SGU_CHUNK), f32)
    w_up_a = jax.random.normal(ks[7], (DEPTH, D_SB, D_MODEL), f32) * D_SB ** -0.5
    w_up_b = jax.random.normal(ks[8], (DEPTH, D_SGU, D_MODEL), f32) * D_SGU ** -0.5
    w_out = jax.random.normal(ks[9], (DEPTH, D_MODEL, D_MODEL), f32) * D_MODEL ** -0.5
    final_norm_g = 1.0 + 0.1 * jax.random.normal(ks[10], (D_MODEL,), f32)
    return {'x': x, 'norm_g': norm_g, 'w_in': w_in, 'sgu_ln_g': sgu_ln_g, 'sgu_ln_b': sgu_ln_b,
            'w_spatial': w_spatial, 'b_spatial': b_spatial, 'w_up_a': w_up_a, 'w_up_b': w_up_b,
            'w_out': w_out, 'final_norm_g': final_norm_g}

def second_block(x, norm_g, w_in, sgu_ln_g, sgu_ln_b, w_spatial, b_spatial, w_up_a, w_up_b, w_out, final_norm_g):
    b, s, _ = x.shape
    pts = split_points()
    for l in range(DEPTH):
        h = rmsnorm_2(x, norm_g[l])
        proj = jnp.einsum('bsd,de->bse', h, w_in[l])
        q, k, v, z_a, u_b, v_b, z_b, g_a, g_b = jnp.split(proj, pts, axis=-1)
        y_a = stick_breaking_attention(
            q.reshape(b, s, N_HEADS_SB, HEAD_DIM_SB),
            k.reshape(b, s, N_HEADS_SB, HEAD_DIM_SB),
            v.reshape(b, s, N_HEADS_SB, HEAD_DIM_SB)).reshape(b, s, D_SB) * jax.nn.silu(z_a)
        y_b = spatial_gating(
            jax.nn.gelu(u_b).reshape(b, s, N_GROUPS_SGU, GROUP_DIM_SGU),
            jax.nn.gelu(v_b).reshape(b, s, N_GROUPS_SGU, GROUP_DIM_SGU),
            sgu_ln_g[l], sgu_ln_b[l], w_spatial[l], b_spatial[l]).reshape(b, s, D_SGU) * jax.nn.silu(z_b)
        p_a = jnp.einsum('bse,ed->bsd', y_a, w_up_a[l])
        p_b = jnp.einsum('bse,ed->bsd', y_b, w_up_b[l])
        merged = jax.nn.sigmoid(g_a) * p_a + jax.nn.sigmoid(g_b) * p_b
        x = x + jnp.einsum('bsd,de->bse', merged, w_out[l])
    return rmsnorm_2(x, final_norm_g)


def setup_inputs(seed=0):
    out = dict(first_inputs(seed))
    for name, value in second_inputs(seed + 1).items():
        if name != "x":
            out[name + "_2"] = value
    return out


def reference(
    x, meta_tokens, mix_norm_w, w_in, rec_lb_logits, rec_norm_w, diff_lambda_q1, diff_lambda_k1,
    diff_lambda_q2, diff_lambda_k2, diff_subln_w, w_out, ffn_norm_w, peer_w_query, peer_subkeys,
    peer_u, peer_v, final_norm_w, norm_g_2, w_in_2, sgu_ln_g_2, sgu_ln_b_2, w_spatial_2,
    b_spatial_2, w_up_a_2, w_up_b_2, w_out_2, final_norm_g_2,
):
    x = first_block(
        x, meta_tokens, mix_norm_w, w_in, rec_lb_logits, rec_norm_w, diff_lambda_q1,
        diff_lambda_k1, diff_lambda_q2, diff_lambda_k2, diff_subln_w, w_out, ffn_norm_w,
        peer_w_query, peer_subkeys, peer_u, peer_v, final_norm_w,
    )
    return second_block(
        x, norm_g_2, w_in_2, sgu_ln_g_2, sgu_ln_b_2, w_spatial_2, b_spatial_2, w_up_a_2,
        w_up_b_2, w_out_2, final_norm_g_2,
    )


_drawn_inputs = setup_inputs


def setup_inputs(seed=0):
    import zlib

    import numpy as np

    out = dict(_drawn_inputs(seed))
    spreads = {}
    factors = {'rec_norm_w': 9.238,
     'diff_lambda_k2': 5.903,
     'diff_subln_w': 2.716,
     'sgu_ln_g_2': 3.324,
     'sgu_ln_b_2': 3.339,
     'b_spatial_2': 2.982,
     'diff_lambda_q1': 2.971,
     'ffn_norm_w': 3.597}
    for name, (base, spread) in spreads.items():
        noise = np.random.default_rng([zlib.crc32(name.encode()), seed]).standard_normal(out[name].shape)
        drawn = base * np.exp(spread * noise) if base else spread * noise
        out[name] = __import__('jax').numpy.asarray(drawn.astype(out[name].dtype))
    for name, factor in factors.items():
        out[name] = (out[name] * factor).astype(out[name].dtype)
    return out
```

```python
from contextlib import ExitStack

import numpy as np
import concourse.bass as bass
from concourse import mybir

ALU = mybir.AluOpType
ACT = mybir.ActivationFunctionType
AXX = mybir.AxisListType.X
F32 = mybir.dt.float32
U32 = mybir.dt.uint32
I32 = mybir.dt.int32

P = 128
D = 1024
KT = D // P
SEQ = 512
NB = SEQ // P
NM = 16
T = NM + SEQ
W = 512
HA, DH = 4, 64
HR = 4
LEVELS = 7
HP = 8
NK = 128
TOP = 16
SLOTS = HP * TOP
RING = 8
H2, DH2 = 8, 64
NG, GC = 8, 64
EPS = 1e-6
NEG = -1e30
FMIN = -3.4028234663852886e38
LAM0 = 0.2
RA = RB = 3

CHUNKS = ["ak", "av", "rf", "ri", "aq", "rq", "rg", "o0", "o1", "p0", "p1", "p2", "p3",
          "q2", "k2", "v2", "za", "ub", "vb", "zb", "ga0", "ga1", "gb0", "gb1", "up0", "up1", "w0", "w1"]
WIN_AT = {"aq": 0, "ak": 1, "av": 2, "rq": 3, "rf": 4, "ri": 5, "rg": 6}
WIN2_AT = {n: i for i, n in enumerate(["q2", "k2", "v2", "za", "ub", "vb", "zb", "ga0", "ga1", "gb0", "gb1"])}

JOBS_A = [("ak", 5), ("av", 5), ("rf", 5), ("ri", 5), ("aq", 4), ("rq", 4), ("rg", 4)]
JOBS_B = [("trA", 10), ("rotk", 5), ("rotq", 4)]
for _b in range(NB):
    for _h in range(HA):
        JOBS_B.append((f"s{_b}{_h}", 4 if _b == NB - 1 else 2))
        JOBS_A.append((f"wt{_b}{_h}", 2 if _b == NB - 1 else 1))
        JOBS_A.append((f"o{_b}{_h}", 1))
JOBS_B += [(f"lv{l}", NB) for l in range(LEVELS + 1)]
JOBS_A += [("kdt", NB + 1)]
JOBS_B += [("st_m", 1)]
for _b in range(NB):
    JOBS_A += [(f"ro{_b}", 1)]
    JOBS_B += [(f"st{_b}", 1)] * (_b < NB - 1)
JOBS_B += [("mixt", 2 * NB), ("o0", NB), ("o1", NB)]
JOBS_A += [("xnt", 2 * NB)]
for _i in range(4):
    JOBS_A += [(f"p{_i}", 4), (f"sc{_i}", NB)]
JOBS_B += [("trH", 2 * NB)]
JOBS_A += [("q2", 4), ("k2", 4), ("v2", 4), ("za", 4), ("ub", 4), ("vb", 4), ("zb", 4), ("ga0", 4), ("ga1", 4), ("gb0", 4),
           ("gb1", 4)]
for _b in range(NB):
    for _h in range(H2):
        JOBS_B.append((f"z{_b}{_h}", 1))
        JOBS_A += [(f"w2{_b}{_h}", 1), (f"o2{_b}{_h}", 1)]
JOBS_B += [("sgu", NB)]
JOBS_A += [("yt", 2 * NB)]
JOBS_B += [("up0", 2 * NB), ("up1", 2 * NB)]
JOBS_A += [("mt", 2 * NB)]
JOBS_B += [("w0", NB), ("w1", NB)]


def ends(jobs):
    at, out = 0, {}
    for name, n in jobs:
        at += n
        out[name] = at
    return out


A_END = ends(JOBS_A)
B_END = ends(JOBS_B)


class Arena:

    def __init__(self, tensor, at, end):
        self.tensor, self.at, self.end = tensor, at, end

    def take(self, n):
        ap = self.tensor[:, self.at:self.at + n]
        self.at += n
        assert self.at <= self.end, (self.at, self.end)
        return ap


def cut(ap, *dims):
    names = "abcd"[:len(dims)]
    return ap.rearrange(f"p ({' '.join(names)}) -> p {' '.join(names)}", **dict(zip(names, dims)))


def build(nc, t, out):
    ctx = ExitStack()
    with ctx:
        def sb(name, words, dt=F32):
            return ctx.enter_context(nc.sbuf_tensor(name, [P, words], dt))

        def sem(name):
            return ctx.enter_context(nc.semaphore(name))

        pa = [ctx.enter_context(nc.psum_tensor(f"pa{i}", [P, 512], F32)) for i in range(RA)]
        pb = [ctx.enter_context(nc.psum_tensor(f"pb{i}", [P, 512], F32)) for i in range(RB)]
        py = [ctx.enter_context(nc.psum_tensor(f"py{i}", [P, 512], F32)) for i in range(2)]

        ident = sb("ident", P)[:, :]
        h = cut(sb("h", NB * D)[:, :], NB, D)
        wbuf = cut(sb("wbuf", 2 * KT * W)[:, :], 2, KT, W)
        small = Arena(sb("small", 768), 0, 768)
        KB = 256
        area = sb("area", 39700)

        tri = sb("tri", P)[:, :]
        stri = sb("stri", P)[:, :]
        normw = small.take(KT)
        normg2 = small.take(KT)
        sublnw = small.take(1)
        recw = small.take(HR)
        lam_in = cut(small.take(4 * DH), 4, DH)
        lblog = cut(small.take(2 * HR), 2, HR)
        lb = small.take(HR)
        olb = small.take(HR)
        lbt = cut(small.take(3 * HR), 3, HR)
        lam = small.take(1)
        lamt = small.take(4)
        epsc = small.take(1)
        ss = small.take(16)
        rt = small.take(16)
        rs = small.take(16)
        mx = cut(small.take(4), 2, 2)
        nm = cut(small.take(4), 2, 2)
        rsum = cut(small.take(4), 2, 2)
        rr = cut(small.take(4), 2, 2)
        el = small.take(16 + HR)
        bs = small.take(NG)

        p1 = Arena(area, 0, 39700)
        _an = p1.take(5 * D)
        an = cut(_an, 5, D)
        v = cut(_an[:, 0:5 * W], 5, W)
        vr = cut(_an[:, 5 * W:10 * W], 5, W)
        _at = p1.take(KT * T)
        aT = cut(_at, KT, T)
        ex = _at[:, 0:2048]
        x0 = _at[:, 2048:4096]
        kT = cut(p1.take(HA * T), HA, T)
        _raw = p1.take(HA * T)
        raw = cut(_raw, HA, T)
        o_att = cut(_raw[:, 0:NB * W], NB, W)
        qT = cut(p1.take(HA * SEQ), HA, SEQ)
        _qr = p1.take(HR * SEQ)
        _kr = p1.take(HR * SEQ)
        mixT = None
        kmt = p1.take(HR * NM + P - NM)
        cumm = p1.take(HR * NM)
        gm = p1.take(HR * NM)
        cum = p1.take(HR * SEQ)
        x1 = p1.take(HR * SEQ)
        kdT = cut(p1.take(5 * W), 5, W)
        rg = cut(p1.take(NB * W), NB, W)
        AT = cut(p1.take(NB * W), NB, W)
        o_rec = cut(p1.take(NB * W), NB, W)
        S = p1.take(W)
        St = p1.take(W)
        masks = cut(p1.take((LEVELS + 1) * P), LEVELS + 1, P)
        _cs = p1.take(2 * T)
        cosT, sinT = _cs[:, 0:T], _cs[:, T:2 * T]
        rotm = p1.take(P)
        _es = p1.take(2 * T)
        es = cut(_es, 2, T)
        xm = _es[:, 0:D]
        wts = cut(p1.take(2 * T), 2, T)
        wT = cut(p1.take(2 * 640), 2, 640)
        mixT = cut(area[:, word(_qr):word(_qr) + KT * SEQ], KT, SEQ)
        sq = S

        p2 = Arena(area, 0, 39700)
        xn = cut(p2.take(NB * D), NB, D)
        _xnt = p2.take(KT * SEQ)
        xnT = cut(_xnt, KT, SEQ)
        qp = cut(p2.take(4 * SEQ), 4, SEQ)
        skT = cut(p2.take(2 * HP * NK), 2 * HP, NK)
        tk = Arena(area, word(_xnt), word(_xnt) + 8192)
        sc = cut(p2.take(NB * 2 * HP * NK), NB, 2 * HP, NK)
        ur = cut(p2.take(RING * D), RING, D)
        vr_ = cut(p2.take(RING * D), RING, D)
        ffnw = p2.take(D)
        dg = cut(p2.take(RING * P), RING, P)
        hid = cut(tk.take(2 * SLOTS), 2, SLOTS)
        idxu = cut(tk.take(2 * SLOTS).bitcast(I32), 2, SLOTS)
        iru = cut(p2.take(2 * RING).bitcast(I32), 2, RING)
        irv = cut(p2.take(2 * RING).bitcast(I32), 2, RING)
        d8 = p2.take(RING)
        dots = tk.take(SLOTS)
        gate = cut(tk.take(2 * SLOTS), 2, SLOTS)
        sv = cut(tk.take(2 * HP * TOP), 2 * HP, TOP)
        si = cut(tk.take(2 * HP * TOP).bitcast(U32), 2 * HP, TOP)
        sif = cut(tk.take(2 * HP * TOP), 2 * HP, TOP)
        s2 = tk.take(NK)
        cand = cut(tk.take(HP * TOP * TOP), HP, TOP, TOP)
        c2 = tk.take(TOP * TOP)
        ts_ = cut(tk.take(HP * TOP), HP, TOP)
        pos = cut(tk.take(HP * TOP).bitcast(U32), HP, TOP)
        pi = cut(tk.take(HP * TOP).bitcast(U32), HP, TOP)
        pif = cut(tk.take(2 * HP * TOP), 2, HP * TOP)
        oh = tk.take(HP * TOP * TOP)
        e01 = cut(tk.take(2 * HP * TOP), 2, HP * TOP)
        gsum = tk.take(2 * HP)
        iota = small.take(TOP)
        finw1 = tk.take(D)
        zero = p2.take(P)

        p3 = Arena(area, 0, 39700)
        _ht = p3.take(KT * SEQ)
        hT = cut(_ht, KT, SEQ)
        o2 = cut(_ht[:, 0:NB * W], NB, W)
        _q2 = p3.take(2 * 4 * SEQ)
        q2T = cut(_q2[:, 0:2048], 4, SEQ)
        k2T = cut(_q2[:, 2048:4096], 4, SEQ)
        mT = cut(_q2, KT, SEQ)
        v2 = cut(p3.take(NB * W), NB, W)
        ub = cut(p3.take(NB * W), NB, W)
        _zz = p3.take(2 * NB * W)
        za = cut(_zz[:, 0:2048], NB, W)
        zb = cut(_zz[:, 2048:4096], NB, W)
        _vb = p3.take(NB * W)
        vb = cut(_vb, NB, W)
        ga = cut(p3.take(NB * D), NB, D)
        gb = cut(p3.take(NB * D), NB, D)
        yT = cut(p3.take(KT * SEQ), KT, SEQ)
        an2 = cut(_zz, NB, D)
        vc = area[:, p3.at - KT * SEQ:p3.at - KT * SEQ + 2048]
        vq = area[:, p3.at - 2048:p3.at]
        rcs = vc[:, 0:W]
        lng = p3.take(W)
        lnb = p3.take(W)
        wsT = cut(p3.take(NG * P), NG, P)
        finw = p3.take(D)
        zs = cut(p3.take(2 * W), 2, W)
        ae = cut(p3.take(2 * W), 2, W)
        sp_ = cut(p3.take(2 * W), 2, W)
        w2T = cut(p3.take(2 * W), 2, W)
        up_t = zs[:, 0, :]
        gst = cut(p3.take(4 * 32), 4, 32)
        ones = p3.take(W)

        ld_x = sem("ld_x")
        ld_c = sem("ld_c")
        ld_p = sem("ld_p")
        ld_q = sem("ld_q")
        w_in_sem = [sem(f"w_full{i}") for i in range(2)]
        h1_done = sem("h1_done")
        a_full, a_free = sem("a_full"), sem("a_free")
        b_full, b_free = sem("b_full"), sem("b_free")
        act_s, dve_s = sem("act_s"), sem("dve_s")
        pool_s = sem("pool_s")
        sq_done, ms_done, rt_done, rs_done = sem("sq_done"), sem("ms_done"), sem("rt_done"), sem("rs_done")
        rows_done = sem("rows_done")
        prm_d, prm_a = sem("prm_d"), sem("prm_a")
        f_raw, f_k, g_done = sem("f_raw"), sem("f_k"), sem("g_done")
        mx_done, e_done, wt_ready = sem("mx_done"), sem("e_done"), sem("wt_ready")
        d_done, ex_done, x_ready, x_used = sem("d_done"), sem("ex_done"), sem("x_ready"), sem("x_used")
        kd_ready, s_ready = sem("kd_ready"), sem("s_ready")
        mixrows = sem("mixrows")
        xn_done = sem("xn_done")
        fv = sem("fv")
        u_free, v_free = sem("u_free"), sem("v_free")
        u_full = [sem(f"u_full{i}") for i in range(RING)]
        v_full = [sem(f"v_full{i}") for i in range(RING)]
        idx_ready, dots_ready, hid_ready = sem("idx_ready"), sem("dots_ready"), sem("hid_ready")
        gexp, gmax = sem("gexp"), sem("gmax")
        dg_ready = sem("dg_ready")
        y_full, y_free = sem("y_full"), sem("y_free")
        zs_ready, l_ready, wl_ready, w_ready = sem("zs_ready"), sem("l_ready"), sem("wl_ready"), sem("w_ready")
        ln_v, ln_r, ln_rt = sem("ln_v"), sem("ln_r"), sem("ln_rt")
        y_ready, m_ready = sem("y_ready"), sem("m_ready")
        fin_ready, st = sem("fin_ready"), sem("st")

        block = ctx.enter_context(nc.Block())

        C1 = 16 * 15
        CP = 16 * 2
        CQ = 16 * 4

        @block.sync
        def _(sp):
            sp.dma_start(h[:, :, :], t["x"].rearrange("(b p) d -> p b d", p=P)).then_inc(ld_x, 16)
            sp.dma_start(xm[0:NM, :], t["meta"]).then_inc(ld_x, 16)
            for dst, name in ((ident, "ident"), (normw, "normw"), (cosT, "cosT"), (sinT, "sinT"), (rotm, "rotm"),
                              (lblog, "lblog"), (lam_in, "lam_in"), (tri, "tri"), (stri, "stri"),
                              (masks.bitcast(I32), "masks"), (sublnw, "sublnw"), (recw, "recw"),
                              (normg2, "normg2"), (iota, "iota"), (bs, "bs")):
                sp.dma_start(dst, t[name]).then_inc(ld_c, 16)
            for n, c in enumerate(CHUNKS):
                slot = wbuf[:, n % 2, :, :]
                if n >= 2:
                    last = CHUNKS[n - 2]
                    if last in A_END:
                        sp.wait_ge(a_full, A_END[last])
                    else:
                        sp.wait_ge(b_full, B_END[last])
                if c in WIN_AT:
                    src = [(0, t["w_in"][:, W * WIN_AT[c]:W * (WIN_AT[c] + 1)], slot)]
                elif c in WIN2_AT:
                    src = [(0, t["w_in_2"][:, W * WIN2_AT[c]:W * (WIN2_AT[c] + 1)], slot)]
                elif c[0] == "p":
                    src = [(0, t["wq"][:, W * int(c[1]):W * (int(c[1]) + 1)], slot)]
                elif c[0] == "o":
                    src = [(0, t["w_out"][:, W * int(c[1]):W * (int(c[1]) + 1)], slot)]
                elif c[0] == "w":
                    src = [(0, t["w_out_2"][:, W * int(c[1]):W * (int(c[1]) + 1)], slot)]
                else:
                    j = int(c[2])
                    sp.dma_start(slot[:, 0:4, :], t["w_up_a"][:, W * j:W * (j + 1)]
                                 .rearrange("(k p) n -> p k n", p=P)).then_inc(w_in_sem[n % 2], 16)
                    sp.dma_start(slot[:, 4:8, :], t["w_up_b"][:, W * j:W * (j + 1)]
                                 .rearrange("(k p) n -> p k n", p=P)).then_inc(w_in_sem[n % 2], 16)
                    continue
                sp.dma_start(src[0][2], src[0][1].rearrange("(k p) n -> p k n", p=P)).then_inc(w_in_sem[n % 2], 16)
                if c == "p0":
                    sp.wait_ge(b_free, B_END["o1"])
                    sp.dma_start(skT, t["skT"]).then_inc(ld_p, 16)
                    sp.dma_start(ffnw, t["ffnw"].broadcast_to([P, D])).then_inc(ld_p, 16)
                if c == "k2":
                    sp.wait_ge(a_free, A_END["sc3"])
                    sp.dma_start(finw1, t["finw1"].broadcast_to([P, D])).then_inc(ld_p, 16)
                    sp.wait_ge(h1_done, 1)
                    sp.dma_start(lng, t["lng"].broadcast_to([P, W])).then_inc(ld_q, 16)
                    sp.dma_start(lnb, t["lnb"].broadcast_to([P, W])).then_inc(ld_q, 16)
                    sp.dma_start(wsT, t["wsT"]).then_inc(ld_q, 16)
                    sp.dma_start(finw, t["finw"].broadcast_to([P, D])).then_inc(ld_q, 16)
            for b in range(NB):
                sp.wait_ge(fin_ready, b + 1)
                sp.dma_start(out[P * b:P * (b + 1), :], h[:, b, :]).then_inc(st, 16)
            sp.wait_ge(st, 16 * NB)

        @block.tensor
        def _(pe):
            na, nb, nw, wl = [0], [0], [0], [0, 0]

            def a_bank():
                n = na[0]
                if n >= RA:
                    pe.wait_ge(a_free, n - RA + 1)
                na[0] += 1
                return pa[n % RA]

            def b_bank():
                n = nb[0]
                if n >= RB:
                    pe.wait_ge(b_free, n - RB + 1)
                nb[0] += 1
                return pb[n % RB]

            def chunk(n_dma=1):
                n = nw[0]
                wl[n % 2] += 16 * n_dma
                pe.wait_ge(w_in_sem[n % 2], wl[n % 2])
                nw[0] += 1
                return wbuf[:, n % 2, :, :]

            def at(name_a=None, name_b=None):
                if name_a:
                    assert na[0] == A_END[name_a], (name_a, na[0], A_END[name_a])
                if name_b:
                    assert nb[0] == B_END[name_b], (name_b, nb[0], B_END[name_b])

            def mm(o, l, r, start, stop):
                return nc.tensor.matmul(o, l, r, start=start, stop=stop, skip_group_check=True)

            def cols_real(w, src, lo, bank):
                for i in range(4):
                    ps = bank()
                    for k in range(KT):
                        last = mm(ps[:, 0:SEQ], w[:, k, P * i:P * (i + 1)], src[:, k, lo:lo + SEQ], k == 0, k == KT - 1)
                    last.then_inc(a_full, 1)
                return last

            def cols_meta(w):
                ps = a_bank()
                for i in range(4):
                    for k in range(KT):
                        last = mm(ps[:, NM * i:NM * (i + 1)], w[:, k, P * i:P * (i + 1)], aT[:, k, 0:NM],
                                  k == 0, k == KT - 1)
                last.then_inc(a_full, 1)
                return last

            def rows_real(w, src, lo):
                for b in range(NB):
                    ps = a_bank()
                    for k in range(KT):
                        last = mm(ps[:, :], src[:, k, lo + P * b:lo + P * (b + 1)], w[:, k, :], k == 0, k == KT - 1)
                    last.then_inc(a_full, 1)

            def rows_meta(w):
                ps = a_bank()
                for k in range(KT):
                    last = mm(ps[0:NM, :], aT[:, k, 0:NM], w[:, k, :], k == 0, k == KT - 1)
                last.then_inc(a_full, 1)

            pe.wait_ge(ld_c, C1)
            for b in [4] + list(range(NB)):
                n = NM if b == 4 else P
                pe.wait_ge(rows_done, 1 if b == 4 else b + 2)
                for g in range(2):
                    ps = b_bank()
                    for k in range(4):
                        last = nc.tensor.transpose(ps[:, P * k:P * k + n], an[0:n, b, P * (4 * g + k):P * (4 * g + k + 1)],
                                                   ident[0:n, 0:n])
                    last.then_inc(b_full, 1)
            at(name_b="trA")
            pe.wait_ge(b_free, B_END["trA"])
            w = chunk()
            cols_real(w, aT, NM, a_bank)
            cols_meta(w)
            w = chunk()
            rows_real(w, aT, NM)
            rows_meta(w)
            pe.wait_ge(a_free, A_END["ak"])
            for i in range(HA):
                mm(b_bank()[:, 0:SEQ], rotm, raw[:, i, NM:T], True, True).then_inc(b_full, 1)
            ps = b_bank()
            for i in range(HA):
                last = mm(ps[:, NM * i:NM * (i + 1)], rotm, raw[:, i, 0:NM], True, True)
            last.then_inc(b_full, 1)
            at("av", "rotk")
            w = chunk()
            cols_real(w, aT, NM, a_bank)
            cols_meta(w)
            w = chunk()
            rows_real(w, aT, NM)
            rows_meta(w)
            w = chunk()
            cols_real(w, aT, NM, a_bank)
            w = chunk()
            cols_real(w, aT, NM, a_bank)
            pe.wait_ge(a_free, A_END["aq"])
            for i in range(HA):
                mm(b_bank()[:, 0:SEQ], rotm, raw[:, i, NM:T], True, True).then_inc(b_full, 1)
            w = chunk()
            rows_real(w, aT, NM)
            at("rg", "rotq")

            pe.wait_ge(b_free, B_END["rotq"])
            pairs = [(b, hh) for b in range(NB) for hh in range(HA)]

            def scores(b, hh):
                lo = NM if b == NB - 1 else 0
                for part in range(2):
                    rows = slice(DH * part, DH * (part + 1))
                    mm(b_bank()[:, 0:NM + P * (b + 1) - lo], qT[rows, hh, P * b:P * (b + 1)],
                       kT[rows, hh, lo:NM + P * (b + 1)], True, True).then_inc(b_full, 1)
                for part in range(2 if lo else 0):
                    rows = slice(DH * part, DH * (part + 1))
                    mm(b_bank()[:, 0:NM], qT[rows, hh, P * b:P * (b + 1)], kT[rows, hh, 0:NM],
                       True, True).then_inc(b_full, 1)

            def sums(n, b, hh):
                pe.wait_ge(wt_ready, n + 1)
                ww = wts[:, n % 2, :]
                tiles = [ww[:, 0:P]] + [ww[:, NM + P * j:NM + P * (j + 1)] for j in range(b + 1)]
                for lo in range(0, len(tiles), 4):
                    ps = a_bank()
                    for j, x in enumerate(tiles[lo:lo + 4]):
                        last = nc.tensor.transpose(ps[:, P * j:P * (j + 1)], x, ident)
                    last.then_inc(a_full, 1)
                pe.wait_ge(a_free, A_END[f"wt{b}{hh}"])
                ps = a_bank()
                vcols = slice(P * hh, P * (hh + 1))
                mm(ps[:, 0:P], wT[0:NM, n % 2, 0:P], v[0:NM, 4, vcols], True, False)
                for j in range(b + 1):
                    last = mm(ps[:, 0:P], wT[:, n % 2, P * (j + 1):P * (j + 2)], v[:, j, vcols], False, j == b)
                last.then_inc(a_full, 1)

            scores(*pairs[0])
            for n, (b, hh) in enumerate(pairs):
                if n + 1 < len(pairs):
                    scores(*pairs[n + 1])
                sums(n, b, hh)
                at(f"o{b}{hh}")

            for l in range(LEVELS + 1):
                if l < LEVELS:
                    pe.wait_ge(x_ready, l + 1)
                for b in range(NB):
                    ps = b_bank()
                    for hh in range(HR):
                        c = slice(SEQ * hh + P * b, SEQ * hh + P * (b + 1))
                        left = (x0, x1)[l % 2][:, c] if l < LEVELS else _kr[:, c]
                        right = (x0, x1)[l % 2][:, c] if l < LEVELS else _qr[:, c]
                        last = mm(ps[:, P * hh:P * (hh + 1)], left, right, True, True)
                    last.then_inc(b_full, 1)
            at(name_b=f"lv{LEVELS}")
            pe.wait_ge(kd_ready, 1)
            for b in [4] + list(range(NB)):
                ps = a_bank()
                for hh in range(HR):
                    src = kmt[:, NM * hh:NM * hh + P] if b == 4 else _kr[:, SEQ * hh + P * b:SEQ * hh + P * (b + 1)]
                    last = nc.tensor.transpose(ps[:, P * hh:P * (hh + 1)], src, ident)
                last.then_inc(a_full, 1)
            pe.wait_ge(a_free, A_END["kdt"])
            ps = b_bank()
            for hh in range(HR):
                c = slice(P * hh, P * (hh + 1))
                last = mm(ps[:, c], kdT[0:NM, 4, c], vr[0:NM, 4, c], True, True)
            last.then_inc(b_full, 1)
            for b in range(NB):
                pe.wait_ge(s_ready, b + 1)
                pe.wait_ge(b_free, B_END[f"lv{LEVELS}"])
                ps = a_bank()
                for hh in range(HR):
                    c = slice(P * hh, P * (hh + 1))
                    mm(ps[:, c], AT[:, b, c], vr[:, b, c], True, False)
                    last = mm(ps[:, c], _qr[:, SEQ * hh + P * b:SEQ * hh + P * (b + 1)], S[:, c], False, True)
                last.then_inc(a_full, 1)
                if b == NB - 1:
                    continue
                ps = b_bank()
                for hh in range(HR):
                    c = slice(P * hh, P * (hh + 1))
                    last = mm(ps[:, c], kdT[:, b, c], vr[:, b, c], True, True)
                last.then_inc(b_full, 1)
            pe.wait_ge(mixrows, 2)
            for src in (o_att, o_rec):
                for b in range(NB):
                    ps = b_bank()
                    for k in range(4):
                        last = nc.tensor.transpose(ps[:, P * k:P * (k + 1)], src[:, b, P * k:P * (k + 1)], ident)
                    last.then_inc(b_full, 1)
            at("ro3", "mixt")
            pe.wait_ge(b_free, B_END["mixt"])
            for j in range(2):
                w = chunk()
                for b in range(NB):
                    ps = b_bank()
                    for k in range(KT):
                        last = mm(ps[:, :], mixT[:, k, P * b:P * (b + 1)], w[:, k, :], k == 0, k == KT - 1)
                    last.then_inc(b_full, 1)
            at(name_b="o1")

            for b in range(NB):
                pe.wait_ge(xn_done, b + 1)
                for g in range(2):
                    ps = a_bank()
                    for k in range(4):
                        last = nc.tensor.transpose(ps[:, P * k:P * (k + 1)],
                                                   xn[:, b, P * (4 * g + k):P * (4 * g + k + 1)], ident)
                    last.then_inc(a_full, 1)
            pe.wait_ge(a_free, A_END["xnt"])
            pe.wait_ge(ld_p, CP)
            for i in range(4):
                w = chunk()
                cols_real(w, xnT, 0, a_bank)
                pe.wait_ge(a_free, A_END[f"p{i}"])
                for b in range(NB):
                    ps = a_bank()
                    for j in range(4):
                        last = mm(ps[:, P * j:P * (j + 1)], qp[:, j, P * b:P * (b + 1)], skT[:, 4 * i + j, :], True, True)
                    last.then_inc(a_full, 1)
                at(f"sc{i}")
            for b in range(NB):
                if b:
                    pe.wait_ge(y_free, b)
                for c in range(2):
                    mm(py[c][:, :], ident, h[:, b, W * c:W * (c + 1)], True, False)
                with pe.Fori(0, SLOTS // RING) as it:
                    for s in range(RING):
                        if s % 4 == 0:
                            pe.wait_ge(dg_ready, it * 2 + (b * (SLOTS // 4) + s // 4 + 1))
                        pe.wait_ge(v_full[s], it * 16 + (b * (SLOTS // RING) * 16 + 16))
                        for c in range(2):
                            last = nc.tensor.matmul(py[c][:, :], dg[:, s, :], vr_[:, s, W * c:W * (c + 1)],
                                                    start=False, stop=False, skip_group_check=True)
                        last.then_inc(v_free, 1)
                for c in range(2):
                    last = mm(py[c][:, :], zero, h[:, b, W * c:W * (c + 1)], False, True)
                last.then_inc(y_full, 1)

            for b in range(NB):
                pe.wait_ge(rows_done, 5 + b + 1)
                for g in range(2):
                    ps = b_bank()
                    for k in range(4):
                        last = nc.tensor.transpose(ps[:, P * k:P * (k + 1)],
                                                   an2[:, b, P * (4 * g + k):P * (4 * g + k + 1)], ident)
                    last.then_inc(b_full, 1)
            pe.wait_ge(b_free, B_END["trH"])
            for c in CHUNKS[13:24]:
                w = chunk()
                if c in ("q2", "k2"):
                    cols_real(w, hT, 0, a_bank)
                else:
                    rows_real(w, hT, 0)
            at("gb1")
            pairs2 = [(b, hh) for b in range(NB) for hh in range(H2)]

            def scores2(b, hh):
                rows = slice(DH2 * (hh % 2), DH2 * (hh % 2 + 1))
                mm(b_bank()[:, 0:P * (b + 1)], q2T[rows, hh // 2, P * b:P * (b + 1)], k2T[rows, hh // 2, 0:P * (b + 1)],
                   True, True).then_inc(b_full, 1)

            scores2(*pairs2[0])
            for n, (b, hh) in enumerate(pairs2):
                if n + 1 < len(pairs2):
                    scores2(*pairs2[n + 1])
                pe.wait_ge(w_ready, n + 1)
                ps = a_bank()
                for j in range(b + 1):
                    last = nc.tensor.transpose(ps[:, P * j:P * (j + 1)], ae[:, n % 2, P * j:P * (j + 1)], ident)
                last.then_inc(a_full, 1)
                pe.wait_ge(a_free, A_END[f"w2{b}{hh}"])
                ps = a_bank()
                for j in range(b + 1):
                    last = mm(ps[:, 0:DH2], w2T[:, n % 2, P * j:P * (j + 1)], v2[:, j, DH2 * hh:DH2 * (hh + 1)],
                              j == 0, j == b)
                last.then_inc(a_full, 1)
                at(f"o2{b}{hh}")
            pe.wait_ge(ln_v, 1)
            for b in range(NB):
                ps = b_bank()
                for g in range(NG):
                    last = mm(ps[:, GC * g:GC * (g + 1)], wsT[:, g, :], vb[:, b, GC * g:GC * (g + 1)], True, True)
                last.then_inc(b_full, 1)
            at(name_b="sgu")
            pe.wait_ge(y_ready, 2)
            for src in (o2, vb):
                for b in range(NB):
                    ps = a_bank()
                    for k in range(4):
                        last = nc.tensor.transpose(ps[:, P * k:P * (k + 1)], src[:, b, P * k:P * (k + 1)], ident)
                    last.then_inc(a_full, 1)
            at("yt")
            pe.wait_ge(a_free, A_END["yt"])
            for j in range(2):
                w = chunk(2)
                for b in range(NB):
                    for half in range(2):
                        ps = b_bank()
                        for k in range(4):
                            last = mm(ps[:, :], yT[:, 4 * half + k, P * b:P * (b + 1)], w[:, 4 * half + k, :],
                                      k == 0, k == 3)
                        last.then_inc(b_full, 1)
            at(name_b="up1")
            pe.wait_ge(b_free, B_END["up1"])
            for b in range(NB):
                for g in range(2):
                    ps = a_bank()
                    for k in range(4):
                        last = nc.tensor.transpose(ps[:, P * k:P * (k + 1)],
                                                   ga[:, b, P * (4 * g + k):P * (4 * g + k + 1)], ident)
                    last.then_inc(a_full, 1)
            at("mt")
            pe.wait_ge(a_free, A_END["mt"])
            for j in range(2):
                w = chunk()
                for b in range(NB):
                    ps = b_bank()
                    for k in range(KT):
                        last = mm(ps[:, :], mT[:, k, P * b:P * (b + 1)], w[:, k, :], k == 0, k == KT - 1)
                    last.then_inc(b_full, 1)
            at(name_b="w1")

        @block.scalar
        def _(act):
            na, own = [0], [0]
            fn = nc.scalar.activation

            def bank():
                act.wait_ge(a_full, na[0] + 1)
                na[0] += 1
                return pa[(na[0] - 1) % RA]

            def step(ins):
                own[0] += 1
                ins.then_inc(act_s, 1)
                act.wait_ge(act_s, own[0])

            def empty(dst, func=ACT.Copy, cols=slice(0, 512), rows=slice(0, P), scale=1.0, view=None):
                ps = bank()[rows, cols]
                if view:
                    ps = view(ps)
                fn(dst, ps, func, scale=scale).then_inc(a_free, 1)

            act.wait_ge(ld_x, 32)
            act.wait_ge(dve_s, 1)
            for b in range(NB):
                fn(an[:, b, :], h[:, b, :], ACT.Square, accum_out=ss[:, b:b + 1])
            fn(an[0:NM, 4, :], xm[0:NM, :], ACT.Square, accum_out=ss[0:NM, 4:5]).then_inc(sq_done, 1)
            act.wait_ge(ms_done, 1)
            fn(rt[:, 0:5], ss[:, 0:5], ACT.Sqrt).then_inc(rt_done, 1)
            act.wait_ge(rs_done, 1)
            act.wait_ge(sq_done, 1)
            fn(an[0:NM, 4, :], xm[0:NM, :], ACT.Copy, scale=rs[0:NM, 4:5]).then_inc(rows_done, 1)
            for b in range(NB):
                fn(an[:, b, :], h[:, b, :], ACT.Copy, scale=rs[:, b:b + 1]).then_inc(rows_done, 1)
            act.wait_ge(prm_d, 1)
            fn(lbt[:, 0:2, :], lbt[:, 0:2, :], ACT.Exp).then_inc(prm_a, 1)
            fn(lamt[:, 0:2], lamt[:, 0:2], ACT.Exp).then_inc(prm_a, 1)
            for i in range(HA):
                empty(raw[:, i, NM:T])
            empty(raw[:, :, 0:NM], cols=slice(0, HA * NM), view=lambda x: cut(x, HA, NM))
            act.wait_ge(b_free, B_END["trA"])
            for b in range(NB):
                empty(v[:, b, :])
            empty(v[0:NM, 4, :], rows=slice(0, NM))
            for i in range(HR):
                empty(_kr[:, SEQ * i:SEQ * (i + 1)], ACT.Sigmoid)
            empty(kmt[:, 0:HR * NM], ACT.Sigmoid, cols=slice(0, HR * NM))
            for b in range(NB):
                empty(vr[:, b, :])
            empty(vr[0:NM, 4, :], rows=slice(0, NM))
            act.wait_ge(f_raw, 1)
            fn(x1, _kr, ACT.Ln)
            fn(gm, kmt[:, 0:HR * NM], ACT.Ln).then_inc(g_done, 1)
            act.wait_ge(b_free, B_END["rotk"])
            for i in range(HA):
                empty(raw[:, i, NM:T])
            for i in range(HR):
                empty(_qr[:, SEQ * i:SEQ * (i + 1)], ACT.Silu)
            for b in range(NB):
                empty(rg[:, b, :], ACT.Silu)
            act.wait_ge(b_free, B_END["rotq"])
            n = 0
            for b in range(NB):
                nk = NM + P * (b + 1)
                for hh in range(HA):
                    act.wait_ge(mx_done, n + 1)
                    for part in range(2):
                        last = fn(es[:, part, 0:nk], es[:, part, 0:nk], ACT.Exp, scale=DH ** -0.5,
                                  bias=nm[:, 0, part:part + 1], accum_out=rsum[:, 0, part:part + 1])
                    last.then_inc(e_done, 1)
                    if b < 3:
                        empty(wT[:, n % 2, 0:P * (b + 2)], cols=slice(0, P * (b + 2)))
                    else:
                        empty(wT[:, n % 2, 0:512])
                        empty(wT[:, n % 2, 512:640], cols=slice(0, P))
                    empty(o_att[:, b, P * hh:P * (hh + 1)], cols=slice(0, P))
                    n += 1
            for l in range(LEVELS):
                half = (P // 2) >> l
                act.wait_ge(d_done, l + 1)
                e3 = ex.rearrange("p (n s) -> p n s", s=2 * half)
                fn(e3[:, :, half:], e3[:, :, half:], ACT.Exp)
                fn(e3[:, :, 0:half], e3[:, :, 0:half], ACT.Exp, scale=-1.0).then_inc(ex_done, 1)
            act.wait_ge(d_done, LEVELS + 1)
            fn(ex, ex, ACT.Exp)
            fn(x0, cum, ACT.Exp)
            fn(gm, gm, ACT.Exp)
            fn(el[:, 0:16], cum[:, P - 1::P], ACT.Exp).then_inc(ex_done, 1)
            for _b in range(5):
                empty(kdT[:, (4, 0, 1, 2, 3)[_b], :])
            for b in range(NB):
                empty(o_rec[:, b, :])
            for k in range(2):
                act.wait_ge(ms_done, 2 + k)
                fn(rt[:, 0:16], ss[:, 0:16], ACT.Sqrt).then_inc(rt_done, 1)
            act.wait_ge(b_free, B_END["o1"])
            for b in range(NB):
                last = fn(xn[:, b, :], h[:, b, :], ACT.Square, accum_out=ss[:, b:b + 1])
            last.then_inc(sq_done, 1)
            act.wait_ge(ms_done, 4)
            fn(rt[:, 0:NB], ss[:, 0:NB], ACT.Sqrt).then_inc(rt_done, 1)
            for b in range(NB):
                for g in range(2):
                    empty(xnT[:, 4 * g:4 * g + 4, P * b:P * (b + 1)], view=lambda x: cut(x, 4, P))
            for i in range(4):
                for j in range(4):
                    empty(qp[:, j, :])
                for b in range(NB):
                    empty(sc[:, b, 4 * i:4 * i + 4, :], view=lambda x: cut(x, 4, P))
            for b in range(NB + 1):
                if b < NB:
                    act.wait_ge(gmax, b + 1)
                    fn(gate[:, b % 2, :], gate[:, b % 2, :], ACT.Exp).then_inc(gexp, 1)
                if b < NB:
                    act.wait_ge(dots_ready, b + 1)
                    fn(dots, dots, ACT.Gelu).then_inc(hid_ready, 1)
            act.wait_ge(y_free, NB)
            for b in range(NB):
                last = fn(xn[:, b, :], h[:, b, :], ACT.Square, accum_out=ss[:, b:b + 1])
            last.then_inc(sq_done, 1)
            act.wait_ge(ms_done, 5)
            fn(rt[:, 0:NB], ss[:, 0:NB], ACT.Sqrt).then_inc(rt_done, 1)
            act.wait_ge(h1_done, 1)
            for b in range(NB):
                last = fn(an2[:, b, :], h[:, b, :], ACT.Square, accum_out=ss[:, b:b + 1])
            last.then_inc(sq_done, 1)
            act.wait_ge(ms_done, 6)
            fn(rt[:, 0:NB], ss[:, 0:NB], ACT.Sqrt).then_inc(rt_done, 1)
            act.wait_ge(rs_done, 6)
            act.wait_ge(sq_done, 4)
            for b in range(NB):
                fn(an2[:, b, :], h[:, b, :], ACT.Copy, scale=rs[:, b:b + 1]).then_inc(rows_done, 1)
            act.wait_ge(b_free, B_END["trH"])
            for i in range(4):
                empty(q2T[:, i, :], scale=DH2 ** -0.5)
            for i in range(4):
                empty(k2T[:, i, :])
            for dst, func in ((v2, ACT.Copy), (za, ACT.Silu), (ub, ACT.Gelu_apprx_tanh), (vb, ACT.Gelu_apprx_tanh),
                              (zb, ACT.Silu)):
                for b in range(NB):
                    empty(dst[:, b, :], func)
            for dst in (ga, gb):
                for j in range(2):
                    for b in range(NB):
                        empty(dst[:, b, W * j:W * (j + 1)], ACT.Sigmoid)
            act.wait_ge(ln_r, 1)
            fn(gst[:, 2, :], gst[:, 1, :], ACT.Sqrt).then_inc(ln_rt, 1)
            n = 0
            for b in range(NB):
                nk = P * (b + 1)
                for hh in range(H2):
                    act.wait_ge(zs_ready, n + 1)
                    e = ae[:, n % 2, 0:nk]
                    step(fn(e, zs[:, n % 2, 0:nk], ACT.Abs))
                    step(fn(e, e, ACT.Exp, scale=-1.0))
                    fn(e, e, ACT.Ln, bias=1.0).then_inc(l_ready, 1)
                    act.wait_ge(wl_ready, n + 1)
                    fn(e, zs[:, n % 2, 0:nk], ACT.Exp).then_inc(w_ready, 1)
                    empty(w2T[:, n % 2, 0:nk], cols=slice(0, nk))
                    empty(o2[:, b, DH2 * hh:DH2 * (hh + 1)], cols=slice(0, DH2))
                    n += 1
            for g in range(2):
                for b in range(NB):
                    empty(yT[:, 4 * g:4 * g + 4, P * b:P * (b + 1)], view=lambda x: cut(x, 4, P))
            for b in range(NB):
                for g in range(2):
                    empty(mT[:, 4 * g:4 * g + 4, P * b:P * (b + 1)], view=lambda x: cut(x, 4, P))
            act.wait_ge(b_free, B_END["w1"])
            for b in range(NB):
                last = fn(gb[:, b, :], h[:, b, :], ACT.Square, accum_out=ss[:, b:b + 1])
            last.then_inc(sq_done, 1)
            act.wait_ge(ms_done, 7)
            fn(rt[:, 0:NB], ss[:, 0:NB], ACT.Sqrt).then_inc(rt_done, 1)

        @block.vector
        def _(dve):
            nb_, own = [0], [0]
            V = nc.vector

            def bank():
                dve.wait_ge(b_full, nb_[0] + 1)
                nb_[0] += 1
                return pb[(nb_[0] - 1) % RB]

            def emptied(ins):
                ins.then_inc(b_free, 1)
                dve.wait_ge(b_free, nb_[0])
    
            def step(ins):
                own[0] += 1
                ins.then_inc(dve_s, 1)
                dve.wait_ge(dve_s, own[0])

            def mean_root(k, n, count):
                V.tensor_scalar(ss[:, 0:n], ss[:, 0:n], 1.0 / count, EPS, ALU.mult, ALU.add).then_inc(ms_done, 1)
                dve.wait_ge(rt_done, k)
                V.reciprocal(rs[:, 0:n], rt[:, 0:n]).then_inc(rs_done, 1)
                dve.wait_ge(rs_done, k)

            def copy_level(l):
                for b in range(NB):
                    emptied(V.copy_predicated(cut(AT[:, b, :], HR, P),
                                              masks[:, l, :].bitcast(I32).unsqueeze(1).broadcast_to([P, HR, P]),
                                              cut(bank()[:, :], HR, P)))

            step(V.memset(ss, 1.0))
            dve.wait_ge(sq_done, 1)
            mean_root(1, 5, D)
            dve.wait_ge(ld_c, C1)
            step(V.tensor_tensor(lbt[:, 2, :], lblog[:, 0, :], lblog[:, 1, :], ALU.max))
            step(V.tensor_tensor(lbt[:, 0, :], lblog[:, 0, :], lbt[:, 2, :], ALU.subtract))
            step(V.tensor_tensor(lbt[:, 1, :], lblog[:, 1, :], lbt[:, 2, :], ALU.subtract))
            step(V.tensor_tensor(lam_in[:, 0, :], lam_in[:, 0, :], lam_in[:, 1, :], ALU.mult))
            step(V.tensor_tensor(lam_in[:, 2, :], lam_in[:, 2, :], lam_in[:, 3, :], ALU.mult))
            step(V.reduce_sum(lamt[:, 0:1], lam_in[:, 0, :], AXX))
            V.reduce_sum(lamt[:, 1:2], lam_in[:, 2, :], AXX).then_inc(prm_d, 1)
            V.memset(kmt, 0.0)
            V.memset(S, 0.0)
            step(V.memset(AT, 0.0))
            dve.wait_ge(prm_a, 2)
            step(V.tensor_tensor(lbt[:, 2, :], lbt[:, 0, :], lbt[:, 1, :], ALU.add))
            step(V.reciprocal(lbt[:, 2, :], lbt[:, 2, :]))
            step(V.tensor_tensor(lb, lbt[:, 0, :], lbt[:, 2, :], ALU.mult))
            step(V.tensor_scalar(olb, lb, -1.0, 1.0, ALU.mult, ALU.add))
            step(V.tensor_tensor(lam, lamt[:, 0:1], lamt[:, 1:2], ALU.subtract))
            step(V.tensor_scalar(lam, lam, LAM0, None, ALU.add))
            for b in [4] + list(range(NB)):
                n = NM if b == 4 else P
                lo = 0 if b == 4 else NM + P * b
                for g in range(2):
                    ps = cut(bank()[:, :], 4, P)[:, :, 0:n]
                    emptied(V.tensor_tensor(aT[:, 4 * g:4 * g + 4, lo:lo + n], ps,
                                    normw[:, 4 * g:4 * g + 4].unsqueeze(2).broadcast_to([P, 4, n]), ALU.mult))
            dve.wait_ge(a_free, A_END["ak"])
            step(V.tensor_tensor(kT, raw, cosT.unsqueeze(1).broadcast_to([P, HA, T]), ALU.mult))
            for i in range(HA):
                ps = bank()
                step(V.tensor_tensor(St, ps[:, 0:SEQ], sinT[:, NM:T], ALU.mult))
                emptied(V.tensor_tensor(kT[:, i, NM:T], kT[:, i, NM:T], St, ALU.add))
            ps = cut(bank()[:, 0:HA * NM], HA, NM)
            step(V.tensor_tensor(cut(St[:, 0:HA * NM], HA, NM), ps, sinT[:, 0:NM].unsqueeze(1).broadcast_to([P, HA, NM]),
                                 ALU.mult))
            emptied(V.tensor_tensor(kT[:, :, 0:NM], kT[:, :, 0:NM], cut(St[:, 0:HA * NM], HA, NM), ALU.add))
            dve.wait_ge(a_free, A_END["rf"])
            for i in range(HR):
                for x in (_kr[:, SEQ * i:SEQ * (i + 1)], kmt[:, NM * i:NM * (i + 1)]):
                    last = V.tensor_scalar(x, x, olb[:, i:i + 1], lb[:, i:i + 1], ALU.mult, ALU.add)
            last.then_inc(f_raw, 1)
            dve.wait_ge(f_raw, 1)
            dve.wait_ge(g_done, 1)
            step(V.tensor_scalar(_kr, _kr, -1.0, 1.0, ALU.mult, ALU.add))
            step(V.tensor_scalar(kmt[:, 0:HR * NM], kmt[:, 0:HR * NM], -1.0, 1.0, ALU.mult, ALU.add))
            step(V.memset(St, 1.0))
            for i in range(HR * NB):
                V.tensor_tensor_scan(cum[:, P * i:P * (i + 1)], St[:, 0:P], x1[:, P * i:P * (i + 1)], 0.0,
                                     ALU.mult, ALU.add)
            for i in range(HR):
                last = V.tensor_tensor_scan(cumm[:, NM * i:NM * (i + 1)], St[:, 0:NM], gm[:, NM * i:NM * (i + 1)], 0.0,
                                            ALU.mult, ALU.add)
            step(last)
            dve.wait_ge(a_free, A_END["aq"])
            step(V.tensor_tensor(qT, raw[:, :, NM:T], cosT[:, NM:T].unsqueeze(1).broadcast_to([P, HA, SEQ]), ALU.mult))
            for i in range(HA):
                ps = bank()
                step(V.tensor_tensor(St, ps[:, 0:SEQ], sinT[:, NM:T], ALU.mult))
                emptied(V.tensor_tensor(qT[:, i, :], qT[:, i, :], St, ALU.add))
            n = 0
            for b in range(NB):
                nk = NM + P * (b + 1)
                dl = NM + P * b
                for hh in range(HA):
                    if n:
                        dve.wait_ge(wt_ready, n)
                    lo = NM if b == NB - 1 else 0
                    for part in range(2):
                        ps = bank()
                        V.tensor_copy(es[:, part, lo:dl], ps[:, 0:dl - lo])
                        emptied(V.tensor_tensor(es[:, part, dl:nk], ps[:, dl - lo:nk - lo], tri, ALU.add))
                    for part in range(2 if lo else 0):
                        emptied(V.tensor_copy(es[:, part, 0:NM], bank()[:, 0:NM]))
                    step(V.tensor_reduce(mx[:, 0, :], es[:, :, 0:nk], AXX, ALU.max))
                    V.tensor_scalar(nm[:, 0, :], mx[:, 0, :], -(DH ** -0.5), None, ALU.mult).then_inc(mx_done, 1)
                    dve.wait_ge(e_done, n + 1)
                    step(V.reciprocal(rr[:, 0, :], rsum[:, 0, :]))
                    step(V.tensor_scalar(rr[:, 0, 1:2], rr[:, 0, 1:2], lam, -1.0, ALU.mult, ALU.mult))
                    if n >= 2:
                        dve.wait_ge(a_free, A_END[f"wt{(n - 2) // HA}{(n - 2) % HA}"])
                    step(V.tensor_scalar(es[:, 0, 0:nk], es[:, 0, 0:nk], rr[:, 0, 0:1], None, ALU.mult))
                    V.scalar_tensor_tensor(wts[:, n % 2, 0:nk], es[:, 1, 0:nk], rr[:, 0, 1:2], es[:, 0, 0:nk],
                                           ALU.mult, ALU.add).then_inc(wt_ready, 1)
                    n += 1
            for l in range(LEVELS):
                half = (P // 2) >> l
                pairs = HR * SEQ // (2 * half)
                c3 = cum.rearrange("p (n s) -> p n s", s=2 * half)
                e3 = ex.rearrange("p (n s) -> p n s", s=2 * half)
                x3 = (x0, x1)[l % 2].rearrange("p (n s) -> p n s", s=2 * half)
                q3 = _qr.rearrange("p (n s) -> p n s", s=2 * half)
                k3 = _kr.rearrange("p (n s) -> p n s", s=2 * half)
                if l:
                    dve.wait_ge(x_ready, l)
                V.tensor_tensor(e3, c3, c3[:, :, half - 1:half].broadcast_to([P, pairs, 2 * half]), ALU.subtract)\
                    .then_inc(d_done, 1)
                if l:
                    copy_level(l - 1)
                dve.wait_ge(ex_done, l + 1)
                V.tensor_tensor(x3[:, :, half:], e3[:, :, half:], q3[:, :, half:], ALU.mult)
                V.tensor_tensor(x3[:, :, 0:half], e3[:, :, 0:half], k3[:, :, 0:half], ALU.mult).then_inc(x_ready, 1)
            for l in (LEVELS - 1, LEVELS):
                copy_level(l)
            dve.wait_ge(x_ready, LEVELS)
            c3 = cum.rearrange("p (n s) -> p n s", s=P)
            cm3 = cumm.rearrange("p (n s) -> p n s", s=NM)
            V.tensor_tensor(cut(gm, HR, NM), cm3[:, :, NM - 1:NM].broadcast_to([P, HR, NM]), cm3, ALU.subtract)
            V.tensor_tensor(ex.rearrange("p (n s) -> p n s", s=P), c3[:, :, P - 1:P].broadcast_to([P, HR * NB, P]), c3,
                            ALU.subtract).then_inc(d_done, 1)
            dve.wait_ge(ex_done, LEVELS + 1)
            V.tensor_tensor(_qr, _qr, x0, ALU.mult)
            V.tensor_tensor(kmt[:, 0:HR * NM], kmt[:, 0:HR * NM], gm, ALU.mult)
            V.tensor_tensor(_kr, _kr, ex, ALU.mult).then_inc(kd_ready, 1)
            dve.wait_ge(kd_ready, 1)
            V.tensor_copy(S, bank()[:, :]).then_inc(s_ready, 1)
            dve.wait_ge(s_ready, 1)
            emptied(V.tensor_copy(St[:, 0:1], S[:, 0:1]))
            for b in range(NB - 1):
                ps = bank()
                dve.wait_ge(a_full, A_END[f"ro{b}"])
                elb = el[:, 0:16].rearrange("p (h b) -> p h b", b=NB)[:, :, b:b + 1].broadcast_to([P, HR, P])
                step(V.tensor_tensor(cut(S, HR, P), cut(S, HR, P), elb, ALU.mult))
                V.tensor_tensor(S, S, ps[:, :], ALU.add).then_inc(s_ready, 1)
                dve.wait_ge(s_ready, b + 2)
                emptied(V.tensor_copy(St[:, 1:2], ps[:, 0:1]))
            for k, (rows, end) in enumerate(((o_att, "o33"), (o_rec, "ro3"))):
                dve.wait_ge(a_free, A_END[end])
                flat = (o_att, o_rec)[k].rearrange("p b n -> p (b n)")
                step(V.tensor_tensor(cum, flat, flat, ALU.mult))
                step(V.tensor_reduce(ss[:, 0:16], cut(cum, 16, P), AXX, ALU.add))
                mean_root(2 + k, 16, P)
                if k == 0:
                    step(V.tensor_scalar(rs[:, 0:16], rs[:, 0:16], 1.0 - LAM0, None, ALU.mult))
                last = V.tensor_tensor(cut(flat, 16, P), cut(flat, 16, P), rs[:, 0:16].unsqueeze(2).broadcast_to([P, 16, P]),
                                       ALU.mult)
                if k == 1:
                    step(last)
                    last = V.tensor_tensor(o_rec, o_rec, rg, ALU.mult)
                last.then_inc(mixrows, 1)
                dve.wait_ge(mixrows, k + 1)
            for k in range(2):
                for b in range(NB):
                    ps = cut(bank()[:, :], 4, P)
                    wgt = recw.unsqueeze(2).broadcast_to([P, 4, P]) if k else sublnw.unsqueeze(2).broadcast_to([P, 4, P])
                    emptied(V.tensor_tensor(mixT[:, 4 * k:4 * k + 4, P * b:P * (b + 1)], ps, wgt, ALU.mult))
            for j in range(2):
                for b in range(NB):
                    emptied(V.tensor_tensor(h[:, b, W * j:W * (j + 1)], h[:, b, W * j:W * (j + 1)], bank()[:, :], ALU.add))
            dve.wait_ge(sq_done, 2)
            mean_root(4, NB, D)
            dve.wait_ge(ld_p, CP)
            for b in range(NB):
                V.scalar_tensor_tensor(xn[:, b, :], h[:, b, :], rs[:, b:b + 1], ffnw, ALU.mult, ALU.mult)\
                    .then_inc(xn_done, 1)
            dve.wait_ge(xn_done, NB)
            dve.wait_ge(a_free, A_END["sc3"])

            def topk(b):
                for i in range(2 * HP):
                    row = sc[:, b, i, :]
                    step(V.max(sv[:, i, 0:8], row))
                    V.max_index(si[:, i, 0:8], sv[:, i, 0:8], row)
                    step(V.match_replace(s2, sv[:, i, 0:8], row, FMIN))
                    step(V.max(sv[:, i, 8:16], s2))
                    step(V.max_index(si[:, i, 8:16], sv[:, i, 8:16], s2))
                step(V.tensor_copy(sif, si))
                sv2 = sv.rearrange("p (h a) k -> p h a k", a=2)
                sf2 = sif.rearrange("p (h a) k -> p h a k", a=2)
                dims = [P, HP, TOP, TOP]
                step(V.tensor_tensor(cand, sv2[:, :, 0, :].unsqueeze(3).broadcast_to(dims),
                                     sv2[:, :, 1, :].unsqueeze(2).broadcast_to(dims), ALU.add))
                for i in range(HP):
                    row = cand[:, i, :, :].rearrange("p a b -> p (a b)")
                    step(V.max(ts_[:, i, 0:8], row))
                    V.max_index(pos[:, i, 0:8], ts_[:, i, 0:8], row)
                    step(V.match_replace(c2, ts_[:, i, 0:8], row, FMIN))
                    step(V.max(ts_[:, i, 8:16], c2))
                    step(V.max_index(pos[:, i, 8:16], ts_[:, i, 8:16], c2))
                g3 = cut(gate[:, b % 2, :], HP, TOP)
                V.tensor_tensor(g3, ts_, ts_[:, :, 0:1].broadcast_to([P, HP, TOP]), ALU.subtract).then_inc(gmax, 1)
                for a in range(2):
                    if a == 0:
                        step(V.tensor_scalar(pi, pos, 4, None, ALU.logical_shift_right))
                    else:
                        step(V.tensor_scalar(pi, pos, TOP - 1, None, ALU.bitwise_and))
                    step(V.tensor_copy(cut(pif[:, a, :], HP, TOP), pi))
                    o4 = cut(oh, HP, TOP, TOP)
                    step(V.tensor_tensor(cut(oh, SLOTS, TOP), pif[:, a, :].unsqueeze(2).broadcast_to([P, SLOTS, TOP]),
                                         iota.unsqueeze(1).broadcast_to([P, SLOTS, TOP]), ALU.is_equal))
                    step(V.tensor_tensor(o4, o4, sf2[:, :, a, :].unsqueeze(2).broadcast_to(dims), ALU.mult))
                    step(V.tensor_reduce(e01[:, a, :], cut(oh, SLOTS, TOP), AXX, ALU.add))
                V.scalar_tensor_tensor(idxu[:, b % 2, :], e01[:, 0, :], float(NK), e01[:, 1, :], ALU.mult, ALU.add)\
                    .then_inc(idx_ready, 1)
                dve.wait_ge(gexp, b + 1)
                step(V.tensor_reduce(gsum[:, 0:HP], g3, AXX, ALU.add))
                step(V.reciprocal(gsum[:, HP:2 * HP], gsum[:, 0:HP]))
                step(V.tensor_tensor(g3, g3, gsum[:, HP:2 * HP].unsqueeze(2).broadcast_to([P, HP, TOP]), ALU.mult))

            V.memset(zero, 0.0).then_inc(v_free, RING)
            V.memset(d8, 0.0).then_inc(u_free, RING)
            dve.wait_ge(u_free, RING)
            for stage in range(NB + 1):
                if stage < NB:
                    topk(stage)
                bb, bv = stage, stage - 1
                with dve.Fori(0, SLOTS // RING) as it:
                    if stage < NB:
                        for s in range(RING):
                            dve.wait_ge(u_full[s], it * 16 + (bb * (SLOTS // RING) * 16 + 16))
                            V.tensor_tensor_reduce(ur[:, s, :], ur[:, s, :], xn[:, bb, :], 1.0, 0.0, ALU.mult, ALU.add,
                                                   d8[:, s:s + 1]).then_inc(u_free, 1)
                        dve.wait_ge(u_free, it * RING + (RING + bb * SLOTS + RING))
                        V.tensor_copy(dots[:, bass.ds(it * RING, RING)], d8).then_inc(fv, 1)
                        dve.wait_ge(fv, it + (bb * (SLOTS // RING) + 1))
                    if stage:
                        for half in range(2):
                            dve.wait_ge(v_free, it * RING + (bv * SLOTS + 4 * half + 4))
                            V.tensor_tensor(dg[:, 4 * half:4 * half + 4, :], ident.unsqueeze(1).broadcast_to([P, 4, P]),
                                            hid[:, bv % 2, bass.ds(it * RING + 4 * half, 4)].unsqueeze(2)
                                            .broadcast_to([P, 4, P]), ALU.mult).then_inc(dg_ready, 1)
                if stage < NB:
                    dve.wait_ge(fv, (bb + 1) * (SLOTS // RING))
                    V.memset(d8, 0.0).then_inc(dots_ready, 1)
                    dve.wait_ge(hid_ready, bb + 1)
                    step(V.tensor_tensor(hid[:, bb % 2, :], dots, gate[:, bb % 2, :], ALU.mult))
                if stage:
                    dve.wait_ge(y_full, stage)
                    for c in range(2):
                        last = V.tensor_copy(h[:, bv, W * c:W * (c + 1)], py[c][:, :])
                    last.then_inc(y_free, 1)
            dve.wait_ge(sq_done, 3)
            mean_root(5, NB, D)
            dve.wait_ge(ld_p, CP + 16)
            for b in range(NB):
                last = V.scalar_tensor_tensor(h[:, b, :], h[:, b, :], rs[:, b:b + 1], finw1, ALU.mult, ALU.mult)
            last.then_inc(h1_done, 1)
            dve.wait_ge(sq_done, 4)
            mean_root(6, NB, D)
            for b in range(NB):
                for g in range(2):
                    ps = cut(bank()[:, :], 4, P)
                    emptied(V.tensor_tensor(hT[:, 4 * g:4 * g + 4, P * b:P * (b + 1)], ps,
                                    normg2[:, 4 * g:4 * g + 4].unsqueeze(2).broadcast_to([P, 4, P]), ALU.mult))
            dve.wait_ge(ld_q, CQ)
            dve.wait_ge(a_free, A_END["vb"])
            vflat = vb.rearrange("p b n -> p (b n)")
            NGB = NB * NG
            v3 = cut(vflat, NGB, GC)
            V.memset(wsT[GC:P, :, 0:GC], 0.0)
            step(V.tensor_reduce(gst[:, 0, :], v3, AXX, ALU.add))
            step(V.tensor_scalar(gst[:, 0, :], gst[:, 0, :], 1.0 / GC, None, ALU.mult))
            step(V.tensor_tensor(cut(vc, NGB, GC), v3, gst[:, 0, :].unsqueeze(2).broadcast_to([P, NGB, GC]), ALU.subtract))
            step(V.tensor_tensor(vq, vc, vc, ALU.mult))
            step(V.tensor_reduce(gst[:, 1, :], cut(vq, NGB, GC), AXX, ALU.add))
            V.tensor_scalar(gst[:, 1, :], gst[:, 1, :], 1.0 / GC, EPS, ALU.mult, ALU.add).then_inc(ln_r, 1)
            dve.wait_ge(ln_rt, 1)
            step(V.reciprocal(gst[:, 3, :], gst[:, 2, :]))
            step(V.tensor_tensor(cut(vc, NGB, GC), cut(vc, NGB, GC), gst[:, 3, :].unsqueeze(2).broadcast_to([P, NGB, GC]),
                                 ALU.mult))
            step(V.tensor_tensor(cut(vc, NB, W), cut(vc, NB, W), lng.unsqueeze(1).broadcast_to([P, NB, W]), ALU.mult))
            V.tensor_tensor(vb, cut(vc, NB, W), lnb.unsqueeze(1).broadcast_to([P, NB, W]), ALU.add).then_inc(ln_v, 1)
            step(V.memset(ones, 1.0))
            n = 0
            for b in range(NB):
                nk = P * (b + 1)
                for hh in range(H2):
                    if n >= 2:
                        dve.wait_ge(w_ready, n - 1)
                    z = zs[:, n % 2, :]
                    ps = bank()
                    if b:
                        V.tensor_copy(z[:, 0:P * b], ps[:, 0:P * b])
                    emptied(V.tensor_tensor(z[:, P * b:nk], ps[:, P * b:nk], stri, ALU.add))
                    V.tensor_copy(sp_[:, n % 2, 0:1], z[:, 0:1]).then_inc(zs_ready, 1)
                    dve.wait_ge(l_ready, n + 1)
                    step(V.scalar_tensor_tensor(sp_[:, n % 2, 0:nk], z[:, 0:nk], 0.0, ae[:, n % 2, 0:nk], ALU.max, ALU.add))
                    rc = sp_[:, n % 2, 0:nk]
                    step(V.tensor_tensor_scan(rcs[:, 0:nk][:, ::-1], ones[:, 0:nk], rc[:, ::-1], 0.0, ALU.mult, ALU.add))
                    V.tensor_tensor(z[:, 0:nk], z[:, 0:nk], rcs[:, 0:nk], ALU.subtract).then_inc(wl_ready, 1)
                    n += 1
            dve.wait_ge(a_free, A_END["o237"])
            for b in range(NB):
                ps = bank()
                step(V.tensor_tensor(cut(up_t, NG, GC), cut(ps[:, :], NG, GC), bs.unsqueeze(2).broadcast_to([P, NG, GC]),
                                     ALU.add))
                step(V.tensor_tensor(up_t, up_t, ub[:, b, :], ALU.mult))
                emptied(V.tensor_tensor(vb[:, b, :], up_t, zb[:, b, :], ALU.mult))
            V.tensor_copy(gst[:, 0, 0:1], up_t[:, 0:1]).then_inc(y_ready, 1)
            V.tensor_tensor(o2, o2, za, ALU.mult).then_inc(y_ready, 1)
            dve.wait_ge(y_ready, 2)
            for j in range(2):
                for b in range(NB):
                    gg, gh = ga[:, b, W * j:W * (j + 1)], gb[:, b, W * j:W * (j + 1)]
                    emptied(V.tensor_tensor(gg, gg, bank()[:, :], ALU.mult))
                    step(V.tensor_tensor(gh, gh, bank()[:, :], ALU.mult))
                    emptied(V.tensor_tensor(gg, gg, gh, ALU.add))
            for j in range(2):
                for b in range(NB):
                    emptied(V.tensor_tensor(h[:, b, W * j:W * (j + 1)], h[:, b, W * j:W * (j + 1)], bank()[:, :], ALU.add))
            dve.wait_ge(sq_done, 5)
            mean_root(7, NB, D)
            for b in range(NB):
                V.scalar_tensor_tensor(h[:, b, :], h[:, b, :], rs[:, b:b + 1], finw, ALU.mult, ALU.mult)\
                    .then_inc(fin_ready, 1)

        @block.gpsimd
        def _(pool):
            steps = 0
            for stage in range(NB + 1):
                bu, bv = stage, stage - 1
                if stage < NB:
                    pool.wait_ge(idx_ready, stage + 1)
                per = (stage < NB) + (stage > 0)
                with pool.Fori(0, SLOTS // (2 * RING)) as it:
                    for turn in range(2):
                        at = it * (2 * RING) + turn * RING
                        if stage < NB:
                            nc.gpsimd.tensor_copy(iru[:, turn, :], idxu[:, bu % 2, bass.ds(at, RING)]).then_inc(pool_s, 1)
                        if stage:
                            nc.gpsimd.tensor_copy(irv[:, turn, :], idxu[:, bv % 2, bass.ds(at, RING)]).then_inc(pool_s, 1)
                        pool.wait_ge(pool_s, it * (2 * per) + (steps + per * (turn + 1)))
                        nc.gpsimd.nop(nofuse=True)
                        for s in range(RING):
                            if stage < NB:
                                pool.wait_ge(u_free, it * (2 * RING) + (bu * SLOTS + turn * RING + s + 1))
                                nc.gpsimd.nop(nofuse=True)
                                nc.gpsimd.indirect_dma_start(ur[:, s, :], None, t["peer_u"], bass.IndirectOffsetOnAxis(
                                    ap=iru[:, turn, s:s + 1].bitcast(U32), axis=0)).then_inc(u_full[s], 16)
                            if stage:
                                pool.wait_ge(v_free, it * (2 * RING) + (bv * SLOTS + turn * RING + s + 1))
                                nc.gpsimd.nop(nofuse=True)
                                nc.gpsimd.indirect_dma_start(vr_[:, s, :], None, t["peer_v"], bass.IndirectOffsetOnAxis(
                                    ap=irv[:, turn, s:s + 1].bitcast(U32), axis=0)).then_inc(v_full[s], 16)
                steps += (SLOTS // RING) * per


def word(ap):
    return ap.offset


def shape_constants():
    d = 2 * (np.arange(DH // 2, dtype=np.float32))
    inv = (np.float32(10000.0) ** (-d / np.float32(DH))).astype(np.float32)
    ang = np.arange(T, dtype=np.float32)[:, None] * inv[None, :]
    ang = np.concatenate([ang, ang], axis=-1)
    cos, sin = np.cos(ang).T.astype(np.float32), np.sin(ang).T.astype(np.float32)
    rot = np.zeros((P, P), np.float32)
    half = DH // 2
    for part in range(2):
        for i in range(half):
            rot[DH * part + half + i, DH * part + i] = -1.0
            rot[DH * part + i, DH * part + half + i] = 1.0
    s, q = np.arange(P)[:, None], np.arange(P)[None, :]
    masks = []
    for l in range(LEVELS):
        hf = (P // 2) >> l
        masks.append((s // (2 * hf) == q // (2 * hf)) & (s % (2 * hf) < hf) & (q % (2 * hf) >= hf))
    masks.append(s == q)
    return {
        "ident": np.eye(P, dtype=np.float32),
        "cosT": np.concatenate([cos, cos], 0), "sinT": np.concatenate([sin, sin], 0), "rotm": rot,
        "masks": np.ascontiguousarray(np.stack(masks, 1).astype(np.int32)),
        "tri": np.where(q <= s, 0.0, NEG).astype(np.float32),
        "stri": np.where(q < s, 0.0, NEG).astype(np.float32),
        "iota": np.ascontiguousarray(np.broadcast_to(np.arange(TOP, dtype=np.float32), (P, TOP))),
    }


def kernel(**inputs):
    import numpy as _np
    import concourse.bacc as _bacc
    from concourse.bass_utils import run_bass_kernel_spmd as _run

    i = {k: _np.asarray(v) for k, v in inputs.items()}
    c = _np.ascontiguousarray
    rep = lambda a: c(_np.broadcast_to(a, (P,) + a.shape))
    arrays = {
        "x": i["x"][0], "meta": i["meta_tokens"], "w_in": i["w_in"][0], "w_out": i["w_out"][0],
        "wq": i["peer_w_query"][0], "peer_u": i["peer_u"][0], "peer_v": i["peer_v"][0],
        "w_in_2": i["w_in_2"][0], "w_up_a": i["w_up_a_2"][0], "w_up_b": i["w_up_b_2"][0], "w_out_2": i["w_out_2"][0],
        "normw": c(i["mix_norm_w"].reshape(KT, P).T), "normg2": c(i["norm_g_2"].reshape(KT, P).T),
        "sublnw": c(i["diff_subln_w"].reshape(P, 1)), "recw": c(i["rec_norm_w"].reshape(HR, P).T),
        "lam_in": rep(_np.stack([i["diff_lambda_q1"][0], i["diff_lambda_k1"][0],
                                 i["diff_lambda_q2"][0], i["diff_lambda_k2"][0]])),
        "lblog": c(i["rec_lb_logits"].reshape(2, HR, P).transpose(2, 0, 1)),
        "skT": c(i["peer_subkeys"].reshape(2 * HP, NK, P).transpose(2, 0, 1)),
        "ffnw": i["ffn_norm_w"], "finw": i["final_norm_g_2"].reshape(1, D),
        "lng": i["sgu_ln_g_2"].reshape(1, W), "lnb": i["sgu_ln_b_2"].reshape(1, W),
        "wsT": c(i["w_spatial_2"][0].transpose(2, 0, 1)), "bs": c(i["b_spatial_2"][0].T),
    }
    arrays.update(shape_constants())
    arrays["finw1"] = i["final_norm_w"].reshape(1, D)
    nc = _bacc.Bacc("TRN2", target_bir_lowering=False, num_devices=1)
    t, feed = {}, {}
    for name, a in arrays.items():
        a = c(a)
        feed[f"in_{name}"] = a
        t[name] = nc.dram_tensor(f"in_{name}", a.shape, mybir.dt.from_np(a.dtype), kind="ExternalInput").ap()
    out = nc.dram_tensor("out_0", (SEQ, D), F32, kind="ExternalOutput").ap()
    build(nc, t, out)
    r = _run(nc, [feed], core_ids=[0])
    return r.results[0]["out_0"].reshape(1, SEQ, D)
```

```python
from contextlib import ExitStack

import numpy as np
import concourse.bass as bass
from concourse import mybir

ALU = mybir.AluOpType
ACT = mybir.ActivationFunctionType
AXX = mybir.AxisListType.X
F32 = mybir.dt.float32
U32 = mybir.dt.uint32
I32 = mybir.dt.int32

P = 128
D = 1024
KT = D // P
SEQ = 512
NB = SEQ // P
NM = 16
T = NM + SEQ
W = 512
HA, DH = 4, 64
HR = 4
HEAD_STEPS = 24
LEVELS = 7
HP = 8
NK = 128
TOP = 16
SLOTS = HP * TOP
RING = 8
ROUNDS = SLOTS // RING
H2, DH2 = 8, 64
NG, GC = 8, 64
EPS = 1e-6
NEG = -1e30
FMIN = -3.4028234663852886e38
LAM0 = 0.2
RA = RB = 3
RC = 2

CHUNKS = ["ak", "av", "rf", "ri", "aq", "rq", "rg", "o0", "o1", "p0", "p1", "p2", "p3",
          "q2", "k2", "v2", "vb", "ub", "za", "zb", "ga0", "ga1", "gb0", "gb1", "up0", "up1", "w0", "w1"]
SIDE = ["vb", "ub", "za", "zb", "ga0", "ga1", "gb0", "gb1"]
UNITS2 = [(b, hh) for b in range(NB) for hh in range(H2)]
SGU_AT = {18: 0, 21: 1, 24: 2, 27: 3}
WIN_AT = {"aq": 0, "ak": 1, "av": 2, "rq": 3, "rf": 4, "ri": 5, "rg": 6}
WIN2_AT = {n: i for i, n in enumerate(["q2", "k2", "v2", "za", "ub", "vb", "zb", "ga0", "ga1", "gb0", "gb1"])}

JOBS_A = [("ak", 5), ("av", 5), ("rf", 5), ("ri", 5), ("aq", 4), ("rq", 4), ("rg", 4)]
JOBS_B = [("trA", 10), ("rotk", 5), ("rotq", 4)]
for _b in range(NB):
    for _h in range(HA):
        JOBS_B.append((f"s{_b}{_h}", 4 if _b == NB - 1 else 2))
        JOBS_A.append((f"wt{_b}{_h}", 2 if _b == NB - 1 else 1))
        JOBS_A.append((f"o{_b}{_h}", 1))
JOBS_B += [(f"lv{l}", NB) for l in range(LEVELS + 1)]
JOBS_A += [("kdt", NB + 1)]
JOBS_B += [("st_m", 1)]
for _b in range(NB):
    JOBS_A += [(f"ro{_b}", 1)]
    JOBS_B += [(f"st{_b}", 1)] * (_b < NB - 1)
JOBS_B += [("mixt", 2 * NB), ("o0", NB), ("o1", NB)]
JOBS_A += [("xnt", 2 * NB)]
for _i in range(4):
    JOBS_A += [(f"p{_i}", 4), (f"sc{_i}", NB)]
JOBS_B += [("trH", 2 * NB)]
JOBS_A += [("q2", 4), ("k2", 4), ("v2", 4)]
JOBS_C = []
JOBS_B += [("z0", 1)]
for _n in range(len(UNITS2)):
    if _n + 1 < len(UNITS2):
        JOBS_B += [(f"z{_n + 1}", 1)]
    if _n in SGU_AT:
        JOBS_B += [(f"sgu{SGU_AT[_n]}", 1)]
    JOBS_A += [(f"w2_{_n}", 1), (f"o2_{_n}", 1)]
for _c in SIDE:
    JOBS_C += [(_c, NB)]
JOBS_A += [("yt", 2 * NB)]
JOBS_B += [("up0", 2 * NB), ("up1", 2 * NB)]
JOBS_A += [("mt", 2 * NB)]
JOBS_B += [("w0", NB), ("w1", NB)]


def ends(jobs):
    at, out = 0, {}
    for name, n in jobs:
        assert name not in out
        at += n
        out[name] = at
    return out


A_END = ends(JOBS_A)
B_END = ends(JOBS_B)
C_END = ends(JOBS_C)


class Arena:

    def __init__(self, tensor, at, end):
        self.tensor, self.at, self.end = tensor, at, end

    def take(self, n):
        ap = self.tensor[:, self.at:self.at + n]
        self.at += n
        assert self.at <= self.end, (self.at, self.end)
        return ap


def cut(ap, *dims):
    names = "abcd"[:len(dims)]
    return ap.rearrange(f"p ({' '.join(names)}) -> p {' '.join(names)}", **dict(zip(names, dims)))


def build(nc, t, out):
    ctx = ExitStack()
    with ctx:
        def sb(name, words, dt=F32):
            return ctx.enter_context(nc.sbuf_tensor(name, [P, words], dt))

        def sem(name):
            return ctx.enter_context(nc.semaphore(name))

        pa = [ctx.enter_context(nc.psum_tensor(f"pa{i}", [P, 512], F32)) for i in range(RA)]
        pb = [ctx.enter_context(nc.psum_tensor(f"pb{i}", [P, 512], F32)) for i in range(RB)]
        py = [ctx.enter_context(nc.psum_tensor(f"py{i}", [P, 512], F32)) for i in range(2)]

        ident = sb("ident", P)[:, :]
        h = cut(sb("h", NB * D)[:, :], NB, D)
        wbuf = cut(sb("wbuf", 2 * KT * W)[:, :], 2, KT, W)
        small = Arena(sb("small", 768), 0, 768)
        KB = 256
        area = sb("area", 39700)

        tri = sb("tri", P)[:, :]
        stri = sb("stri", P)[:, :]
        normw = small.take(KT)
        normg2 = small.take(KT)
        sublnw = small.take(1)
        recw = small.take(HR)
        lam_in = cut(small.take(4 * DH), 4, DH)
        lblog = cut(small.take(2 * HR), 2, HR)
        lb = small.take(HR)
        olb = small.take(HR)
        lbt = cut(small.take(3 * HR), 3, HR)
        lam = small.take(1)
        lamt = small.take(4)
        epsc = small.take(1)
        ss = small.take(16)
        rt = small.take(16)
        rs = small.take(16)
        mx = cut(small.take(4), 2, 2)
        nm = cut(small.take(4), 2, 2)
        rsum = cut(small.take(4), 2, 2)
        rr = cut(small.take(4), 2, 2)
        el = small.take(16 + HR)
        bs = small.take(NG)

        p1 = Arena(area, 0, 39700)
        _an = p1.take(5 * D)
        an = cut(_an, 5, D)
        v = cut(_an[:, 0:5 * W], 5, W)
        vr = cut(_an[:, 5 * W:10 * W], 5, W)
        _at = p1.take(KT * T)
        aT = cut(_at, KT, T)
        ex = _at[:, 0:2048]
        x0 = _at[:, 2048:4096]
        kT = cut(p1.take(HA * T), HA, T)
        _raw = p1.take(HA * T)
        raw = cut(_raw, HA, T)
        o_att = cut(_raw[:, 0:NB * W], NB, W)
        qT = cut(p1.take(HA * SEQ), HA, SEQ)
        _qr = p1.take(HR * SEQ)
        _kr = p1.take(HR * SEQ)
        mixT = None
        kmt = p1.take(HR * NM + P - NM)
        cumm = p1.take(HR * NM)
        gm = p1.take(HR * NM)
        cum = p1.take(HR * SEQ)
        x1 = p1.take(HR * SEQ)
        kdT = cut(p1.take(5 * W), 5, W)
        rg = cut(p1.take(NB * W), NB, W)
        AT = cut(p1.take(NB * W), NB, W)
        o_rec = cut(p1.take(NB * W), NB, W)
        S = p1.take(W)
        St = p1.take(W)
        masks = cut(p1.take((LEVELS + 1) * P), LEVELS + 1, P)
        _cs = p1.take(2 * T)
        cosT, sinT = _cs[:, 0:T], _cs[:, T:2 * T]
        rotm = p1.take(P)
        _es = p1.take(2 * T)
        es = cut(_es, 2, T)
        xm = _es[:, 0:D]
        wts = cut(p1.take(2 * T), 2, T)
        wT = cut(p1.take(2 * 640), 2, 640)
        mixT = cut(area[:, word(_qr):word(_qr) + KT * SEQ], KT, SEQ)
        sq = S

        p2 = Arena(area, 0, 39700)
        xn = cut(p2.take(NB * D), NB, D)
        _xnt = p2.take(KT * SEQ)
        xnT = cut(_xnt, KT, SEQ)
        qp = cut(p2.take(4 * SEQ), 4, SEQ)
        skT = cut(p2.take(2 * HP * NK), 2 * HP, NK)
        sc = cut(p2.take(NB * 2 * HP * NK), NB, 2 * HP * NK)
        ur = cut(p2.take(RING * D), RING, D)
        vr_ = cut(p2.take(RING * D), RING, D)
        _ffn = p2.take(D)
        ffnw = _ffn
        dg = cut(_xnt[:, 0:2 * RING * P], 2, RING, P)
        finw1 = _xnt[:, 2 * RING * P:2 * RING * P + D]
        hid = cut(p2.take(2 * SLOTS), 2, SLOTS)
        idxu = cut(p2.take(3 * SLOTS).bitcast(I32), 3, SLOTS)
        gate = cut(p2.take(2 * SLOTS), 2, SLOTS)
        dots = p2.take(SLOTS)
        iru = cut(p2.take(2 * RING).bitcast(I32), 2, RING)
        irv = cut(p2.take(2 * RING).bitcast(I32), 2, RING)
        d8 = p2.take(RING)
        gsum = p2.take(2 * HP)
        zero = p2.take(P)
        mark = p2.take(2)
        iota = small.take(TOP)
        tk = Arena(area, word(_ffn), word(_ffn) + D)
        rows2 = cut(tk.take(2 * NK), 2, NK)
        s2 = tk.take(NK)
        sv = cut(tk.take(2 * TOP), 2, TOP)
        si = cut(tk.take(2 * TOP).bitcast(U32), 2, TOP)
        sif = cut(tk.take(2 * TOP), 2, TOP)
        cand = tk.take(TOP * TOP)
        top_s = tk.take(TOP)
        pos = tk.take(TOP).bitcast(U32)
        pi = tk.take(TOP).bitcast(U32)
        e01 = cut(tk.take(2 * TOP), 2, TOP)
        c2 = rows2.rearrange("p a k -> p (a k)")
        oh = cut(c2, TOP, TOP)

        p3 = Arena(area, 0, 39700)
        _ht = p3.take(KT * SEQ)
        hT = cut(_ht, KT, SEQ)
        _q2 = p3.take(2 * 4 * SEQ)
        q2T = cut(_q2[:, 0:2048], 4, SEQ)
        k2T = cut(_q2[:, 2048:4096], 4, SEQ)
        mT = cut(_q2, KT, SEQ)
        v2 = cut(p3.take(NB * W), NB, W)
        ub = cut(p3.take(NB * W), NB, W)
        _zz = p3.take(2 * NB * W)
        za = cut(_zz[:, 0:2048], NB, W)
        zb = cut(_zz[:, 2048:4096], NB, W)
        _vb = p3.take(NB * W)
        vb = cut(_vb, NB, W)
        ga = cut(p3.take(NB * D), NB, D)
        gb = cut(p3.take(NB * D), NB, D)
        yT = cut(p3.take(KT * SEQ), KT, SEQ)
        an2 = cut(_zz, NB, D)
        vc = area[:, p3.at - KT * SEQ:p3.at - KT * SEQ + 2048]
        o2 = cut(area[:, p3.at - 2048:p3.at], NB, W)
        vq = gb.rearrange("p b n -> p (b n)")[:, 0:2048]
        lng = p3.take(W)
        lnb = p3.take(W)
        wsT = cut(p3.take(NG * P), NG, P)
        finw = p3.take(D)
        zs = cut(p3.take(2 * W), 2, W)
        ae = cut(p3.take(2 * W), 2, W)
        sp_ = cut(p3.take(2 * W), 2, W)
        w2T = cut(p3.take(2 * W), 2, W)
        rcs = p3.take(W)
        up_t = p3.take(W)
        gst = cut(p3.take(4 * 32), 4, 32)
        ones = p3.take(W)

        ld_x = sem("ld_x")
        ld_c = sem("ld_c")
        ld_p = sem("ld_p")
        ld_q = sem("ld_q")
        w_in_sem = [sem(f"w_full{i}") for i in range(2)]
        h1_done = sem("h1_done")
        a_full, a_free = sem("a_full"), sem("a_free")
        b_full, b_free = sem("b_full"), sem("b_free")
        c_full, c_free = sem("c_full"), sem("c_free")
        act_s, dve_s = sem("act_s"), sem("dve_s")
        pool_s = sem("pool_s")
        sq_done, ms_done, rt_done, rs_done = sem("sq_done"), sem("ms_done"), sem("rt_done"), sem("rs_done")
        rows_done = sem("rows_done")
        prm_d, prm_a = sem("prm_d"), sem("prm_a")
        f_raw, f_k, g_done = sem("f_raw"), sem("f_k"), sem("g_done")
        mx_done, e_done, wt_ready = sem("mx_done"), sem("e_done"), sem("wt_ready")
        d_done, ex_done, x_ready, x_used = sem("d_done"), sem("ex_done"), sem("x_ready"), sem("x_used")
        kd_ready, s_ready = sem("kd_ready"), sem("s_ready")
        mixrows = sem("mixrows")
        xn_done = sem("xn_done")
        fv = sem("fv")
        u_free, v_free = sem("u_free"), sem("v_free")
        u_full = [sem(f"u_full{i}") for i in range(RING)]
        v_full = [sem(f"v_full{i}") for i in range(RING)]
        idx_ready, dots_ready, hid_ready = sem("idx_ready"), sem("dots_ready"), sem("hid_ready")
        gexp, gmax = sem("gexp"), sem("gmax")
        dg_ready = sem("dg_ready")
        y_full, y_free = sem("y_full"), sem("y_free")
        zs_ready, l_ready, wl_ready, w_ready = sem("zs_ready"), sem("l_ready"), sem("wl_ready"), sem("w_ready")
        ln_v, ln_r, ln_rt = sem("ln_v"), sem("ln_r"), sem("ln_rt")
        fn_done = sem("fn_done")
        y_ready, m_ready = sem("y_ready"), sem("m_ready")
        fin_ready, st = sem("fin_ready"), sem("st")

        block = ctx.enter_context(nc.Block())

        C1 = 16 * 15
        CP = 16 * 2
        CQ = 16 * 4

        @block.sync
        def _(sp):
            sp.dma_start(h[:, :, :], t["x"].rearrange("(b p) d -> p b d", p=P)).then_inc(ld_x, 16)
            sp.dma_start(xm[0:NM, :], t["meta"]).then_inc(ld_x, 16)
            for dst, name in ((ident, "ident"), (normw, "normw"), (cosT, "cosT"), (sinT, "sinT"), (rotm, "rotm"),
                              (lblog, "lblog"), (lam_in, "lam_in"), (tri, "tri"), (stri, "stri"),
                              (masks.bitcast(I32), "masks"), (sublnw, "sublnw"), (recw, "recw"),
                              (normg2, "normg2"), (iota, "iota"), (bs, "bs")):
                sp.dma_start(dst, t[name]).then_inc(ld_c, 16)
            for n, c in enumerate(CHUNKS):
                slot = wbuf[:, n % 2, :, :]
                if n >= 2:
                    last = CHUNKS[n - 2]
                    if last in C_END:
                        sp.wait_ge(c_full, C_END[last])
                    elif last in A_END:
                        sp.wait_ge(a_full, A_END[last])
                    else:
                        sp.wait_ge(b_full, B_END[last])
                if c in WIN_AT:
                    src = [(0, t["w_in"][:, W * WIN_AT[c]:W * (WIN_AT[c] + 1)], slot)]
                elif c in WIN2_AT:
                    src = [(0, t["w_in_2"][:, W * WIN2_AT[c]:W * (WIN2_AT[c] + 1)], slot)]
                elif c[0] == "p":
                    src = [(0, t["wq"][:, W * int(c[1]):W * (int(c[1]) + 1)], slot)]
                elif c[0] == "o":
                    src = [(0, t["w_out"][:, W * int(c[1]):W * (int(c[1]) + 1)], slot)]
                elif c[0] == "w":
                    src = [(0, t["w_out_2"][:, W * int(c[1]):W * (int(c[1]) + 1)], slot)]
                else:
                    j = int(c[2])
                    sp.dma_start(slot[:, 0:4, :], t["w_up_a"][:, W * j:W * (j + 1)]
                                 .rearrange("(k p) n -> p k n", p=P)).then_inc(w_in_sem[n % 2], 16)
                    sp.dma_start(slot[:, 4:8, :], t["w_up_b"][:, W * j:W * (j + 1)]
                                 .rearrange("(k p) n -> p k n", p=P)).then_inc(w_in_sem[n % 2], 16)
                    continue
                sp.dma_start(src[0][2], src[0][1].rearrange("(k p) n -> p k n", p=P)).then_inc(w_in_sem[n % 2], 16)
                if c == "p0":
                    sp.wait_ge(b_free, B_END["o1"])
                    sp.dma_start(skT, t["skT"]).then_inc(ld_p, 16)
                    sp.dma_start(ffnw, t["ffnw"].broadcast_to([P, D])).then_inc(ld_p, 16)
                if c == "k2":
                    sp.wait_ge(a_free, A_END["sc3"])
                    sp.dma_start(finw1, t["finw1"].broadcast_to([P, D])).then_inc(ld_p, 16)
                    sp.wait_ge(h1_done, 1)
                    sp.dma_start(lng, t["lng"].broadcast_to([P, W])).then_inc(ld_q, 16)
                    sp.dma_start(lnb, t["lnb"].broadcast_to([P, W])).then_inc(ld_q, 16)
                    sp.dma_start(wsT, t["wsT"]).then_inc(ld_q, 16)
                    sp.dma_start(finw, t["finw"].broadcast_to([P, D])).then_inc(ld_q, 16)
            for b in range(NB):
                sp.wait_ge(fin_ready, b + 1)
                sp.dma_start(out[P * b:P * (b + 1), :], h[:, b, :]).then_inc(st, 16)
            sp.wait_ge(st, 16 * NB)

        @block.tensor
        def _(pe):
            na, nb, n_c, nw, wl = [0], [0], [0], [0], [0, 0]

            def a_bank():
                n = na[0]
                if n >= RA:
                    pe.wait_ge(a_free, n - RA + 1)
                na[0] += 1
                return pa[n % RA]

            def b_bank():
                n = nb[0]
                if n >= RB:
                    pe.wait_ge(b_free, n - RB + 1)
                nb[0] += 1
                return pb[n % RB]

            def c_bank():
                n = n_c[0]
                if n >= RC:
                    pe.wait_ge(c_free, n - RC + 1)
                n_c[0] += 1
                return py[n % RC]

            def chunk(n_dma=1):
                n = nw[0]
                wl[n % 2] += 16 * n_dma
                pe.wait_ge(w_in_sem[n % 2], wl[n % 2])
                nw[0] += 1
                return wbuf[:, n % 2, :, :]

            def at(name_a=None, name_b=None):
                if name_a:
                    assert na[0] == A_END[name_a], (name_a, na[0], A_END[name_a])
                if name_b:
                    assert nb[0] == B_END[name_b], (name_b, nb[0], B_END[name_b])

            def mm(o, l, r, start, stop):
                return nc.tensor.matmul(o, l, r, start=start, stop=stop, skip_group_check=True)

            def cols_real(w, src, lo, bank):
                for i in range(4):
                    ps = bank()
                    for k in range(KT):
                        last = mm(ps[:, 0:SEQ], w[:, k, P * i:P * (i + 1)], src[:, k, lo:lo + SEQ], k == 0, k == KT - 1)
                    last.then_inc(a_full, 1)
                return last

            def cols_meta(w):
                ps = a_bank()
                for i in range(4):
                    for k in range(KT):
                        last = mm(ps[:, NM * i:NM * (i + 1)], w[:, k, P * i:P * (i + 1)], aT[:, k, 0:NM],
                                  k == 0, k == KT - 1)
                last.then_inc(a_full, 1)
                return last

            def rows_real(w, src, lo):
                for b in range(NB):
                    ps = a_bank()
                    for k in range(KT):
                        last = mm(ps[:, :], src[:, k, lo + P * b:lo + P * (b + 1)], w[:, k, :], k == 0, k == KT - 1)
                    last.then_inc(a_full, 1)

            def rows_meta(w):
                ps = a_bank()
                for k in range(KT):
                    last = mm(ps[0:NM, :], aT[:, k, 0:NM], w[:, k, :], k == 0, k == KT - 1)
                last.then_inc(a_full, 1)

            pe.wait_ge(ld_c, C1)
            for b in [4] + list(range(NB)):
                n = NM if b == 4 else P
                pe.wait_ge(rows_done, 1 if b == 4 else b + 2)
                for g in range(2):
                    ps = b_bank()
                    for k in range(4):
                        last = nc.tensor.transpose(ps[:, P * k:P * k + n], an[0:n, b, P * (4 * g + k):P * (4 * g + k + 1)],
                                                   ident[0:n, 0:n])
                    last.then_inc(b_full, 1)
            at(name_b="trA")
            pe.wait_ge(b_free, B_END["trA"])
            w = chunk()
            cols_real(w, aT, NM, a_bank)
            cols_meta(w)
            w = chunk()
            rows_real(w, aT, NM)
            rows_meta(w)
            pe.wait_ge(a_free, A_END["ak"])
            for i in range(HA):
                mm(b_bank()[:, 0:SEQ], rotm, raw[:, i, NM:T], True, True).then_inc(b_full, 1)
            ps = b_bank()
            for i in range(HA):
                last = mm(ps[:, NM * i:NM * (i + 1)], rotm, raw[:, i, 0:NM], True, True)
            last.then_inc(b_full, 1)
            at("av", "rotk")
            w = chunk()
            cols_real(w, aT, NM, a_bank)
            cols_meta(w)
            w = chunk()
            rows_real(w, aT, NM)
            rows_meta(w)
            w = chunk()
            cols_real(w, aT, NM, a_bank)
            w = chunk()
            cols_real(w, aT, NM, a_bank)
            pe.wait_ge(a_free, A_END["aq"])
            for i in range(HA):
                mm(b_bank()[:, 0:SEQ], rotm, raw[:, i, NM:T], True, True).then_inc(b_full, 1)
            w = chunk()
            rows_real(w, aT, NM)
            at("rg", "rotq")

            pe.wait_ge(b_free, B_END["rotq"])
            pairs = [(b, hh) for b in range(NB) for hh in range(HA)]

            def scores(b, hh):
                lo = NM if b == NB - 1 else 0
                for part in range(2):
                    rows = slice(DH * part, DH * (part + 1))
                    mm(b_bank()[:, 0:NM + P * (b + 1) - lo], qT[rows, hh, P * b:P * (b + 1)],
                       kT[rows, hh, lo:NM + P * (b + 1)], True, True).then_inc(b_full, 1)
                for part in range(2 if lo else 0):
                    rows = slice(DH * part, DH * (part + 1))
                    mm(b_bank()[:, 0:NM], qT[rows, hh, P * b:P * (b + 1)], kT[rows, hh, 0:NM],
                       True, True).then_inc(b_full, 1)

            def sums(n, b, hh):
                pe.wait_ge(wt_ready, n + 1)
                ww = wts[:, n % 2, :]
                tiles = [ww[:, 0:P]] + [ww[:, NM + P * j:NM + P * (j + 1)] for j in range(b + 1)]
                for lo in range(0, len(tiles), 4):
                    ps = a_bank()
                    for j, x in enumerate(tiles[lo:lo + 4]):
                        last = nc.tensor.transpose(ps[:, P * j:P * (j + 1)], x, ident)
                    last.then_inc(a_full, 1)
                pe.wait_ge(a_free, A_END[f"wt{b}{hh}"])
                ps = a_bank()
                vcols = slice(P * hh, P * (hh + 1))
                mm(ps[:, 0:P], wT[0:NM, n % 2, 0:P], v[0:NM, 4, vcols], True, False)
                for j in range(b + 1):
                    last = mm(ps[:, 0:P], wT[:, n % 2, P * (j + 1):P * (j + 2)], v[:, j, vcols], False, j == b)
                last.then_inc(a_full, 1)

            scores(*pairs[0])
            for n, (b, hh) in enumerate(pairs):
                if n + 1 < len(pairs):
                    scores(*pairs[n + 1])
                sums(n, b, hh)
                at(f"o{b}{hh}")

            for l in range(LEVELS + 1):
                if l < LEVELS:
                    pe.wait_ge(x_ready, l + 1)
                for b in range(NB):
                    ps = b_bank()
                    for hh in range(HR):
                        c = slice(SEQ * hh + P * b, SEQ * hh + P * (b + 1))
                        left = (x0, x1)[l % 2][:, c] if l < LEVELS else _kr[:, c]
                        right = (x0, x1)[l % 2][:, c] if l < LEVELS else _qr[:, c]
                        last = mm(ps[:, P * hh:P * (hh + 1)], left, right, True, True)
                    last.then_inc(b_full, 1)
            at(name_b=f"lv{LEVELS}")
            pe.wait_ge(kd_ready, 1)
            for b in [4] + list(range(NB)):
                ps = a_bank()
                for hh in range(HR):
                    src = kmt[:, NM * hh:NM * hh + P] if b == 4 else _kr[:, SEQ * hh + P * b:SEQ * hh + P * (b + 1)]
                    last = nc.tensor.transpose(ps[:, P * hh:P * (hh + 1)], src, ident)
                last.then_inc(a_full, 1)
            pe.wait_ge(a_free, A_END["kdt"])
            ps = b_bank()
            for hh in range(HR):
                c = slice(P * hh, P * (hh + 1))
                last = mm(ps[:, c], kdT[0:NM, 4, c], vr[0:NM, 4, c], True, True)
            last.then_inc(b_full, 1)
            for b in range(NB):
                pe.wait_ge(s_ready, b + 1)
                pe.wait_ge(b_free, B_END[f"lv{LEVELS}"])
                ps = a_bank()
                for hh in range(HR):
                    c = slice(P * hh, P * (hh + 1))
                    mm(ps[:, c], AT[:, b, c], vr[:, b, c], True, False)
                    last = mm(ps[:, c], _qr[:, SEQ * hh + P * b:SEQ * hh + P * (b + 1)], S[:, c], False, True)
                last.then_inc(a_full, 1)
                if b == NB - 1:
                    continue
                ps = b_bank()
                for hh in range(HR):
                    c = slice(P * hh, P * (hh + 1))
                    last = mm(ps[:, c], kdT[:, b, c], vr[:, b, c], True, True)
                last.then_inc(b_full, 1)
            pe.wait_ge(mixrows, 2)
            for src in (o_att, o_rec):
                for b in range(NB):
                    ps = b_bank()
                    for k in range(4):
                        last = nc.tensor.transpose(ps[:, P * k:P * (k + 1)], src[:, b, P * k:P * (k + 1)], ident)
                    last.then_inc(b_full, 1)
            at("ro3", "mixt")
            pe.wait_ge(b_free, B_END["mixt"])
            for j in range(2):
                w = chunk()
                for b in range(NB):
                    ps = b_bank()
                    for k in range(KT):
                        last = mm(ps[:, :], mixT[:, k, P * b:P * (b + 1)], w[:, k, :], k == 0, k == KT - 1)
                    last.then_inc(b_full, 1)
            at(name_b="o1")

            for b in range(NB):
                pe.wait_ge(xn_done, b + 1)
                for g in range(2):
                    ps = a_bank()
                    for k in range(4):
                        last = nc.tensor.transpose(ps[:, P * k:P * (k + 1)],
                                                   xn[:, b, P * (4 * g + k):P * (4 * g + k + 1)], ident)
                    last.then_inc(a_full, 1)
            pe.wait_ge(a_free, A_END["xnt"])
            pe.wait_ge(ld_p, CP)
            for i in range(4):
                w = chunk()
                cols_real(w, xnT, 0, a_bank)
                pe.wait_ge(a_free, A_END[f"p{i}"])
                for b in range(NB):
                    ps = a_bank()
                    for j in range(4):
                        last = mm(ps[:, P * j:P * (j + 1)], qp[:, j, P * b:P * (b + 1)], skT[:, 4 * i + j, :], True, True)
                    last.then_inc(a_full, 1)
                at(f"sc{i}")
            for b in range(NB):
                if b:
                    pe.wait_ge(y_free, b)
                for c in range(2):
                    mm(py[c][:, :], ident, h[:, b, W * c:W * (c + 1)], True, False)
                with pe.Fori(0, ROUNDS // 2) as it:
                    for turn in range(2):
                        pe.wait_ge(dg_ready, it * 2 + (b * ROUNDS + turn + 1))
                        for s in range(RING):
                            pe.wait_ge(v_full[s], it * 32 + (b * ROUNDS * 16 + 16 * turn + 16))
                            for c in range(2):
                                last = nc.tensor.matmul(py[c][:, :], dg[:, turn, s, :], vr_[:, s, W * c:W * (c + 1)],
                                                        start=False, stop=False, skip_group_check=True)
                            last.then_inc(v_free, 1)
                for c in range(2):
                    last = mm(py[c][:, :], zero, h[:, b, W * c:W * (c + 1)], False, True)
                last.then_inc(y_full, 1)

            for b in range(NB):
                pe.wait_ge(rows_done, 5 + b + 1)
                for g in range(2):
                    ps = b_bank()
                    for k in range(4):
                        last = nc.tensor.transpose(ps[:, P * k:P * (k + 1)],
                                                   an2[:, b, P * (4 * g + k):P * (4 * g + k + 1)], ident)
                    last.then_inc(b_full, 1)
            pe.wait_ge(b_free, B_END["trH"])
            cols_real(chunk(), hT, 0, a_bank)
            cols_real(chunk(), hT, 0, a_bank)
            rows_real(chunk(), hT, 0)
            at("v2")

            def scores2(b, hh):
                rows = slice(DH2 * (hh % 2), DH2 * (hh % 2 + 1))
                mm(b_bank()[:, 0:P * (b + 1)], q2T[rows, hh // 2, P * b:P * (b + 1)], k2T[rows, hh // 2, 0:P * (b + 1)],
                   True, True).then_inc(b_full, 1)

            pe.wait_ge(a_free, A_END["k2"])
            scores2(*UNITS2[0])
            pe.wait_ge(y_free, NB)
            for n, (b, hh) in enumerate(UNITS2):
                if n + 1 < len(UNITS2):
                    scores2(*UNITS2[n + 1])
                if n in SGU_AT:
                    g_b = SGU_AT[n]
                    pe.wait_ge(ln_v, 1)
                    ps = b_bank()
                    for g in range(NG):
                        last = mm(ps[:, GC * g:GC * (g + 1)], wsT[:, g, :], vb[:, g_b, GC * g:GC * (g + 1)], True, True)
                    last.then_inc(b_full, 1)
                if n % NB == 0:
                    w = chunk()
                rows = slice(P * (n % NB), P * (n % NB + 1))
                side = c_bank()
                for k in range(KT // 2):
                    mm(side[:, :], hT[:, k, rows], w[:, k, :], k == 0, False)
                pe.wait_ge(w_ready, n + 1)
                ps = a_bank()
                for j in range(b + 1):
                    last = nc.tensor.transpose(ps[:, P * j:P * (j + 1)], ae[:, n % 2, P * j:P * (j + 1)], ident)
                last.then_inc(a_full, 1)
                for k in range(KT // 2, KT):
                    last = mm(side[:, :], hT[:, k, rows], w[:, k, :], False, k == KT - 1)
                last.then_inc(c_full, 1)
                pe.wait_ge(a_free, A_END[f"w2_{n}"])
                ps = a_bank()
                for j in range(b + 1):
                    last = mm(ps[:, 0:DH2], w2T[:, n % 2, P * j:P * (j + 1)], v2[:, j, DH2 * hh:DH2 * (hh + 1)],
                              j == 0, j == b)
                last.then_inc(a_full, 1)
                at(f"o2_{n}")
            at(name_b=f"z{len(UNITS2) - 1}")
            for src in (o2, vb):
                for b in range(NB):
                    if src is o2:
                        pe.wait_ge(y_ready, 2 if b == NB - 1 else 1)
                    ps = a_bank()
                    for k in range(4):
                        last = nc.tensor.transpose(ps[:, P * k:P * (k + 1)], src[:, b, P * k:P * (k + 1)], ident)
                    last.then_inc(a_full, 1)
            at("yt")
            pe.wait_ge(a_free, A_END["yt"])
            for j in range(2):
                w = chunk(2)
                for b in range(NB):
                    for half in range(2):
                        ps = b_bank()
                        for k in range(4):
                            last = mm(ps[:, :], yT[:, 4 * half + k, P * b:P * (b + 1)], w[:, 4 * half + k, :],
                                      k == 0, k == 3)
                        last.then_inc(b_full, 1)
            at(name_b="up1")
            pe.wait_ge(b_free, B_END["up1"])
            for b in range(NB):
                for g in range(2):
                    ps = a_bank()
                    for k in range(4):
                        last = nc.tensor.transpose(ps[:, P * k:P * (k + 1)],
                                                   ga[:, b, P * (4 * g + k):P * (4 * g + k + 1)], ident)
                    last.then_inc(a_full, 1)
            at("mt")
            pe.wait_ge(a_free, A_END["mt"])
            for j in range(2):
                w = chunk()
                for b in range(NB):
                    ps = b_bank()
                    for k in range(KT):
                        last = mm(ps[:, :], mT[:, k, P * b:P * (b + 1)], w[:, k, :], k == 0, k == KT - 1)
                    last.then_inc(b_full, 1)
            at(name_b="w1")

        @block.scalar
        def _(act):
            na, n_c, own = [0], [0], [0]
            fn = nc.scalar.activation

            def bank():
                act.wait_ge(a_full, na[0] + 1)
                na[0] += 1
                return pa[(na[0] - 1) % RA]

            def c_empty(dst):
                act.wait_ge(c_full, n_c[0] + 1)
                n_c[0] += 1
                fn(dst, py[(n_c[0] - 1) % RC][:, :], ACT.Copy).then_inc(c_free, 1)

            def step(ins):
                own[0] += 1
                ins.then_inc(act_s, 1)
                act.wait_ge(act_s, own[0])

            def empty(dst, func=ACT.Copy, cols=slice(0, 512), rows=slice(0, P), scale=1.0, view=None):
                ps = bank()[rows, cols]
                if view:
                    ps = view(ps)
                fn(dst, ps, func, scale=scale).then_inc(a_free, 1)

            act.wait_ge(ld_x, 32)
            act.wait_ge(dve_s, 1)
            for b in range(NB):
                fn(an[:, b, :], h[:, b, :], ACT.Square, accum_out=ss[:, b:b + 1])
            fn(an[0:NM, 4, :], xm[0:NM, :], ACT.Square, accum_out=ss[0:NM, 4:5]).then_inc(sq_done, 1)
            act.wait_ge(ms_done, 1)
            fn(rt[:, 0:5], ss[:, 0:5], ACT.Sqrt).then_inc(rt_done, 1)
            act.wait_ge(rs_done, 1)
            act.wait_ge(sq_done, 1)
            fn(an[0:NM, 4, :], xm[0:NM, :], ACT.Copy, scale=rs[0:NM, 4:5]).then_inc(rows_done, 1)
            for b in range(NB):
                fn(an[:, b, :], h[:, b, :], ACT.Copy, scale=rs[:, b:b + 1]).then_inc(rows_done, 1)
            act.wait_ge(prm_d, 1)
            fn(lbt[:, 0:2, :], lbt[:, 0:2, :], ACT.Exp).then_inc(prm_a, 1)
            fn(lamt[:, 0:2], lamt[:, 0:2], ACT.Exp).then_inc(prm_a, 1)
            for i in range(HA):
                empty(raw[:, i, NM:T])
            empty(raw[:, :, 0:NM], cols=slice(0, HA * NM), view=lambda x: cut(x, HA, NM))
            act.wait_ge(b_free, B_END["trA"])
            for b in range(NB):
                empty(v[:, b, :])
            empty(v[0:NM, 4, :], rows=slice(0, NM))
            for i in range(HR):
                empty(_kr[:, SEQ * i:SEQ * (i + 1)], ACT.Sigmoid)
            empty(kmt[:, 0:HR * NM], ACT.Sigmoid, cols=slice(0, HR * NM))
            for b in range(NB):
                empty(vr[:, b, :])
            empty(vr[0:NM, 4, :], rows=slice(0, NM))
            act.wait_ge(f_raw, 1)
            fn(x1, _kr, ACT.Ln)
            fn(gm, kmt[:, 0:HR * NM], ACT.Ln).then_inc(g_done, 1)
            act.wait_ge(b_free, B_END["rotk"])
            for i in range(HA):
                empty(raw[:, i, NM:T])
            for i in range(HR):
                empty(_qr[:, SEQ * i:SEQ * (i + 1)], ACT.Silu)
            for b in range(NB):
                empty(rg[:, b, :], ACT.Silu)
            act.wait_ge(b_free, B_END["rotq"])
            n = 0
            for b in range(NB):
                nk = NM + P * (b + 1)
                for hh in range(HA):
                    act.wait_ge(mx_done, n + 1)
                    for part in range(2):
                        last = fn(es[:, part, 0:nk], es[:, part, 0:nk], ACT.Exp, scale=DH ** -0.5,
                                  bias=nm[:, 0, part:part + 1], accum_out=rsum[:, 0, part:part + 1])
                    last.then_inc(e_done, 1)
                    if b < 3:
                        empty(wT[:, n % 2, 0:P * (b + 2)], cols=slice(0, P * (b + 2)))
                    else:
                        empty(wT[:, n % 2, 0:512])
                        empty(wT[:, n % 2, 512:640], cols=slice(0, P))
                    empty(o_att[:, b, P * hh:P * (hh + 1)], cols=slice(0, P))
                    n += 1
            for l in range(LEVELS):
                half = (P // 2) >> l
                act.wait_ge(d_done, l + 1)
                e3 = ex.rearrange("p (n s) -> p n s", s=2 * half)
                fn(e3[:, :, half:], e3[:, :, half:], ACT.Exp)
                fn(e3[:, :, 0:half], e3[:, :, 0:half], ACT.Exp, scale=-1.0).then_inc(ex_done, 1)
            act.wait_ge(d_done, LEVELS + 1)
            fn(ex, ex, ACT.Exp)
            fn(x0, cum, ACT.Exp)
            fn(gm, gm, ACT.Exp)
            fn(el[:, 0:16], cum[:, P - 1::P], ACT.Exp).then_inc(ex_done, 1)
            for _b in range(5):
                empty(kdT[:, (4, 0, 1, 2, 3)[_b], :])
            for b in range(NB):
                empty(o_rec[:, b, :])
            for k in range(2):
                act.wait_ge(ms_done, 2 + k)
                fn(rt[:, 0:16], ss[:, 0:16], ACT.Sqrt).then_inc(rt_done, 1)
            act.wait_ge(b_free, B_END["o1"])
            for b in range(NB):
                last = fn(xn[:, b, :], h[:, b, :], ACT.Square, accum_out=ss[:, b:b + 1])
            last.then_inc(sq_done, 1)
            act.wait_ge(ms_done, 4)
            fn(rt[:, 0:NB], ss[:, 0:NB], ACT.Sqrt).then_inc(rt_done, 1)
            for b in range(NB):
                for g in range(2):
                    empty(xnT[:, 4 * g:4 * g + 4, P * b:P * (b + 1)], view=lambda x: cut(x, 4, P))
            for i in range(4):
                for j in range(4):
                    empty(qp[:, j, :])
                for b in range(NB):
                    empty(sc[:, b, W * i:W * (i + 1)])
            for b in range(NB + 1):
                if b:
                    act.wait_ge(dots_ready, b)
                    fn(dots, dots, ACT.Gelu).then_inc(hid_ready, 1)
                if b < NB:
                    act.wait_ge(gmax, b + 1)
                    fn(gate[:, b % 2, :], gate[:, b % 2, :], ACT.Exp).then_inc(gexp, 1)
            act.wait_ge(y_free, NB)
            for b in range(NB):
                last = fn(xn[:, b, :], h[:, b, :], ACT.Square, accum_out=ss[:, b:b + 1])
            last.then_inc(sq_done, 1)
            act.wait_ge(ms_done, 5)
            fn(rt[:, 0:NB], ss[:, 0:NB], ACT.Sqrt).then_inc(rt_done, 1)
            act.wait_ge(h1_done, 1)
            for b in range(NB):
                last = fn(an2[:, b, :], h[:, b, :], ACT.Square, accum_out=ss[:, b:b + 1])
            last.then_inc(sq_done, 1)
            act.wait_ge(ms_done, 6)
            fn(rt[:, 0:NB], ss[:, 0:NB], ACT.Sqrt).then_inc(rt_done, 1)
            act.wait_ge(rs_done, 6)
            act.wait_ge(sq_done, 4)
            for b in range(NB):
                fn(an2[:, b, :], h[:, b, :], ACT.Copy, scale=rs[:, b:b + 1]).then_inc(rows_done, 1)
            act.wait_ge(b_free, B_END["trH"])
            for i in range(4):
                empty(q2T[:, i, :], scale=DH2 ** -0.5)
            for i in range(4):
                empty(k2T[:, i, :])
            for b in range(NB):
                empty(v2[:, b, :])

            def log_part(n):
                e = ae[:, n % 2, 0:P * (UNITS2[n][0] + 1)]
                act.wait_ge(zs_ready, n + 1)
                step(fn(e, zs[:, n % 2, 0:P * (UNITS2[n][0] + 1)], ACT.Abs))
                step(fn(e, e, ACT.Exp, scale=-1.0))
                fn(e, e, ACT.Ln, bias=1.0).then_inc(l_ready, 1)

            side = {"vb": vb, "ub": ub, "za": za, "zb": zb, "ga0": ga[:, :, 0:W], "ga1": ga[:, :, W:D],
                    "gb0": gb[:, :, 0:W], "gb1": gb[:, :, W:D]}
            log_part(0)
            for n, (b, hh) in enumerate(UNITS2):
                nk = P * (b + 1)
                act.wait_ge(wl_ready, n + 1)
                fn(ae[:, n % 2, 0:nk], zs[:, n % 2, 0:nk], ACT.Exp).then_inc(w_ready, 1)
                if n + 1 < len(UNITS2):
                    log_part(n + 1)
                empty(w2T[:, n % 2, 0:nk], cols=slice(0, nk))
                c_empty(side[SIDE[n // NB]][:, n % NB, :])
                empty(o2[:, b, DH2 * hh:DH2 * (hh + 1)], cols=slice(0, DH2))
                if n == 2 * NB - 1:
                    act.wait_ge(c_free, C_END["ub"])
                    fn(vb, vb, ACT.Gelu_apprx_tanh)
                    fn(ub, ub, ACT.Gelu_apprx_tanh).then_inc(fn_done, 1)
                if n == 2 * NB + 2:
                    act.wait_ge(ln_r, 1)
                    fn(gst[:, 2, :], gst[:, 1, :], ACT.Sqrt).then_inc(ln_rt, 1)
                if n == 4 * NB - 1:
                    act.wait_ge(c_free, C_END["zb"])
                    fn(za, za, ACT.Silu)
                    fn(zb, zb, ACT.Silu).then_inc(fn_done, 1)
                    act.wait_ge(ln_v, 1)
            for g in range(2):
                for b in range(NB):
                    empty(yT[:, 4 * g:4 * g + 4, P * b:P * (b + 1)], view=lambda x: cut(x, 4, P))
            act.wait_ge(c_free, C_END["gb1"])
            fn(ga, ga, ACT.Sigmoid)
            fn(gb, gb, ACT.Sigmoid).then_inc(fn_done, 1)
            for b in range(NB):
                for g in range(2):
                    empty(mT[:, 4 * g:4 * g + 4, P * b:P * (b + 1)], view=lambda x: cut(x, 4, P))
            act.wait_ge(b_free, B_END["w1"])
            for b in range(NB):
                last = fn(gb[:, b, :], h[:, b, :], ACT.Square, accum_out=ss[:, b:b + 1])
            last.then_inc(sq_done, 1)
            act.wait_ge(ms_done, 7)
            fn(rt[:, 0:NB], ss[:, 0:NB], ACT.Sqrt).then_inc(rt_done, 1)

        @block.vector
        def _(dve):
            nb_, own = [0], [0]
            V = nc.vector

            def bank():
                dve.wait_ge(b_full, nb_[0] + 1)
                nb_[0] += 1
                return pb[(nb_[0] - 1) % RB]

            def emptied(ins):
                ins.then_inc(b_free, 1)
                dve.wait_ge(b_free, nb_[0])
    
            def step(ins, it=None):
                own[0] += 1
                ins.then_inc(dve_s, 1)
                if it is None:
                    dve.wait_ge(dve_s, own[0])
                else:
                    dve.wait_ge(dve_s, it * HEAD_STEPS + own[0])
                    V.nop(nofuse=True)

            def mean_root(k, n, count):
                V.tensor_scalar(ss[:, 0:n], ss[:, 0:n], 1.0 / count, EPS, ALU.mult, ALU.add).then_inc(ms_done, 1)
                dve.wait_ge(rt_done, k)
                V.reciprocal(rs[:, 0:n], rt[:, 0:n]).then_inc(rs_done, 1)
                dve.wait_ge(rs_done, k)

            def copy_level(l):
                for b in range(NB):
                    emptied(V.copy_predicated(cut(AT[:, b, :], HR, P),
                                              masks[:, l, :].bitcast(I32).unsqueeze(1).broadcast_to([P, HR, P]),
                                              cut(bank()[:, :], HR, P)))

            step(V.memset(ss, 1.0))
            dve.wait_ge(sq_done, 1)
            mean_root(1, 5, D)
            dve.wait_ge(ld_c, C1)
            step(V.tensor_tensor(lbt[:, 2, :], lblog[:, 0, :], lblog[:, 1, :], ALU.max))
            step(V.tensor_tensor(lbt[:, 0, :], lblog[:, 0, :], lbt[:, 2, :], ALU.subtract))
            step(V.tensor_tensor(lbt[:, 1, :], lblog[:, 1, :], lbt[:, 2, :], ALU.subtract))
            step(V.tensor_tensor(lam_in[:, 0, :], lam_in[:, 0, :], lam_in[:, 1, :], ALU.mult))
            step(V.tensor_tensor(lam_in[:, 2, :], lam_in[:, 2, :], lam_in[:, 3, :], ALU.mult))
            step(V.reduce_sum(lamt[:, 0:1], lam_in[:, 0, :], AXX))
            V.reduce_sum(lamt[:, 1:2], lam_in[:, 2, :], AXX).then_inc(prm_d, 1)
            V.memset(kmt, 0.0)
            V.memset(S, 0.0)
            step(V.memset(AT, 0.0))
            dve.wait_ge(prm_a, 2)
            step(V.tensor_tensor(lbt[:, 2, :], lbt[:, 0, :], lbt[:, 1, :], ALU.add))
            step(V.reciprocal(lbt[:, 2, :], lbt[:, 2, :]))
            step(V.tensor_tensor(lb, lbt[:, 0, :], lbt[:, 2, :], ALU.mult))
            step(V.tensor_scalar(olb, lb, -1.0, 1.0, ALU.mult, ALU.add))
            step(V.tensor_tensor(lam, lamt[:, 0:1], lamt[:, 1:2], ALU.subtract))
            step(V.tensor_scalar(lam, lam, LAM0, None, ALU.add))
            for b in [4] + list(range(NB)):
                n = NM if b == 4 else P
                lo = 0 if b == 4 else NM + P * b
                for g in range(2):
                    ps = cut(bank()[:, :], 4, P)[:, :, 0:n]
                    emptied(V.tensor_tensor(aT[:, 4 * g:4 * g + 4, lo:lo + n], ps,
                                    normw[:, 4 * g:4 * g + 4].unsqueeze(2).broadcast_to([P, 4, n]), ALU.mult))
            dve.wait_ge(a_free, A_END["ak"])
            step(V.tensor_tensor(kT, raw, cosT.unsqueeze(1).broadcast_to([P, HA, T]), ALU.mult))
            for i in range(HA):
                ps = bank()
                step(V.tensor_tensor(St, ps[:, 0:SEQ], sinT[:, NM:T], ALU.mult))
                emptied(V.tensor_tensor(kT[:, i, NM:T], kT[:, i, NM:T], St, ALU.add))
            ps = cut(bank()[:, 0:HA * NM], HA, NM)
            step(V.tensor_tensor(cut(St[:, 0:HA * NM], HA, NM), ps, sinT[:, 0:NM].unsqueeze(1).broadcast_to([P, HA, NM]),
                                 ALU.mult))
            emptied(V.tensor_tensor(kT[:, :, 0:NM], kT[:, :, 0:NM], cut(St[:, 0:HA * NM], HA, NM), ALU.add))
            dve.wait_ge(a_free, A_END["rf"])
            for i in range(HR):
                for x in (_kr[:, SEQ * i:SEQ * (i + 1)], kmt[:, NM * i:NM * (i + 1)]):
                    last = V.tensor_scalar(x, x, olb[:, i:i + 1], lb[:, i:i + 1], ALU.mult, ALU.add)
            last.then_inc(f_raw, 1)
            dve.wait_ge(f_raw, 1)
            dve.wait_ge(g_done, 1)
            step(V.tensor_scalar(_kr, _kr, -1.0, 1.0, ALU.mult, ALU.add))
            step(V.tensor_scalar(kmt[:, 0:HR * NM], kmt[:, 0:HR * NM], -1.0, 1.0, ALU.mult, ALU.add))
            step(V.memset(St, 1.0))
            for i in range(HR * NB):
                V.tensor_tensor_scan(cum[:, P * i:P * (i + 1)], St[:, 0:P], x1[:, P * i:P * (i + 1)], 0.0,
                                     ALU.mult, ALU.add)
            for i in range(HR):
                last = V.tensor_tensor_scan(cumm[:, NM * i:NM * (i + 1)], St[:, 0:NM], gm[:, NM * i:NM * (i + 1)], 0.0,
                                            ALU.mult, ALU.add)
            step(last)
            dve.wait_ge(a_free, A_END["aq"])
            step(V.tensor_tensor(qT, raw[:, :, NM:T], cosT[:, NM:T].unsqueeze(1).broadcast_to([P, HA, SEQ]), ALU.mult))
            for i in range(HA):
                ps = bank()
                step(V.tensor_tensor(St, ps[:, 0:SEQ], sinT[:, NM:T], ALU.mult))
                emptied(V.tensor_tensor(qT[:, i, :], qT[:, i, :], St, ALU.add))
            n = 0
            for b in range(NB):
                nk = NM + P * (b + 1)
                dl = NM + P * b
                for hh in range(HA):
                    if n:
                        dve.wait_ge(wt_ready, n)
                    lo = NM if b == NB - 1 else 0
                    for part in range(2):
                        ps = bank()
                        V.tensor_copy(es[:, part, lo:dl], ps[:, 0:dl - lo])
                        emptied(V.tensor_tensor(es[:, part, dl:nk], ps[:, dl - lo:nk - lo], tri, ALU.add))
                    for part in range(2 if lo else 0):
                        emptied(V.tensor_copy(es[:, part, 0:NM], bank()[:, 0:NM]))
                    step(V.tensor_reduce(mx[:, 0, :], es[:, :, 0:nk], AXX, ALU.max))
                    V.tensor_scalar(nm[:, 0, :], mx[:, 0, :], -(DH ** -0.5), None, ALU.mult).then_inc(mx_done, 1)
                    dve.wait_ge(e_done, n + 1)
                    step(V.reciprocal(rr[:, 0, :], rsum[:, 0, :]))
                    step(V.tensor_scalar(rr[:, 0, 1:2], rr[:, 0, 1:2], lam, -1.0, ALU.mult, ALU.mult))
                    if n >= 2:
                        dve.wait_ge(a_free, A_END[f"wt{(n - 2) // HA}{(n - 2) % HA}"])
                    step(V.tensor_scalar(es[:, 0, 0:nk], es[:, 0, 0:nk], rr[:, 0, 0:1], None, ALU.mult))
                    V.scalar_tensor_tensor(wts[:, n % 2, 0:nk], es[:, 1, 0:nk], rr[:, 0, 1:2], es[:, 0, 0:nk],
                                           ALU.mult, ALU.add).then_inc(wt_ready, 1)
                    n += 1
            for l in range(LEVELS):
                half = (P // 2) >> l
                pairs = HR * SEQ // (2 * half)
                c3 = cum.rearrange("p (n s) -> p n s", s=2 * half)
                e3 = ex.rearrange("p (n s) -> p n s", s=2 * half)
                x3 = (x0, x1)[l % 2].rearrange("p (n s) -> p n s", s=2 * half)
                q3 = _qr.rearrange("p (n s) -> p n s", s=2 * half)
                k3 = _kr.rearrange("p (n s) -> p n s", s=2 * half)
                if l:
                    dve.wait_ge(x_ready, l)
                V.tensor_tensor(e3, c3, c3[:, :, half - 1:half].broadcast_to([P, pairs, 2 * half]), ALU.subtract)\
                    .then_inc(d_done, 1)
                if l:
                    copy_level(l - 1)
                dve.wait_ge(ex_done, l + 1)
                V.tensor_tensor(x3[:, :, half:], e3[:, :, half:], q3[:, :, half:], ALU.mult)
                V.tensor_tensor(x3[:, :, 0:half], e3[:, :, 0:half], k3[:, :, 0:half], ALU.mult).then_inc(x_ready, 1)
            for l in (LEVELS - 1, LEVELS):
                copy_level(l)
            dve.wait_ge(x_ready, LEVELS)
            c3 = cum.rearrange("p (n s) -> p n s", s=P)
            cm3 = cumm.rearrange("p (n s) -> p n s", s=NM)
            V.tensor_tensor(cut(gm, HR, NM), cm3[:, :, NM - 1:NM].broadcast_to([P, HR, NM]), cm3, ALU.subtract)
            V.tensor_tensor(ex.rearrange("p (n s) -> p n s", s=P), c3[:, :, P - 1:P].broadcast_to([P, HR * NB, P]), c3,
                            ALU.subtract).then_inc(d_done, 1)
            dve.wait_ge(ex_done, LEVELS + 1)
            V.tensor_tensor(_qr, _qr, x0, ALU.mult)
            V.tensor_tensor(kmt[:, 0:HR * NM], kmt[:, 0:HR * NM], gm, ALU.mult)
            V.tensor_tensor(_kr, _kr, ex, ALU.mult).then_inc(kd_ready, 1)
            dve.wait_ge(kd_ready, 1)
            V.tensor_copy(S, bank()[:, :]).then_inc(s_ready, 1)
            dve.wait_ge(s_ready, 1)
            emptied(V.tensor_copy(St[:, 0:1], S[:, 0:1]))
            for b in range(NB - 1):
                ps = bank()
                dve.wait_ge(a_full, A_END[f"ro{b}"])
                elb = el[:, 0:16].rearrange("p (h b) -> p h b", b=NB)[:, :, b:b + 1].broadcast_to([P, HR, P])
                step(V.tensor_tensor(cut(S, HR, P), cut(S, HR, P), elb, ALU.mult))
                V.tensor_tensor(S, S, ps[:, :], ALU.add).then_inc(s_ready, 1)
                dve.wait_ge(s_ready, b + 2)
                emptied(V.tensor_copy(St[:, 1:2], ps[:, 0:1]))
            for k, (rows, end) in enumerate(((o_att, "o33"), (o_rec, "ro3"))):
                dve.wait_ge(a_free, A_END[end])
                flat = (o_att, o_rec)[k].rearrange("p b n -> p (b n)")
                step(V.tensor_tensor(cum, flat, flat, ALU.mult))
                step(V.tensor_reduce(ss[:, 0:16], cut(cum, 16, P), AXX, ALU.add))
                mean_root(2 + k, 16, P)
                if k == 0:
                    step(V.tensor_scalar(rs[:, 0:16], rs[:, 0:16], 1.0 - LAM0, None, ALU.mult))
                last = V.tensor_tensor(cut(flat, 16, P), cut(flat, 16, P), rs[:, 0:16].unsqueeze(2).broadcast_to([P, 16, P]),
                                       ALU.mult)
                if k == 1:
                    step(last)
                    last = V.tensor_tensor(o_rec, o_rec, rg, ALU.mult)
                last.then_inc(mixrows, 1)
                dve.wait_ge(mixrows, k + 1)
            for k in range(2):
                for b in range(NB):
                    ps = cut(bank()[:, :], 4, P)
                    wgt = recw.unsqueeze(2).broadcast_to([P, 4, P]) if k else sublnw.unsqueeze(2).broadcast_to([P, 4, P])
                    emptied(V.tensor_tensor(mixT[:, 4 * k:4 * k + 4, P * b:P * (b + 1)], ps, wgt, ALU.mult))
            for j in range(2):
                for b in range(NB):
                    emptied(V.tensor_tensor(h[:, b, W * j:W * (j + 1)], h[:, b, W * j:W * (j + 1)], bank()[:, :], ALU.add))
            dve.wait_ge(sq_done, 2)
            mean_root(4, NB, D)
            dve.wait_ge(ld_p, CP)
            for b in range(NB):
                V.scalar_tensor_tensor(xn[:, b, :], h[:, b, :], rs[:, b:b + 1], ffnw, ALU.mult, ALU.mult)\
                    .then_inc(xn_done, 1)
            dve.wait_ge(xn_done, NB)

            def best_keys(b, it, first, a):
                if a == 0:
                    step(V.tensor_copy(rows2.rearrange("p a k -> p (a k)"),
                                       sc[:, b, bass.ds(it * (2 * NK) + first * 2 * NK, 2 * NK)]), it)
                step(V.max(sv[:, a, 0:8], rows2[:, a, :]), it)
                V.max_index(si[:, a, 0:8], sv[:, a, 0:8], rows2[:, a, :])
                step(V.match_replace(s2, sv[:, a, 0:8], rows2[:, a, :], FMIN), it)
                step(V.max(sv[:, a, 8:16], s2), it)
                step(V.max_index(si[:, a, 8:16], sv[:, a, 8:16], s2), it)

            def best_sums(b, it, first):
                V.tensor_copy(sif, si)
                step(V.tensor_tensor(cut(cand, TOP, TOP), sv[:, 0, :].unsqueeze(2).broadcast_to([P, TOP, TOP]),
                                     sv[:, 1, :].unsqueeze(1).broadcast_to([P, TOP, TOP]), ALU.add), it)
                step(V.max(top_s[:, 0:8], cand), it)
                V.max_index(pos[:, 0:8], top_s[:, 0:8], cand)
                step(V.match_replace(c2, top_s[:, 0:8], cand, FMIN), it)
                step(V.max(top_s[:, 8:16], c2), it)
                step(V.max_index(pos[:, 8:16], top_s[:, 8:16], c2), it)
                step(V.tensor_scalar(gate[:, b % 2, bass.ds(it * TOP + first * TOP, TOP)], top_s, top_s[:, 0:1], None,
                                     ALU.subtract), it)

            def experts(b, it, first):
                for a in range(2):
                    if a == 0:
                        step(V.tensor_scalar(pi, pos, 4, None, ALU.logical_shift_right), it)
                    else:
                        step(V.tensor_scalar(pi, pos, TOP - 1, None, ALU.bitwise_and), it)
                    step(V.tensor_tensor(oh, pi.unsqueeze(2).broadcast_to([P, TOP, TOP]),
                                         iota.unsqueeze(1).broadcast_to([P, TOP, TOP]), ALU.is_equal), it)
                    step(V.tensor_tensor(oh, oh, sif[:, a, :].unsqueeze(1).broadcast_to([P, TOP, TOP]), ALU.mult), it)
                    step(V.tensor_reduce(e01[:, a, :], oh, AXX, ALU.add), it)
                step(V.scalar_tensor_tensor(idxu[:, b % 3, bass.ds(it * TOP + first * TOP, TOP)], e01[:, 0, :],
                                            float(NK), e01[:, 1, :], ALU.mult, ALU.add), it)

            def gates(b):
                V.tensor_copy(mark[:, 1:2], gate[:, b % 2, 0:1]).then_inc(gmax, 1)
                dve.wait_ge(gexp, b + 1)
                g3 = cut(gate[:, b % 2, :], HP, TOP)
                step(V.tensor_reduce(gsum[:, 0:HP], g3, AXX, ALU.add))
                step(V.reciprocal(gsum[:, HP:2 * HP], gsum[:, 0:HP]))
                step(V.tensor_tensor(g3, g3, gsum[:, HP:2 * HP].unsqueeze(2).broadcast_to([P, HP, TOP]), ALU.mult))

            for i in range(4):
                dve.wait_ge(a_free, A_END[f"sc{i}"])
                base = own[0]
                with dve.Fori(0, 2) as it:
                    best_keys(0, it, 2 * i, 0)
                    best_keys(0, it, 2 * i, 1)
                    best_sums(0, it, 2 * i)
                    experts(0, it, 2 * i)
                assert own[0] - base == HEAD_STEPS, own[0] - base
                own[0] += HEAD_STEPS
            V.tensor_copy(mark[:, 0:1], gate[:, 0, 0:1]).then_inc(idx_ready, 1)
            gates(0)
            V.memset(zero, 0.0).then_inc(v_free, 2 * RING)
            V.memset(d8, 0.0).then_inc(u_free, RING)
            dve.wait_ge(u_free, RING)
            for stage in range(NB + 1):
                bb, bv = stage, stage - 1
                with dve.Fori(0, ROUNDS // 2) as it:
                    for turn in range(2):
                        if stage:
                            dve.wait_ge(v_free, it * (2 * RING) + (RING + bv * SLOTS + turn * RING))
                            V.tensor_tensor(dg[:, turn, :, :], ident.unsqueeze(1).broadcast_to([P, RING, P]),
                                            hid[:, bv % 2, bass.ds(it * (2 * RING) + turn * RING, RING)].unsqueeze(2)
                                            .broadcast_to([P, RING, P]), ALU.mult).then_inc(dg_ready, 1)
                        for s in range(RING if stage < NB else 0):
                            dve.wait_ge(u_full[s], it * 32 + (bb * ROUNDS * 16 + 16 * turn + 16))
                            V.tensor_tensor_reduce(ur[:, s, :], ur[:, s, :], xn[:, bb, :], 1.0, 0.0, ALU.mult, ALU.add,
                                                   d8[:, s:s + 1]).then_inc(u_free, 1)
                            if stage < NB - 1 and s % 4 == 3:
                                if turn == 0:
                                    best_keys(bb + 1, it, 0, s // 4)
                                elif s == 3:
                                    best_sums(bb + 1, it, 0)
                                else:
                                    experts(bb + 1, it, 0)
                        if stage < NB:
                            dve.wait_ge(u_free, it * (2 * RING) + (RING + bb * SLOTS + (turn + 1) * RING))
                            V.tensor_copy(dots[:, bass.ds(it * (2 * RING) + turn * RING, RING)], d8).then_inc(fv, 1)
                            dve.wait_ge(fv, it * 2 + (bb * ROUNDS + turn + 1))
                if stage < NB - 1:
                    own[0] += HEAD_STEPS * (ROUNDS // 2 - 1)
                    V.tensor_copy(mark[:, 0:1], gate[:, (bb + 1) % 2, 0:1]).then_inc(idx_ready, 1)
                if stage < NB:
                    V.memset(d8, 0.0).then_inc(dots_ready, 1)
                    dve.wait_ge(hid_ready, bb + 1)
                    step(V.tensor_tensor(hid[:, bb % 2, :], dots, gate[:, bb % 2, :], ALU.mult))
                if stage < NB - 1:
                    gates(bb + 1)
                if stage:
                    dve.wait_ge(y_full, stage)
                    for c in range(2):
                        last = V.tensor_copy(h[:, bv, W * c:W * (c + 1)], py[c][:, :])
                    last.then_inc(y_free, 1)
            dve.wait_ge(sq_done, 3)
            mean_root(5, NB, D)
            dve.wait_ge(ld_p, CP + 16)
            for b in range(NB):
                last = V.scalar_tensor_tensor(h[:, b, :], h[:, b, :], rs[:, b:b + 1], finw1, ALU.mult, ALU.mult)
            last.then_inc(h1_done, 1)
            dve.wait_ge(sq_done, 4)
            mean_root(6, NB, D)
            for b in range(NB):
                for g in range(2):
                    ps = cut(bank()[:, :], 4, P)
                    emptied(V.tensor_tensor(hT[:, 4 * g:4 * g + 4, P * b:P * (b + 1)], ps,
                                    normg2[:, 4 * g:4 * g + 4].unsqueeze(2).broadcast_to([P, 4, P]), ALU.mult))
            dve.wait_ge(ld_q, CQ)
            V.memset(wsT[GC:P, :, 0:GC], 0.0)
            step(V.memset(ones, 1.0))
            vflat = vb.rearrange("p b n -> p (b n)")
            NGB = NB * NG
            v3 = cut(vflat, NGB, GC)
            c3 = cut(vc, NGB, GC)

            def layer_norm(part):
                if part == 0:
                    dve.wait_ge(fn_done, 1)
                    step(V.tensor_reduce(gst[:, 0, :], v3, AXX, ALU.add))
                    step(V.tensor_scalar(gst[:, 0, :], gst[:, 0, :], 1.0 / GC, None, ALU.mult))
                    step(V.tensor_tensor(c3, v3, gst[:, 0, :].unsqueeze(2).broadcast_to([P, NGB, GC]), ALU.subtract))
                elif part == 1:
                    step(V.tensor_tensor(vq, vc, vc, ALU.mult))
                    step(V.tensor_reduce(gst[:, 1, :], cut(vq, NGB, GC), AXX, ALU.add))
                    V.tensor_scalar(gst[:, 1, :], gst[:, 1, :], 1.0 / GC, EPS, ALU.mult, ALU.add).then_inc(ln_r, 1)
                elif part == 2:
                    dve.wait_ge(ln_rt, 1)
                    step(V.reciprocal(gst[:, 3, :], gst[:, 2, :]))
                    step(V.tensor_tensor(c3, c3, gst[:, 3, :].unsqueeze(2).broadcast_to([P, NGB, GC]), ALU.mult))
                else:
                    step(V.tensor_tensor(cut(vc, NB, W), cut(vc, NB, W), lng.unsqueeze(1).broadcast_to([P, NB, W]),
                                         ALU.mult))
                    V.tensor_tensor(vb, cut(vc, NB, W), lnb.unsqueeze(1).broadcast_to([P, NB, W]), ALU.add)\
                        .then_inc(ln_v, 1)

            def spatial_rows(b):
                ps = bank()
                step(V.tensor_tensor(cut(up_t, NG, GC), cut(ps[:, :], NG, GC), bs.unsqueeze(2).broadcast_to([P, NG, GC]),
                                     ALU.add))
                step(V.tensor_tensor(up_t, up_t, ub[:, b, :], ALU.mult))
                emptied(V.tensor_tensor(vb[:, b, :], up_t, zb[:, b, :], ALU.mult))

            def take_z(n):
                b = UNITS2[n][0]
                z = zs[:, n % 2, :]
                ps = bank()
                if n >= 2:
                    dve.wait_ge(w_ready, n - 1)
                if b:
                    V.tensor_copy(z[:, 0:P * b], ps[:, 0:P * b])
                emptied(V.tensor_tensor(z[:, P * b:P * (b + 1)], ps[:, P * b:P * (b + 1)], stri, ALU.add))
                V.tensor_copy(sp_[:, n % 2, 0:1], z[:, 0:1]).then_inc(zs_ready, 1)

            def log_weights(n):
                nk = P * (UNITS2[n][0] + 1)
                z, soft = zs[:, n % 2, 0:nk], sp_[:, n % 2, 0:nk]
                dve.wait_ge(l_ready, n + 1)
                step(V.scalar_tensor_tensor(soft, z, 0.0, ae[:, n % 2, 0:nk], ALU.max, ALU.add))
                step(V.tensor_tensor_scan(rcs[:, 0:nk][:, ::-1], ones[:, 0:nk], soft[:, ::-1], 0.0, ALU.mult, ALU.add))
                V.tensor_tensor(z, z, rcs[:, 0:nk], ALU.subtract).then_inc(wl_ready, 1)

            take_z(0)
            for n in range(len(UNITS2)):
                log_weights(n)
                if n + 1 < len(UNITS2):
                    take_z(n + 1)
                if 2 * NB <= n < 2 * NB + 2:
                    layer_norm(n - 2 * NB)
                if 2 * NB + 3 <= n < 2 * NB + 5:
                    layer_norm(n - 2 * NB - 1)
                if n in SGU_AT:
                    if SGU_AT[n] == 0:
                        dve.wait_ge(fn_done, 2)
                    spatial_rows(SGU_AT[n])
                if n == len(UNITS2) - 3:
                    dve.wait_ge(a_free, A_END[f"o2_{3 * H2 - 1}"])
                    V.tensor_tensor(o2[:, 0:3, :], o2[:, 0:3, :], za[:, 0:3, :], ALU.mult).then_inc(y_ready, 1)
            dve.wait_ge(a_free, A_END[f"o2_{len(UNITS2) - 1}"])
            V.tensor_tensor(o2[:, 3, :], o2[:, 3, :], za[:, 3, :], ALU.mult).then_inc(y_ready, 1)
            dve.wait_ge(y_ready, 2)
            dve.wait_ge(fn_done, 3)
            for j in range(2):
                for b in range(NB):
                    gg, gh = ga[:, b, W * j:W * (j + 1)], gb[:, b, W * j:W * (j + 1)]
                    emptied(V.tensor_tensor(gg, gg, bank()[:, :], ALU.mult))
                    step(V.tensor_tensor(gh, gh, bank()[:, :], ALU.mult))
                    emptied(V.tensor_tensor(gg, gg, gh, ALU.add))
            for j in range(2):
                for b in range(NB):
                    emptied(V.tensor_tensor(h[:, b, W * j:W * (j + 1)], h[:, b, W * j:W * (j + 1)], bank()[:, :], ALU.add))
            dve.wait_ge(sq_done, 5)
            mean_root(7, NB, D)
            for b in range(NB):
                V.scalar_tensor_tensor(h[:, b, :], h[:, b, :], rs[:, b:b + 1], finw, ALU.mult, ALU.mult)\
                    .then_inc(fin_ready, 1)

        @block.gpsimd
        def _(pool):
            steps = 0
            for stage in range(NB + 1):
                bu, bv = stage, stage - 1
                if stage < NB:
                    pool.wait_ge(idx_ready, stage + 1)
                per = (stage < NB) + (stage > 0)
                with pool.Fori(0, SLOTS // (2 * RING)) as it:
                    for turn in range(2):
                        at = it * (2 * RING) + turn * RING
                        if stage < NB:
                            nc.gpsimd.tensor_copy(iru[:, turn, :], idxu[:, bu % 3, bass.ds(at, RING)]).then_inc(pool_s, 1)
                        if stage:
                            nc.gpsimd.tensor_copy(irv[:, turn, :], idxu[:, bv % 3, bass.ds(at, RING)]).then_inc(pool_s, 1)
                        pool.wait_ge(pool_s, it * (2 * per) + (steps + per * (turn + 1)))
                        nc.gpsimd.nop(nofuse=True)
                        for s in range(RING):
                            if stage < NB:
                                pool.wait_ge(u_free, it * (2 * RING) + (bu * SLOTS + turn * RING + s + 1))
                                nc.gpsimd.nop(nofuse=True)
                                nc.gpsimd.indirect_dma_start(ur[:, s, :], None, t["peer_u"], bass.IndirectOffsetOnAxis(
                                    ap=iru[:, turn, s:s + 1].bitcast(U32), axis=0)).then_inc(u_full[s], 16)
                            if stage:
                                pool.wait_ge(v_free, it * (2 * RING) + (RING + bv * SLOTS + turn * RING + s + 1))
                                nc.gpsimd.nop(nofuse=True)
                                nc.gpsimd.indirect_dma_start(vr_[:, s, :], None, t["peer_v"], bass.IndirectOffsetOnAxis(
                                    ap=irv[:, turn, s:s + 1].bitcast(U32), axis=0)).then_inc(v_full[s], 16)
                steps += (SLOTS // RING) * per


def word(ap):
    return ap.offset


def shape_constants():
    d = 2 * (np.arange(DH // 2, dtype=np.float32))
    inv = (np.float32(10000.0) ** (-d / np.float32(DH))).astype(np.float32)
    ang = np.arange(T, dtype=np.float32)[:, None] * inv[None, :]
    ang = np.concatenate([ang, ang], axis=-1)
    cos, sin = np.cos(ang).T.astype(np.float32), np.sin(ang).T.astype(np.float32)
    rot = np.zeros((P, P), np.float32)
    half = DH // 2
    for part in range(2):
        for i in range(half):
            rot[DH * part + half + i, DH * part + i] = -1.0
            rot[DH * part + i, DH * part + half + i] = 1.0
    s, q = np.arange(P)[:, None], np.arange(P)[None, :]
    masks = []
    for l in range(LEVELS):
        hf = (P // 2) >> l
        masks.append((s // (2 * hf) == q // (2 * hf)) & (s % (2 * hf) < hf) & (q % (2 * hf) >= hf))
    masks.append(s == q)
    return {
        "ident": np.eye(P, dtype=np.float32),
        "cosT": np.concatenate([cos, cos], 0), "sinT": np.concatenate([sin, sin], 0), "rotm": rot,
        "masks": np.ascontiguousarray(np.stack(masks, 1).astype(np.int32)),
        "tri": np.where(q <= s, 0.0, NEG).astype(np.float32),
        "stri": np.where(q < s, 0.0, NEG).astype(np.float32),
        "iota": np.ascontiguousarray(np.broadcast_to(np.arange(TOP, dtype=np.float32), (P, TOP))),
    }


def kernel(**inputs):
    import numpy as _np
    import concourse.bacc as _bacc
    from concourse.bass_utils import run_bass_kernel_spmd as _run

    i = {k: _np.asarray(v) for k, v in inputs.items()}
    c = _np.ascontiguousarray
    rep = lambda a: c(_np.broadcast_to(a, (P,) + a.shape))
    arrays = {
        "x": i["x"][0], "meta": i["meta_tokens"], "w_in": i["w_in"][0], "w_out": i["w_out"][0],
        "wq": i["peer_w_query"][0], "peer_u": i["peer_u"][0], "peer_v": i["peer_v"][0],
        "w_in_2": i["w_in_2"][0], "w_up_a": i["w_up_a_2"][0], "w_up_b": i["w_up_b_2"][0], "w_out_2": i["w_out_2"][0],
        "normw": c(i["mix_norm_w"].reshape(KT, P).T), "normg2": c(i["norm_g_2"].reshape(KT, P).T),
        "sublnw": c(i["diff_subln_w"].reshape(P, 1)), "recw": c(i["rec_norm_w"].reshape(HR, P).T),
        "lam_in": rep(_np.stack([i["diff_lambda_q1"][0], i["diff_lambda_k1"][0],
                                 i["diff_lambda_q2"][0], i["diff_lambda_k2"][0]])),
        "lblog": c(i["rec_lb_logits"].reshape(2, HR, P).transpose(2, 0, 1)),
        "skT": c(i["peer_subkeys"].reshape(2 * HP, NK, P).transpose(2, 0, 1)),
        "ffnw": i["ffn_norm_w"], "finw": i["final_norm_g_2"].reshape(1, D),
        "lng": i["sgu_ln_g_2"].reshape(1, W), "lnb": i["sgu_ln_b_2"].reshape(1, W),
        "wsT": c(i["w_spatial_2"][0].transpose(2, 0, 1)), "bs": c(i["b_spatial_2"][0].T),
    }
    arrays.update(shape_constants())
    arrays["finw1"] = i["final_norm_w"].reshape(1, D)
    nc = _bacc.Bacc("TRN2", target_bir_lowering=False, num_devices=1)
    t, feed = {}, {}
    for name, a in arrays.items():
        a = c(a)
        feed[f"in_{name}"] = a
        t[name] = nc.dram_tensor(f"in_{name}", a.shape, mybir.dt.from_np(a.dtype), kind="ExternalInput").ap()
    out = nc.dram_tensor("out_0", (SEQ, D), F32, kind="ExternalOutput").ap()
    build(nc, t, out)
    r = _run(nc, [feed], core_ids=[0])
    return r.results[0]["out_0"].reshape(1, SEQ, D)
```

```python
from contextlib import ExitStack

import numpy as np
import concourse.bass as bass
from concourse import mybir

ALU = mybir.AluOpType
ACT = mybir.ActivationFunctionType
AXX = mybir.AxisListType.X
F32 = mybir.dt.float32
U32 = mybir.dt.uint32
I32 = mybir.dt.int32

P = 128
D = 1024
KT = D // P
SEQ = 512
NB = SEQ // P
NM = 16
T = NM + SEQ
W = 512
HA, DH = 4, 64
HR = 4
HEAD_STEPS = 14
LEVELS = 7
HP = 8
NK = 128
TOP = 16
SLOTS = HP * TOP
RING = 8
ROUNDS = SLOTS // RING
LAG = 5
LEAD = 2
HEADS = NB * HP
H2, DH2 = 8, 64
NG, GC = 8, 64
EPS = 1e-6
NEG = -1e30
FMIN = -3.4028234663852886e38
LAM0 = 0.2
AREA = 39700
RA = RB = 3
RC = 2

CHUNKS = ["rf", "rq", "ak", "av", "aq", "ri", "rg", "o0", "o1", "p0", "p1", "p2", "p3", "r0", "r1", "r2", "r3",
          "q2", "k2", "v2", "vb", "ub", "za", "zb", "ga0", "ga1", "gb0", "gb1", "up0", "up1", "w0", "w1"]
SIDE = ["vb", "ub", "za", "zb", "ga0", "ga1", "gb0", "gb1"]
UNITS2 = [(b, hh) for b in range(NB) for hh in range(H2)]
SGU_AT = {18: 0, 21: 1, 24: 2, 27: 3}
WIN_AT = {"aq": 0, "ak": 1, "av": 2, "rq": 3, "rf": 4, "ri": 5, "rg": 6}
WIN2_AT = {n: i for i, n in enumerate(["q2", "k2", "v2", "za", "ub", "vb", "zb", "ga0", "ga1", "gb0", "gb1"])}

STEPS1 = [("ak", 0), ("ak", 1), "lv0", ("ak", 2), "lv1", ("ak", 3), ("ak", 4), "lv2", ("av", 0), "rotk", ("av", 1), "lv3",
          ("av", 2), ("av", 3), "lv4", ("av", 4), ("aq", 0), "lv5", ("aq", 1), "lv6", ("aq", 2), "lv7", ("aq", 3), "rotq"]
UNITS = [(b, hh) for b in range(NB) for hh in range(HA)]
SIDE_AT = {3: ("ri", 0), 4: ("ri", 1), 5: ("ri", 2), 6: ("ri", 3), 7: ("ri", 4),
           12: ("rg", 0), 13: ("rg", 1), 14: ("rg", 2), 15: ("rg", 3)}
STATE_AT = {8: None, 9: 0, 11: 1, 13: 2, 15: 3}
KDT_AT = 5

JOBS_A = [("rf", 5), ("rq", 4), ("ak", 5), ("av", 5), ("aq", 4)]
JOBS_B = [("trA", 10)]
for _s in STEPS1:
    if isinstance(_s, str):
        JOBS_B += [(_s, {"rotk": 5}.get(_s, 4))]
STATE_JOBS = []
JOBS_B.append(("s00", 2))
for _n, (_b, _h) in enumerate(UNITS):
    if _n + 1 < len(UNITS):
        JOBS_B.append(("s%d%d" % UNITS[_n + 1], 4 if UNITS[_n + 1][0] == NB - 1 else 2))
    if _n in STATE_AT and _n + 1 < len(UNITS):
        JOBS_B.append((f"st_{STATE_AT[_n]}", 1))
    JOBS_A.append((f"wt{_b}{_h}", 2 if _b == NB - 1 else 1))
    if _n in STATE_AT and STATE_AT[_n] is not None:
        JOBS_A.append((f"ro{STATE_AT[_n]}", 1))
    if _n in STATE_AT and _n + 1 < len(UNITS):
        STATE_JOBS.append(_n)
    JOBS_A.append((f"o{_b}{_h}", 1))
    if _n == KDT_AT:
        JOBS_A += [("kdt", NB + 1)]
JOBS_C = [("ri", 5), ("rg", 4)]
JOBS_B += [("mixt", 2 * NB), ("o0", 2 * NB - 1), ("o1", 1)]
JOBS_A += [("xnt", 2 * NB)]
for _i in range(4):
    JOBS_A += [(f"p{_i}", 1)] + [(f"sc{_i - 1}", 1)] * (_i > 0)
JOBS_A += [("sc3", 1)]
for _i in range(4):
    JOBS_A += [(f"r{_i}", 4), (f"sr{_i}", NB - 1)]
JOBS_B += [("trH", 2 * NB)]
JOBS_A += [("q2", 4), ("k2", 4), ("v2", 4)]
JOBS_B += [("z0", 1)]
for _n in range(len(UNITS2)):
    if _n + 1 < len(UNITS2):
        JOBS_B += [(f"z{_n + 1}", 1)]
    if _n in SGU_AT:
        JOBS_B += [(f"sgu{SGU_AT[_n]}", 1)]
    JOBS_A += [(f"w2_{_n}", 1), (f"o2_{_n}", 1)]
for _c in SIDE:
    JOBS_C += [(_c, NB)]
JOBS_A += [("yt", 2 * NB)]
JOBS_B += [("up0", 2 * NB), ("up1", 2 * NB)]
JOBS_A += [("mt", 2 * NB)]
JOBS_B += [("w0", NB), ("w1", NB)]


def ends(jobs):
    at, out = 0, {}
    for name, n in jobs:
        assert name not in out
        at += n
        out[name] = at
    return out


A_END = ends(JOBS_A)
B_END = ends(JOBS_B)
C_END = ends(JOBS_C)


class Arena:

    def __init__(self, tensor, at, end):
        self.tensor, self.at, self.end = tensor, at, end

    def take(self, n):
        ap = self.tensor[:, self.at:self.at + n]
        self.at += n
        assert self.at <= self.end, (self.at, self.end)
        return ap


def cut(ap, *dims):
    names = "abcd"[:len(dims)]
    return ap.rearrange(f"p ({' '.join(names)}) -> p {' '.join(names)}", **dict(zip(names, dims)))


def build(nc, t, out):
    ctx = ExitStack()
    with ctx:
        def sb(name, words, dt=F32):
            return ctx.enter_context(nc.sbuf_tensor(name, [P, words], dt))

        def sem(name):
            return ctx.enter_context(nc.semaphore(name))

        psum_a = [ctx.enter_context(nc.psum_tensor(f"pa{i}", [P, 512], F32)) for i in range(RA)]
        psum_b = [ctx.enter_context(nc.psum_tensor(f"pb{i}", [P, 512], F32)) for i in range(RB)]
        psum_c = [ctx.enter_context(nc.psum_tensor(f"py{i}", [P, 512], F32)) for i in range(2)]

        ident = sb("ident", P)[:, :]
        h = cut(sb("h", NB * D)[:, :], NB, D)
        wbuf = cut(sb("wbuf", 2 * KT * W)[:, :], 2, KT, W)
        small = Arena(sb("small", 768), 0, 768)
        area = sb("area", AREA)

        tri = sb("tri", P)[:, :]
        stri = sb("stri", P)[:, :]
        normw = small.take(KT)
        normg2 = small.take(KT)
        sublnw = small.take(1)
        recw = small.take(HR)
        lam_in = cut(small.take(4 * DH), 4, DH)
        lblog = cut(small.take(2 * HR), 2, HR)
        lb = small.take(HR)
        olb = small.take(HR)
        lbt = cut(small.take(3 * HR), 3, HR)
        lam = small.take(1)
        lamt = small.take(4)
        ss = small.take(16)
        rt = small.take(16)
        rs = small.take(16)
        mx = cut(small.take(4), 2, 2)
        nm = cut(small.take(4), 2, 2)
        rsum = cut(small.take(4), 2, 2)
        rr = cut(small.take(4), 2, 2)
        el = small.take(16 + HR)
        bs = small.take(NG)

        p1 = Arena(area, 0, AREA)
        an_words = p1.take(5 * D)
        an = cut(an_words, 5, D)
        v = cut(an_words[:, 0:5 * W], 5, W)
        rec_v = cut(an_words[:, 5 * W:10 * W], 5, W)
        aT = cut(p1.take(KT * T), KT, T)
        x0 = an_words[:, 5 * W:9 * W]
        kT = cut(p1.take(HA * T), HA, T)
        raw_words = p1.take(HA * T)
        raw = cut(raw_words, HA, T)
        o_att = cut(raw_words[:, 0:NB * W], NB, W)
        qT = cut(p1.take(HA * SEQ), HA, SEQ)
        rec_q = p1.take(HR * SEQ)
        rec_k = p1.take(HR * SEQ)
        rec_k_meta = p1.take(HR * NM + P - NM)
        cum_meta = p1.take(HR * NM)
        g_meta = p1.take(HR * NM)
        cum = p1.take(HR * SEQ)
        x1 = p1.take(HR * SEQ)
        kdT = cut(p1.take(5 * W), 5, W)
        ex = p1.take(NB * W)
        rec_gate = cut(ex, NB, W)
        AT = cut(p1.take(NB * W), NB, W)
        o_rec = cut(p1.take(NB * W), NB, W)
        S = p1.take(W)
        St = p1.take(W)
        masks = cut(p1.take((LEVELS + 1) * P), LEVELS + 1, P)
        cos_sin = p1.take(2 * T)
        cosT, sinT = cos_sin[:, 0:T], cos_sin[:, T:2 * T]
        rotm = p1.take(P)
        es_words = p1.take(4 * T)
        es = cut(es_words, 2, 2, T)
        xm = es_words[:, 0:D]
        wts = cut(x1[:, 0:2 * T], 2, T)
        wT = cut(p1.take(2 * 640), 2, 640)
        mixT = cut(area[:, word(rec_q):word(rec_q) + KT * SEQ], KT, SEQ)

        p2 = Arena(area, 0, AREA)
        xn = cut(p2.take(NB * D), NB, D)
        xnt_words = p2.take(KT * SEQ)
        xnT = cut(xnt_words, KT, SEQ)
        qp = cut(p2.take(4 * SEQ), 4, SEQ)
        skT = cut(p2.take(2 * HP * NK), 2 * HP, NK)
        sc_flat = p2.take(HEADS * 2 * NK)
        sc = cut(sc_flat, NB, 2 * HP * NK)
        u_rows = cut(p2.take(RING * D), RING, D)
        v_rows = cut(p2.take(RING * D), RING, D)
        ffnw = p2.take(D)
        dg = cut(xnt_words[:, 0:2 * RING * P], 2, RING, P)
        finw1 = xnt_words[:, 2 * RING * P:2 * RING * P + D]
        dots = p2.take(NB * SLOTS)
        expert_ids = p2.take(NB * SLOTS).bitcast(I32)
        gate = p2.take(NB * SLOTS)
        u_ids = cut(p2.take(2 * RING).bitcast(I32), 2, RING)
        v_ids = cut(p2.take(2 * RING).bitcast(I32), 2, RING)
        d8 = p2.take(RING)
        gsum = p2.take(2)
        zero = p2.take(P)
        iota = small.take(TOP)
        tk = Arena(area, word(ffnw), word(ffnw) + D)
        tk_words = tk.take(2 * NK + TOP * TOP)
        rows2 = cut(tk_words[:, 0:2 * NK], 2, NK)
        cand = tk_words[:, 2 * NK:]
        sv = cut(tk.take(2 * TOP), 2, TOP)
        si = cut(tk.take(2 * TOP).bitcast(U32), 2, TOP)
        sif = cut(tk.take(2 * TOP), 2, TOP)
        s2 = cut(cand, 2, NK)
        top_s = tk.take(TOP)
        pos = tk.take(TOP).bitcast(U32)
        pi = cut(tk.take(2 * TOP).bitcast(U32), 2, TOP)
        e01 = cut(tk.take(2 * TOP), 2, TOP)
        c2 = rows2.rearrange("p a k -> p (a k)")
        oh = cut(tk_words, 2, TOP, TOP)

        p3 = Arena(area, 0, AREA)
        hT = cut(p3.take(KT * SEQ), KT, SEQ)
        q2_words = p3.take(2 * 4 * SEQ)
        q2T = cut(q2_words[:, 0:2048], 4, SEQ)
        k2T = cut(q2_words[:, 2048:4096], 4, SEQ)
        mT = cut(q2_words, KT, SEQ)
        v2 = cut(p3.take(NB * W), NB, W)
        ub = cut(p3.take(NB * W), NB, W)
        z_words = p3.take(2 * NB * W)
        za = cut(z_words[:, 0:2048], NB, W)
        zb = cut(z_words[:, 2048:4096], NB, W)
        vb = cut(p3.take(NB * W), NB, W)
        ga = cut(p3.take(NB * D), NB, D)
        gb = cut(p3.take(NB * D), NB, D)
        yT = cut(p3.take(KT * SEQ), KT, SEQ)
        an2 = cut(z_words, NB, D)
        vc = area[:, p3.at - KT * SEQ:p3.at - KT * SEQ + 2048]
        o2 = cut(area[:, p3.at - 2048:p3.at], NB, W)
        vq = gb.rearrange("p b n -> p (b n)")[:, 0:2048]
        lng = p3.take(W)
        lnb = p3.take(W)
        wsT = cut(p3.take(NG * P), NG, P)
        finw = p3.take(D)
        zs = cut(p3.take(2 * W), 2, W)
        ae = cut(p3.take(2 * W), 2, W)
        softplus = cut(p3.take(2 * W), 2, W)
        w2T = cut(p3.take(2 * W), 2, W)
        rcs = p3.take(W)
        up_t = p3.take(W)
        gst = cut(p3.take(4 * 32), 4, 32)
        ones = p3.take(W)

        ld_x = sem("ld_x")
        ld_c = sem("ld_c")
        ld_p = sem("ld_p")
        ld_q = sem("ld_q")
        w_full = [sem(f"w_full{i}") for i in range(2)]
        h1_done = sem("h1_done")
        a_full, a_free = sem("a_full"), sem("a_free")
        b_full, b_free = sem("b_full"), sem("b_free")
        c_full, c_free = sem("c_full"), sem("c_free")
        act_s, dve_s, pool_s = sem("act_s"), sem("dve_s"), sem("pool_s")
        sq_done, ms_done, rt_done, rs_done = sem("sq_done"), sem("ms_done"), sem("rt_done"), sem("rs_done")
        rows_done = sem("rows_done")
        lam_sums, lam_exps = sem("lam_sums"), sem("lam_exps")
        f_raw, g_done = sem("f_raw"), sem("g_done")
        mx_done, e_done, wt_ready = sem("mx_done"), sem("e_done"), sem("wt_ready")
        d_done, ex_done, x_ready = sem("d_done"), sem("ex_done"), sem("x_ready")
        kd_ready, s_ready = sem("kd_ready"), sem("s_ready")
        mixrows = sem("mixrows")
        rg_done = sem("rg_done")
        xn_done = sem("xn_done")
        idx_ready = sem("idx_ready")
        gmax, gexp = sem("gmax"), sem("gexp")
        u_free, v_free = sem("u_free"), sem("v_free")
        u_full = [sem(f"u_full{i}") for i in range(RING)]
        v_full = [sem(f"v_full{i}") for i in range(RING)]
        dots_ready, hid_ready, hid_done = sem("dots_ready"), sem("hid_ready"), sem("hid_done")
        dg_ready = sem("dg_ready")
        y_full, y_free = sem("y_full"), sem("y_free")
        zs_ready, l_ready, wl_ready, w_ready = sem("zs_ready"), sem("l_ready"), sem("wl_ready"), sem("w_ready")
        ln_r, ln_rt, ln_v = sem("ln_r"), sem("ln_rt"), sem("ln_v")
        fn_done = sem("fn_done")
        y_ready = sem("y_ready")
        fin_ready, stored = sem("fin_ready"), sem("stored")

        block = ctx.enter_context(nc.Block())

        LOADED_C = 16 * 15
        LOADED_P = 16 * 2
        LOADED_Q = 16 * 4

        @block.sync
        def _(sp):
            sp.dma_start(h[:, :, :], t["x"].rearrange("(b p) d -> p b d", p=P)).then_inc(ld_x, 16)
            sp.dma_start(xm[0:NM, :], t["meta"]).then_inc(ld_x, 16)
            for dst, name in ((ident, "ident"), (normw, "normw"), (cosT, "cosT"), (sinT, "sinT"), (rotm, "rotm"),
                              (lblog, "lblog"), (lam_in, "lam_in"), (tri, "tri"), (stri, "stri"),
                              (masks.bitcast(I32), "masks"), (sublnw, "sublnw"), (recw, "recw"),
                              (normg2, "normg2"), (iota, "iota"), (bs, "bs")):
                sp.dma_start(dst, t[name]).then_inc(ld_c, 16)
            for n, c in enumerate(CHUNKS):
                slot = wbuf[:, n % 2, :, :]
                if n >= 2:
                    last = CHUNKS[n - 2]
                    if last in C_END:
                        sp.wait_ge(c_full, C_END[last])
                    elif last in A_END:
                        sp.wait_ge(a_full, A_END[last])
                    else:
                        sp.wait_ge(b_full, B_END[last])
                if c in WIN_AT:
                    src = [(0, t["w_in"][:, W * WIN_AT[c]:W * (WIN_AT[c] + 1)], slot)]
                elif c in WIN2_AT:
                    src = [(0, t["w_in_2"][:, W * WIN2_AT[c]:W * (WIN2_AT[c] + 1)], slot)]
                elif c[0] in "pr":
                    src = [(0, t["wq"][:, W * int(c[1]):W * (int(c[1]) + 1)], slot)]
                elif c[0] == "o":
                    src = [(0, t["w_out"][:, W * int(c[1]):W * (int(c[1]) + 1)], slot)]
                elif c[0] == "w":
                    src = [(0, t["w_out_2"][:, W * int(c[1]):W * (int(c[1]) + 1)], slot)]
                else:
                    j = int(c[2])
                    sp.dma_start(slot[:, 0:4, :], t["w_up_a"][:, W * j:W * (j + 1)]
                                 .rearrange("(k p) n -> p k n", p=P)).then_inc(w_full[n % 2], 16)
                    sp.dma_start(slot[:, 4:8, :], t["w_up_b"][:, W * j:W * (j + 1)]
                                 .rearrange("(k p) n -> p k n", p=P)).then_inc(w_full[n % 2], 16)
                    continue
                sp.dma_start(src[0][2], src[0][1].rearrange("(k p) n -> p k n", p=P)).then_inc(w_full[n % 2], 16)
                if c == "o1":
                    sp.wait_ge(b_free, B_END["mixt"])
                    sp.dma_start(skT, t["skT"]).then_inc(ld_p, 16)
                    sp.dma_start(ffnw, t["ffnw"].broadcast_to([P, D])).then_inc(ld_p, 16)
                if c == "k2":
                    sp.wait_ge(a_free, A_END["sr3"])
                    sp.dma_start(finw1, t["finw1"].broadcast_to([P, D])).then_inc(ld_p, 16)
                    sp.wait_ge(h1_done, NB)
                    sp.dma_start(lng, t["lng"].broadcast_to([P, W])).then_inc(ld_q, 16)
                    sp.dma_start(lnb, t["lnb"].broadcast_to([P, W])).then_inc(ld_q, 16)
                    sp.dma_start(wsT, t["wsT"]).then_inc(ld_q, 16)
                    sp.dma_start(finw, t["finw"].broadcast_to([P, D])).then_inc(ld_q, 16)
            for b in range(NB):
                sp.wait_ge(fin_ready, b + 1)
                sp.dma_start(out[P * b:P * (b + 1), :], h[:, b, :]).then_inc(stored, 16)
            sp.wait_ge(stored, 16 * NB)

        @block.tensor
        def _(pe):
            na, nb, n_c, nw, wl = [0], [0], [0], [0], [0, 0]

            def a_bank():
                n = na[0]
                if n >= RA:
                    pe.wait_ge(a_free, n - RA + 1)
                na[0] += 1
                return psum_a[n % RA]

            def b_bank():
                n = nb[0]
                if n >= RB:
                    pe.wait_ge(b_free, n - RB + 1)
                nb[0] += 1
                return psum_b[n % RB]

            def c_bank():
                n = n_c[0]
                if n >= RC:
                    pe.wait_ge(c_free, n - RC + 1)
                n_c[0] += 1
                return psum_c[n % RC]

            def chunk(n_dma=1):
                n = nw[0]
                wl[n % 2] += 16 * n_dma
                pe.wait_ge(w_full[n % 2], wl[n % 2])
                nw[0] += 1
                return wbuf[:, n % 2, :, :]

            def at(name_a=None, name_b=None):
                if name_a:
                    assert na[0] == A_END[name_a], (name_a, na[0], A_END[name_a])
                if name_b:
                    assert nb[0] == B_END[name_b], (name_b, nb[0], B_END[name_b])

            def mm(o, l, r, start, stop):
                return nc.tensor.matmul(o, l, r, start=start, stop=stop, skip_group_check=True)

            def cols_real(w, src, lo, bank):
                for i in range(4):
                    ps = bank()
                    for k in range(KT):
                        last = mm(ps[:, 0:SEQ], w[:, k, P * i:P * (i + 1)], src[:, k, lo:lo + SEQ], k == 0, k == KT - 1)
                    last.then_inc(a_full, 1)
                return last

            def cols_meta(w):
                ps = a_bank()
                for i in range(4):
                    for k in range(KT):
                        last = mm(ps[:, NM * i:NM * (i + 1)], w[:, k, P * i:P * (i + 1)], aT[:, k, 0:NM],
                                  k == 0, k == KT - 1)
                last.then_inc(a_full, 1)
                return last

            def rows_real(w, src, lo):
                for b in range(NB):
                    ps = a_bank()
                    for k in range(KT):
                        last = mm(ps[:, :], src[:, k, lo + P * b:lo + P * (b + 1)], w[:, k, :], k == 0, k == KT - 1)
                    last.then_inc(a_full, 1)

            def rows_meta(w):
                ps = a_bank()
                for k in range(KT):
                    last = mm(ps[0:NM, :], aT[:, k, 0:NM], w[:, k, :], k == 0, k == KT - 1)
                last.then_inc(a_full, 1)

            pe.wait_ge(ld_c, LOADED_C)
            for b in [4] + list(range(NB)):
                n = NM if b == 4 else P
                pe.wait_ge(rows_done, 1 if b == 4 else b + 2)
                for g in range(2):
                    ps = b_bank()
                    for k in range(4):
                        last = nc.tensor.transpose(ps[:, P * k:P * k + n], an[0:n, b, P * (4 * g + k):P * (4 * g + k + 1)],
                                                   ident[0:n, 0:n])
                    last.then_inc(b_full, 1)
            at(name_b="trA")
            pe.wait_ge(b_free, B_END["trA"])
            w = chunk()
            cols_real(w, aT, NM, a_bank)
            cols_meta(w)
            cols_real(chunk(), aT, NM, a_bank)

            def rows_part(ps, w, i, ks):
                n, lo = (NM, 0) if i == NB else (P, NM + P * i)
                for k in ks:
                    last = mm(ps[0:n, :], aT[:, k, lo:lo + n], w[:, k, :], k == 0, k == KT - 1)
                return last

            def rotate(src, meta):
                for i in range(HA):
                    mm(b_bank()[:, 0:SEQ], rotm, src[:, i, NM:T], True, True).then_inc(b_full, 1)
                if meta:
                    ps = b_bank()
                    for i in range(HA):
                        last = mm(ps[:, NM * i:NM * (i + 1)], rotm, src[:, i, 0:NM], True, True)
                    last.then_inc(b_full, 1)

            for step in STEPS1:
                if step in ("rotk", "rotq"):
                    pe.wait_ge(a_free, A_END["ak" if step == "rotk" else "aq"])
                    rotate(raw, step == "rotk")
                elif isinstance(step, str):
                    l = int(step[2])
                    if l < LEVELS:
                        pe.wait_ge(x_ready, l + 1)
                    for b in range(NB):
                        ps = b_bank()
                        for hh in range(HR):
                            c = slice(SEQ * hh + P * b, SEQ * hh + P * (b + 1))
                            left = (x0, x1)[l % 2][:, c] if l < LEVELS else rec_k[:, c]
                            right = (x0, x1)[l % 2][:, c] if l < LEVELS else rec_q[:, c]
                            last = mm(ps[:, P * hh:P * (hh + 1)], left, right, True, True)
                        last.then_inc(b_full, 1)
                    at(name_b=step)
                else:
                    name, i = step
                    if i == 0:
                        w = chunk()
                    if name == "av":
                        rows_part(a_bank(), w, i, range(KT)).then_inc(a_full, 1)
                    elif i == NB:
                        cols_meta(w)
                    else:
                        ps = a_bank()
                        for k in range(KT):
                            last = mm(ps[:, 0:SEQ], w[:, k, P * i:P * (i + 1)], aT[:, k, NM:T], k == 0, k == KT - 1)
                        last.then_inc(a_full, 1)
            at("aq", "rotq")

            pe.wait_ge(b_free, B_END["rotq"])

            def scores(b, hh):
                lo = NM if b == NB - 1 else 0
                for part in range(2):
                    rows = slice(DH * part, DH * (part + 1))
                    mm(b_bank()[:, 0:NM + P * (b + 1) - lo], qT[rows, hh, P * b:P * (b + 1)],
                       kT[rows, hh, lo:NM + P * (b + 1)], True, True).then_inc(b_full, 1)
                for part in range(2 if lo else 0):
                    rows = slice(DH * part, DH * (part + 1))
                    mm(b_bank()[:, 0:NM], qT[rows, hh, P * b:P * (b + 1)], kT[rows, hh, 0:NM],
                       True, True).then_inc(b_full, 1)

            def state_step(b):
                if b is None:
                    pe.wait_ge(a_free, A_END["kdt"])
                    pe.wait_ge(c_free, C_END["ri"])
                else:
                    pe.wait_ge(s_ready, b + 1)
                    ps = a_bank()
                    for kh in range(HR):
                        c = slice(P * kh, P * (kh + 1))
                        mm(ps[:, c], AT[:, b, c], rec_v[:, b, c], True, False)
                        last = mm(ps[:, c], rec_q[:, SEQ * kh + P * b:SEQ * kh + P * (b + 1)], S[:, c], False, True)
                    last.then_inc(a_full, 1)
                if b != NB - 1:
                    ps = b_bank()
                    n, kb = (NM, 4) if b is None else (P, b)
                    for kh in range(HR):
                        c = slice(P * kh, P * (kh + 1))
                        last = mm(ps[:, c], kdT[0:n, kb, c], rec_v[0:n, kb, c], True, True)
                    last.then_inc(b_full, 1)

            scores(*UNITS[0])
            for n, (b, hh) in enumerate(UNITS):
                if n + 1 < len(UNITS):
                    scores(*UNITS[n + 1])
                if n in SIDE_AT:
                    i = SIDE_AT[n][1]
                    if i == 0:
                        w = chunk()
                    side = c_bank()
                    rows_part(side, w, i, range(KT // 2))
                pe.wait_ge(wt_ready, n + 1)
                ww = wts[:, n % 2, :]
                tiles = [ww[:, 0:P]] + [ww[:, NM + P * j:NM + P * (j + 1)] for j in range(b + 1)]
                for lo in range(0, len(tiles), 4):
                    ps = a_bank()
                    for j, x in enumerate(tiles[lo:lo + 4]):
                        last = nc.tensor.transpose(ps[:, P * j:P * (j + 1)], x, ident)
                    last.then_inc(a_full, 1)
                if n in SIDE_AT:
                    rows_part(side, w, i, range(KT // 2, KT)).then_inc(c_full, 1)
                if n in STATE_AT:
                    state_step(STATE_AT[n])
                pe.wait_ge(a_free, A_END[f"wt{b}{hh}"])
                ps = a_bank()
                vcols = slice(P * hh, P * (hh + 1))
                mm(ps[:, 0:P], wT[0:NM, n % 2, 0:P], v[0:NM, 4, vcols], True, False)
                for j in range(b + 1):
                    last = mm(ps[:, 0:P], wT[:, n % 2, P * (j + 1):P * (j + 2)], v[:, j, vcols], False, j == b)
                last.then_inc(a_full, 1)
                at(f"o{b}{hh}")
                if n == KDT_AT:
                    pe.wait_ge(kd_ready, 1)
                    for kb in [4] + list(range(NB)):
                        ps = a_bank()
                        for kh in range(HR):
                            at_k = SEQ * kh + P * kb
                            src = rec_k_meta[:, NM * kh:NM * kh + P] if kb == 4 else rec_k[:, at_k:at_k + P]
                            last = nc.tensor.transpose(ps[:, P * kh:P * (kh + 1)], src, ident)
                        last.then_inc(a_full, 1)

            pe.wait_ge(mixrows, 2)
            for src in (o_att, o_rec):
                for b in range(NB):
                    ps = b_bank()
                    for k in range(4):
                        last = nc.tensor.transpose(ps[:, P * k:P * (k + 1)], src[:, b, P * k:P * (k + 1)], ident)
                    last.then_inc(b_full, 1)
            at("o33", "mixt")
            pe.wait_ge(b_free, B_END["mixt"])
            halves = [chunk(), chunk()]
            for b in range(NB):
                for w in halves:
                    ps = b_bank()
                    for k in range(KT):
                        last = mm(ps[:, :], mixT[:, k, P * b:P * (b + 1)], w[:, k, :], k == 0, k == KT - 1)
                    last.then_inc(b_full, 1)
            at(name_b="o1")

            for b in range(NB):
                pe.wait_ge(xn_done, b + 1)
                for g in range(2):
                    ps = a_bank()
                    for k in range(4):
                        last = nc.tensor.transpose(ps[:, P * k:P * (k + 1)],
                                                   xn[:, b, P * (4 * g + k):P * (4 * g + k + 1)], ident)
                    last.then_inc(a_full, 1)
            pe.wait_ge(a_free, A_END["xnt"])
            pe.wait_ge(ld_p, LOADED_P)

            def key_scores(i, b, at):
                ps = a_bank()
                for j in range(4):
                    last = mm(ps[:, P * j:P * (j + 1)], qp[:, j, P * at:P * (at + 1)], skT[:, 4 * i + j, :], True, True)
                last.then_inc(a_full, 1)

            for i in range(4):
                w = chunk()
                ps = a_bank()
                for j in range(4):
                    for k in range(KT):
                        last = mm(ps[:, P * j:P * (j + 1)], w[:, k, P * j:P * (j + 1)], xnT[:, k, 0:P], k == 0, k == KT - 1)
                last.then_inc(a_full, 1)
                if i:
                    pe.wait_ge(a_free, A_END[f"p{i - 1}"])
                    key_scores(i - 1, 0, i - 1)
            pe.wait_ge(a_free, A_END["p3"])
            key_scores(3, 0, 3)
            at("sc3")
            for i in range(4):
                w = chunk()
                for j in range(4):
                    ps = a_bank()
                    for k in range(KT):
                        last = mm(ps[:, P:SEQ], w[:, k, P * j:P * (j + 1)], xnT[:, k, P:SEQ], k == 0, k == KT - 1)
                    last.then_inc(a_full, 1)
                pe.wait_ge(a_free, A_END[f"r{i}"])
                for b in range(1, NB):
                    key_scores(i, b, b)
                at(f"sr{i}")
            for b in range(NB):
                y = psum_a if b % 2 else psum_c
                if b == 0:
                    pe.wait_ge(c_free, C_END["rg"])
                if b == 1:
                    pe.wait_ge(a_free, A_END["sr3"])
                if b >= 2:
                    pe.wait_ge(y_free, b - 1)
                for c in range(2):
                    mm(y[c][:, :], ident, h[:, b, W * c:W * (c + 1)], True, False)
                with pe.Fori(0, ROUNDS // 2) as it:
                    for turn in range(2):
                        pe.wait_ge(dg_ready, it * 2 + (b * ROUNDS + turn + 1))
                        for s in range(RING):
                            pe.wait_ge(v_full[s], it * 32 + (b * ROUNDS * 16 + 16 * turn + 16))
                            for c in range(2):
                                last = nc.tensor.matmul(y[c][:, :], dg[:, turn, s, :], v_rows[:, s, W * c:W * (c + 1)],
                                                        start=False, stop=False, skip_group_check=True)
                            last.then_inc(v_free, 1)
                for c in range(2):
                    last = mm(y[c][:, :], zero, h[:, b, W * c:W * (c + 1)], False, True)
                last.then_inc(y_full, 1)

            for b in range(NB):
                pe.wait_ge(rows_done, 5 + b + 1)
                for g in range(2):
                    ps = b_bank()
                    for k in range(4):
                        last = nc.tensor.transpose(ps[:, P * k:P * (k + 1)],
                                                   an2[:, b, P * (4 * g + k):P * (4 * g + k + 1)], ident)
                    last.then_inc(b_full, 1)
            pe.wait_ge(b_free, B_END["trH"])
            pe.wait_ge(y_free, NB)
            cols_real(chunk(), hT, 0, a_bank)
            cols_real(chunk(), hT, 0, a_bank)
            rows_real(chunk(), hT, 0)
            at("v2")

            def scores2(b, hh):
                rows = slice(DH2 * (hh % 2), DH2 * (hh % 2 + 1))
                mm(b_bank()[:, 0:P * (b + 1)], q2T[rows, hh // 2, P * b:P * (b + 1)], k2T[rows, hh // 2, 0:P * (b + 1)],
                   True, True).then_inc(b_full, 1)

            pe.wait_ge(a_free, A_END["k2"])
            scores2(*UNITS2[0])
            for n, (b, hh) in enumerate(UNITS2):
                if n + 1 < len(UNITS2):
                    scores2(*UNITS2[n + 1])
                if n in SGU_AT:
                    g_b = SGU_AT[n]
                    pe.wait_ge(ln_v, 1)
                    ps = b_bank()
                    for g in range(NG):
                        last = mm(ps[:, GC * g:GC * (g + 1)], wsT[:, g, :], vb[:, g_b, GC * g:GC * (g + 1)], True, True)
                    last.then_inc(b_full, 1)
                if n % NB == 0:
                    w = chunk()
                rows = slice(P * (n % NB), P * (n % NB + 1))
                side = c_bank()
                for k in range(KT // 2):
                    mm(side[:, :], hT[:, k, rows], w[:, k, :], k == 0, False)
                pe.wait_ge(w_ready, n + 1)
                ps = a_bank()
                for j in range(b + 1):
                    last = nc.tensor.transpose(ps[:, P * j:P * (j + 1)], ae[:, n % 2, P * j:P * (j + 1)], ident)
                last.then_inc(a_full, 1)
                for k in range(KT // 2, KT):
                    last = mm(side[:, :], hT[:, k, rows], w[:, k, :], False, k == KT - 1)
                last.then_inc(c_full, 1)
                pe.wait_ge(a_free, A_END[f"w2_{n}"])
                ps = a_bank()
                for j in range(b + 1):
                    last = mm(ps[:, 0:DH2], w2T[:, n % 2, P * j:P * (j + 1)], v2[:, j, DH2 * hh:DH2 * (hh + 1)],
                              j == 0, j == b)
                last.then_inc(a_full, 1)
                at(f"o2_{n}")
            at(name_b=f"z{len(UNITS2) - 1}")
            for src in (o2, vb):
                for b in range(NB):
                    if src is o2:
                        pe.wait_ge(y_ready, 2 if b == NB - 1 else 1)
                    ps = a_bank()
                    for k in range(4):
                        last = nc.tensor.transpose(ps[:, P * k:P * (k + 1)], src[:, b, P * k:P * (k + 1)], ident)
                    last.then_inc(a_full, 1)
            at("yt")
            pe.wait_ge(a_free, A_END["yt"])
            for j in range(2):
                w = chunk(2)
                for b in range(NB):
                    for half in range(2):
                        ps = b_bank()
                        for k in range(4):
                            last = mm(ps[:, :], yT[:, 4 * half + k, P * b:P * (b + 1)], w[:, 4 * half + k, :],
                                      k == 0, k == 3)
                        last.then_inc(b_full, 1)
            at(name_b="up1")
            pe.wait_ge(b_free, B_END["up1"])
            for b in range(NB):
                for g in range(2):
                    ps = a_bank()
                    for k in range(4):
                        last = nc.tensor.transpose(ps[:, P * k:P * (k + 1)],
                                                   ga[:, b, P * (4 * g + k):P * (4 * g + k + 1)], ident)
                    last.then_inc(a_full, 1)
            at("mt")
            pe.wait_ge(a_free, A_END["mt"])
            for j in range(2):
                w = chunk()
                for b in range(NB):
                    ps = b_bank()
                    for k in range(KT):
                        last = mm(ps[:, :], mT[:, k, P * b:P * (b + 1)], w[:, k, :], k == 0, k == KT - 1)
                    last.then_inc(b_full, 1)
            at(name_b="w1")

        @block.scalar
        def _(act):
            na, n_c, own = [0], [0], [0]
            fn = nc.scalar.activation

            def bank():
                act.wait_ge(a_full, na[0] + 1)
                na[0] += 1
                return psum_a[(na[0] - 1) % RA]

            def c_empty(dst, rows=slice(0, P)):
                act.wait_ge(c_full, n_c[0] + 1)
                n_c[0] += 1
                fn(dst, psum_c[(n_c[0] - 1) % RC][rows, :], ACT.Copy).then_inc(c_free, 1)

            def step(ins):
                own[0] += 1
                ins.then_inc(act_s, 1)
                act.wait_ge(act_s, own[0])

            def empty(dst, func=ACT.Copy, cols=slice(0, 512), rows=slice(0, P), scale=1.0, view=None):
                ps = bank()[rows, cols]
                if view:
                    ps = view(ps)
                fn(dst, ps, func, scale=scale).then_inc(a_free, 1)

            act.wait_ge(ld_x, 32)
            act.wait_ge(dve_s, 1)
            for b in range(NB):
                fn(an[:, b, :], h[:, b, :], ACT.Square, accum_out=ss[:, b:b + 1])
            fn(an[0:NM, 4, :], xm[0:NM, :], ACT.Square, accum_out=ss[0:NM, 4:5]).then_inc(sq_done, 1)
            act.wait_ge(ms_done, 1)
            fn(rt[:, 0:5], ss[:, 0:5], ACT.Sqrt).then_inc(rt_done, 1)
            act.wait_ge(rs_done, 1)
            act.wait_ge(sq_done, 1)
            fn(an[0:NM, 4, :], xm[0:NM, :], ACT.Copy, scale=rs[0:NM, 4:5]).then_inc(rows_done, 1)
            for b in range(NB):
                fn(an[:, b, :], h[:, b, :], ACT.Copy, scale=rs[:, b:b + 1]).then_inc(rows_done, 1)
            act.wait_ge(lam_sums, 1)
            fn(lbt[:, 0:2, :], lbt[:, 0:2, :], ACT.Exp).then_inc(lam_exps, 1)
            fn(lamt[:, 0:2], lamt[:, 0:2], ACT.Exp).then_inc(lam_exps, 1)
            for i in range(HR):
                empty(rec_k[:, SEQ * i:SEQ * (i + 1)], ACT.Sigmoid)
            empty(rec_k_meta[:, 0:HR * NM], ACT.Sigmoid, cols=slice(0, HR * NM))
            for i in range(HR):
                empty(rec_q[:, SEQ * i:SEQ * (i + 1)], ACT.Silu)
            act.wait_ge(f_raw, 1)
            fn(x1, rec_k, ACT.Ln)
            fn(g_meta, rec_k_meta[:, 0:HR * NM], ACT.Ln).then_inc(g_done, 1)

            def level_exps(l):
                half = (P // 2) >> l
                act.wait_ge(d_done, l + 1)
                e3 = ex.rearrange("p (n s) -> p n s", s=2 * half)
                fn(e3[:, :, half:], e3[:, :, half:], ACT.Exp)
                fn(e3[:, :, 0:half], e3[:, :, 0:half], ACT.Exp, scale=-1.0).then_inc(ex_done, 1)

            level_exps(0)
            for step1 in STEPS1:
                if step1 in ("rotk", "rotq", f"lv{LEVELS}", f"lv{LEVELS - 1}"):
                    continue
                if isinstance(step1, str):
                    level_exps(int(step1[2]) + 1)
                    continue
                name, i = step1
                if name == "av":
                    empty(v[:, i, :] if i < NB else v[0:NM, 4, :], rows=slice(0, P if i < NB else NM))
                elif i == NB:
                    empty(raw[:, :, 0:NM], cols=slice(0, HA * NM), view=lambda x: cut(x, HA, NM))
                else:
                    if name == "aq" and i == 0:
                        act.wait_ge(b_free, B_END["rotk"])
                    empty(raw[:, i, NM:T])

            def exps(n):
                nk = NM + P * (UNITS[n][0] + 1)
                act.wait_ge(mx_done, n + 1)
                for part in range(2):
                    last = fn(es[:, n % 2, part, 0:nk], es[:, n % 2, part, 0:nk], ACT.Exp, scale=DH ** -0.5,
                              bias=nm[:, n % 2, part:part + 1], accum_out=rsum[:, n % 2, part:part + 1])
                last.then_inc(e_done, 1)

            exps(0)
            for n, (b, hh) in enumerate(UNITS):
                if n + 1 < len(UNITS):
                    exps(n + 1)
                if n == 0:
                    act.wait_ge(b_free, B_END["rotq"])
                if n == 0:
                    act.wait_ge(d_done, LEVELS + 1)
                    fn(ex, ex, ACT.Exp)
                    fn(x0, cum, ACT.Exp)
                    fn(g_meta, g_meta, ACT.Exp)
                    fn(el[:, 0:16], cum[:, P - 1::P], ACT.Exp).then_inc(ex_done, 1)
                if b < 3:
                    empty(wT[:, n % 2, 0:P * (b + 2)], cols=slice(0, P * (b + 2)))
                else:
                    empty(wT[:, n % 2, 0:512])
                    empty(wT[:, n % 2, 512:640], cols=slice(0, P))
                if STATE_AT.get(n) is not None:
                    empty(o_rec[:, STATE_AT[n], :])
                if n in SIDE_AT:
                    name, i = SIDE_AT[n]
                    if i == NB:
                        c_empty(rec_v[0:NM, 4, :], rows=slice(0, NM))
                    else:
                        c_empty((rec_v if name == "ri" else rec_gate)[:, i, :])
                empty(o_att[:, b, P * hh:P * (hh + 1)], cols=slice(0, P))
                if n == KDT_AT:
                    for kb in [4] + list(range(NB)):
                        empty(kdT[:, kb, :])
            act.wait_ge(c_free, C_END["rg"])
            fn(rec_gate, rec_gate, ACT.Silu).then_inc(rg_done, 1)
            for k in range(2):
                act.wait_ge(ms_done, 2 + k)
                fn(rt[:, 0:16], ss[:, 0:16], ACT.Sqrt).then_inc(rt_done, 1)
            for b in range(NB):
                act.wait_ge(b_free, B_END["mixt"] + 2 * (b + 1))
                fn(xn[:, b, :], h[:, b, :], ACT.Square, accum_out=ss[:, b:b + 1]).then_inc(sq_done, 1)
                act.wait_ge(ms_done, 4 + b)
                fn(rt[:, b:b + 1], ss[:, b:b + 1], ACT.Sqrt).then_inc(rt_done, 1)
            for b in range(NB):
                for g in range(2):
                    empty(xnT[:, 4 * g:4 * g + 4, P * b:P * (b + 1)], view=lambda x: cut(x, 4, P))
            for i in range(4):
                empty(qp[:, :, P * i:P * (i + 1)], view=lambda x: cut(x, 4, P))
                if i:
                    empty(sc[:, 0, W * (i - 1):W * i])
            empty(sc[:, 0, 3 * W:4 * W])
            for i in range(4):
                for j in range(4):
                    empty(qp[:, j, P:SEQ], cols=slice(P, SEQ))
                for b in range(1, NB):
                    empty(sc[:, b, W * i:W * (i + 1)])
            def head_functions(first, count, ahead=True):
                with act.Fori(0, count) as it:
                    if ahead:
                        gate_exps(it, first + LEAD)
                    act.wait_ge(dots_ready, it * 2 + (2 * first + 2))
                    part = dots[:, bass.ds(it * TOP + first * TOP, TOP)]
                    fn(part, part, ACT.Gelu).then_inc(hid_ready, 1)

            def gate_exps(it, g):
                act.wait_ge(gmax, it + (g + 1))
                part = gate[:, bass.ds(it * TOP + g * TOP, TOP)]
                fn(part, part, ACT.Exp).then_inc(gexp, 1)

            def norms(b):
                scratch = u_rows[:, 0, :] if b == NB - 1 else xn[:, b, :]
                act.wait_ge(y_free, b + 1)
                fn(scratch, h[:, b, :], ACT.Square, accum_out=ss[:, b:b + 1]).then_inc(sq_done, 1)
                act.wait_ge(ms_done, 8 + 2 * b)
                fn(rt[:, b:b + 1], ss[:, b:b + 1], ACT.Sqrt).then_inc(rt_done, 1)
                act.wait_ge(h1_done, b + 1)
                fn(scratch, h[:, b, :], ACT.Square, accum_out=ss[:, 4 + b:5 + b]).then_inc(sq_done, 1)
                act.wait_ge(ms_done, 9 + 2 * b)
                fn(rt[:, 4 + b:5 + b], ss[:, 4 + b:5 + b], ACT.Sqrt).then_inc(rt_done, 1)
                act.wait_ge(rs_done, 9 + 2 * b)

            with act.Fori(0, LEAD) as it:
                gate_exps(it, 0)
            for b in range(NB):
                head_functions(b * HP, HP if b < NB - 1 else HP - LEAD)
                if b == NB - 1:
                    head_functions(HEADS - LEAD, LEAD, ahead=False)
                if b:
                    norms(b - 1)
                if b == NB - 1:
                    for done in range(b):
                        fn(an2[:, done, :], h[:, done, :], ACT.Copy, scale=rs[:, 4 + done:5 + done]).then_inc(rows_done, 1)
            norms(NB - 1)
            fn(an2[:, NB - 1, :], h[:, NB - 1, :], ACT.Copy, scale=rs[:, 3 + NB:4 + NB]).then_inc(rows_done, 1)
            act.wait_ge(b_free, B_END["trH"])
            for i in range(4):
                empty(q2T[:, i, :], scale=DH2 ** -0.5)
            for i in range(4):
                empty(k2T[:, i, :])
            for b in range(NB):
                empty(v2[:, b, :])

            def log_part(n):
                e = ae[:, n % 2, 0:P * (UNITS2[n][0] + 1)]
                act.wait_ge(zs_ready, n + 1)
                step(fn(e, zs[:, n % 2, 0:P * (UNITS2[n][0] + 1)], ACT.Abs))
                step(fn(e, e, ACT.Exp, scale=-1.0))
                fn(e, e, ACT.Ln, bias=1.0).then_inc(l_ready, 1)

            side = {"vb": vb, "ub": ub, "za": za, "zb": zb, "ga0": ga[:, :, 0:W], "ga1": ga[:, :, W:D],
                    "gb0": gb[:, :, 0:W], "gb1": gb[:, :, W:D]}
            log_part(0)
            for n, (b, hh) in enumerate(UNITS2):
                nk = P * (b + 1)
                act.wait_ge(wl_ready, n + 1)
                fn(ae[:, n % 2, 0:nk], zs[:, n % 2, 0:nk], ACT.Exp).then_inc(w_ready, 1)
                if n + 1 < len(UNITS2):
                    log_part(n + 1)
                empty(w2T[:, n % 2, 0:nk], cols=slice(0, nk))
                c_empty(side[SIDE[n // NB]][:, n % NB, :])
                empty(o2[:, b, DH2 * hh:DH2 * (hh + 1)], cols=slice(0, DH2))
                if n == 2 * NB - 1:
                    act.wait_ge(c_free, C_END["ub"])
                    fn(vb, vb, ACT.Gelu_apprx_tanh)
                    fn(ub, ub, ACT.Gelu_apprx_tanh).then_inc(fn_done, 1)
                if n == 2 * NB + 2:
                    act.wait_ge(ln_r, 1)
                    fn(gst[:, 2, :], gst[:, 1, :], ACT.Sqrt).then_inc(ln_rt, 1)
                if n == 4 * NB - 1:
                    act.wait_ge(c_free, C_END["zb"])
                    fn(za, za, ACT.Silu)
                    fn(zb, zb, ACT.Silu).then_inc(fn_done, 1)
                    act.wait_ge(ln_v, 1)
            for g in range(2):
                for b in range(NB):
                    empty(yT[:, 4 * g:4 * g + 4, P * b:P * (b + 1)], view=lambda x: cut(x, 4, P))
            act.wait_ge(c_free, C_END["gb1"])
            fn(ga, ga, ACT.Sigmoid)
            fn(gb, gb, ACT.Sigmoid).then_inc(fn_done, 1)
            for b in range(NB):
                for g in range(2):
                    empty(mT[:, 4 * g:4 * g + 4, P * b:P * (b + 1)], view=lambda x: cut(x, 4, P))
            act.wait_ge(b_free, B_END["w1"])
            for b in range(NB):
                last = fn(gb[:, b, :], h[:, b, :], ACT.Square, accum_out=ss[:, b:b + 1])
            last.then_inc(sq_done, 1)
            act.wait_ge(ms_done, 16)
            fn(rt[:, 0:NB], ss[:, 0:NB], ACT.Sqrt).then_inc(rt_done, 1)

        @block.vector
        def _(dve):
            n_b, own = [0], [0]
            V = nc.vector

            def bank():
                dve.wait_ge(b_full, n_b[0] + 1)
                n_b[0] += 1
                return psum_b[(n_b[0] - 1) % RB]

            def emptied(ins):
                ins.then_inc(b_free, 1)
                dve.wait_ge(b_free, n_b[0])

            def step(ins, it=None):
                own[0] += 1
                ins.then_inc(dve_s, 1)
                if it is None:
                    dve.wait_ge(dve_s, own[0])
                else:
                    dve.wait_ge(dve_s, it * HEAD_STEPS + own[0])
                    V.nop(nofuse=True)

            def mean_root(k, n, count):
                V.tensor_scalar(ss[:, n], ss[:, n], 1.0 / count, EPS, ALU.mult, ALU.add).then_inc(ms_done, 1)
                dve.wait_ge(rt_done, k)
                V.reciprocal(rs[:, n], rt[:, n]).then_inc(rs_done, 1)
                dve.wait_ge(rs_done, k)

            def copy_level(l):
                for b in range(NB):
                    emptied(V.copy_predicated(cut(AT[:, b, :], HR, P),
                                              masks[:, l, :].bitcast(I32).unsqueeze(1).broadcast_to([P, HR, P]),
                                              cut(bank()[:, :], HR, P)))

            step(V.memset(ss, 1.0))
            dve.wait_ge(sq_done, 1)
            mean_root(1, slice(0, 5), D)
            dve.wait_ge(ld_c, LOADED_C)
            step(V.tensor_tensor(lbt[:, 2, :], lblog[:, 0, :], lblog[:, 1, :], ALU.max))
            step(V.tensor_tensor(lbt[:, 0, :], lblog[:, 0, :], lbt[:, 2, :], ALU.subtract))
            step(V.tensor_tensor(lbt[:, 1, :], lblog[:, 1, :], lbt[:, 2, :], ALU.subtract))
            step(V.tensor_tensor(lam_in[:, 0, :], lam_in[:, 0, :], lam_in[:, 1, :], ALU.mult))
            step(V.tensor_tensor(lam_in[:, 2, :], lam_in[:, 2, :], lam_in[:, 3, :], ALU.mult))
            step(V.reduce_sum(lamt[:, 0:1], lam_in[:, 0, :], AXX))
            V.reduce_sum(lamt[:, 1:2], lam_in[:, 2, :], AXX).then_inc(lam_sums, 1)
            V.memset(rec_k_meta, 0.0)
            V.memset(S, 0.0)
            step(V.memset(AT, 0.0))
            dve.wait_ge(lam_exps, 2)
            step(V.tensor_tensor(lbt[:, 2, :], lbt[:, 0, :], lbt[:, 1, :], ALU.add))
            step(V.reciprocal(lbt[:, 2, :], lbt[:, 2, :]))
            step(V.tensor_tensor(lb, lbt[:, 0, :], lbt[:, 2, :], ALU.mult))
            step(V.tensor_scalar(olb, lb, -1.0, 1.0, ALU.mult, ALU.add))
            step(V.tensor_tensor(lam, lamt[:, 0:1], lamt[:, 1:2], ALU.subtract))
            step(V.tensor_scalar(lam, lam, LAM0, None, ALU.add))
            for b in [4] + list(range(NB)):
                n = NM if b == 4 else P
                lo = 0 if b == 4 else NM + P * b
                for g in range(2):
                    ps = cut(bank()[:, :], 4, P)[:, :, 0:n]
                    emptied(V.tensor_tensor(aT[:, 4 * g:4 * g + 4, lo:lo + n], ps,
                                    normw[:, 4 * g:4 * g + 4].unsqueeze(2).broadcast_to([P, 4, n]), ALU.mult))

            def rope_k():
                dve.wait_ge(a_free, A_END["ak"])
                step(V.tensor_tensor(kT, raw, cosT.unsqueeze(1).broadcast_to([P, HA, T]), ALU.mult))
                for i in range(HA):
                    ps = bank()
                    step(V.tensor_tensor(St, ps[:, 0:SEQ], sinT[:, NM:T], ALU.mult))
                    emptied(V.tensor_tensor(kT[:, i, NM:T], kT[:, i, NM:T], St, ALU.add))
                ps = cut(bank()[:, 0:HA * NM], HA, NM)
                step(V.tensor_tensor(cut(St[:, 0:HA * NM], HA, NM), ps, sinT[:, 0:NM].unsqueeze(1).broadcast_to([P, HA, NM]),
                                     ALU.mult))
                emptied(V.tensor_tensor(kT[:, :, 0:NM], kT[:, :, 0:NM], cut(St[:, 0:HA * NM], HA, NM), ALU.add))

            dve.wait_ge(a_free, A_END["rf"])
            for i in range(HR):
                for x in (rec_k[:, SEQ * i:SEQ * (i + 1)], rec_k_meta[:, NM * i:NM * (i + 1)]):
                    last = V.tensor_scalar(x, x, olb[:, i:i + 1], lb[:, i:i + 1], ALU.mult, ALU.add)
            last.then_inc(f_raw, 1)
            dve.wait_ge(f_raw, 1)
            dve.wait_ge(g_done, 1)
            step(V.tensor_scalar(rec_k, rec_k, -1.0, 1.0, ALU.mult, ALU.add))
            step(V.tensor_scalar(rec_k_meta[:, 0:HR * NM], rec_k_meta[:, 0:HR * NM], -1.0, 1.0, ALU.mult, ALU.add))
            step(V.memset(St, 1.0))
            for i in range(HR * NB):
                V.tensor_tensor_scan(cum[:, P * i:P * (i + 1)], St[:, 0:P], x1[:, P * i:P * (i + 1)], 0.0,
                                     ALU.mult, ALU.add)
            for i in range(HR):
                last = V.tensor_tensor_scan(cum_meta[:, NM * i:NM * (i + 1)], St[:, 0:NM], g_meta[:, NM * i:NM * (i + 1)], 0.0,
                                            ALU.mult, ALU.add)
            step(last)

            for l in range(LEVELS):
                half = (P // 2) >> l
                pairs = HR * SEQ // (2 * half)
                c3 = cum.rearrange("p (n s) -> p n s", s=2 * half)
                e3 = ex.rearrange("p (n s) -> p n s", s=2 * half)
                x3 = (x0, x1)[l % 2].rearrange("p (n s) -> p n s", s=2 * half)
                q3 = rec_q.rearrange("p (n s) -> p n s", s=2 * half)
                k3 = rec_k.rearrange("p (n s) -> p n s", s=2 * half)
                if l:
                    dve.wait_ge(x_ready, l)
                V.tensor_tensor(e3, c3, c3[:, :, half - 1:half].broadcast_to([P, pairs, 2 * half]), ALU.subtract)\
                    .then_inc(d_done, 1)
                if l:
                    copy_level(l - 1)
                dve.wait_ge(ex_done, l + 1)
                V.tensor_tensor(x3[:, :, half:], e3[:, :, half:], q3[:, :, half:], ALU.mult)
                V.tensor_tensor(x3[:, :, 0:half], e3[:, :, 0:half], k3[:, :, 0:half], ALU.mult).then_inc(x_ready, 1)
                if l == 3:
                    rope_k()
            for l in (LEVELS - 1, LEVELS):
                copy_level(l)
            dve.wait_ge(a_free, A_END["aq"])
            step(V.tensor_tensor(qT, raw[:, :, NM:T], cosT[:, NM:T].unsqueeze(1).broadcast_to([P, HA, SEQ]), ALU.mult))
            for i in range(HA):
                ps = bank()
                step(V.tensor_tensor(St, ps[:, 0:SEQ], sinT[:, NM:T], ALU.mult))
                emptied(V.tensor_tensor(qT[:, i, :], qT[:, i, :], St, ALU.add))

            def take_scores(n):
                b = UNITS[n][0]
                nk, dl = NM + P * (b + 1), NM + P * b
                e = es[:, n % 2, :, :]
                if n >= 2:
                    dve.wait_ge(wt_ready, n - 1)
                lo = NM if b == NB - 1 else 0
                for part in range(2):
                    ps = bank()
                    V.tensor_copy(e[:, part, lo:dl], ps[:, 0:dl - lo])
                    emptied(V.tensor_tensor(e[:, part, dl:nk], ps[:, dl - lo:nk - lo], tri, ALU.add))
                for part in range(2 if lo else 0):
                    emptied(V.tensor_copy(e[:, part, 0:NM], bank()[:, 0:NM]))
                step(V.tensor_reduce(mx[:, n % 2, :], e[:, :, 0:nk], AXX, ALU.max))
                V.tensor_scalar(nm[:, n % 2, :], mx[:, n % 2, :], -(DH ** -0.5), None, ALU.mult).then_inc(mx_done, 1)

            def weigh(n):
                b = UNITS[n][0]
                nk, e, q = NM + P * (b + 1), es[:, n % 2, :, :], n % 2
                dve.wait_ge(e_done, n + 1)
                step(V.reciprocal(rr[:, q, :], rsum[:, q, :]))
                step(V.tensor_scalar(rr[:, q, 1:2], rr[:, q, 1:2], lam, -1.0, ALU.mult, ALU.mult))
                if n >= 2:
                    dve.wait_ge(a_free, A_END[f"wt{(n - 2) // HA}{(n - 2) % HA}"])
                step(V.tensor_scalar(e[:, 0, 0:nk], e[:, 0, 0:nk], rr[:, q, 0:1], None, ALU.mult))
                V.scalar_tensor_tensor(wts[:, q, 0:nk], e[:, 1, 0:nk], rr[:, q, 1:2], e[:, 0, 0:nk],
                                       ALU.mult, ALU.add).then_inc(wt_ready, 1)

            def take_state(b):
                ps = bank()
                if b is None:
                    dve.wait_ge(kd_ready, 2)
                    V.tensor_copy(S, ps[:, :]).then_inc(s_ready, 1)
                    dve.wait_ge(s_ready, 1)
                else:
                    dve.wait_ge(a_full, A_END[f"ro{b}"])
                    elb = el[:, 0:16].rearrange("p (h b) -> p h b", b=NB)[:, :, b:b + 1].broadcast_to([P, HR, P])
                    step(V.tensor_tensor(cut(S, HR, P), cut(S, HR, P), elb, ALU.mult))
                    V.tensor_tensor(S, S, ps[:, :], ALU.add).then_inc(s_ready, 1)
                    dve.wait_ge(s_ready, b + 2)
                emptied(V.tensor_copy(St[:, 1:2], ps[:, 0:1]))

            take_scores(0)
            for n in range(len(UNITS)):
                if n + 1 < len(UNITS):
                    take_scores(n + 1)
                weigh(n)
                if n == 0:
                    c3 = cum.rearrange("p (n s) -> p n s", s=P)
                    cm3 = cum_meta.rearrange("p (n s) -> p n s", s=NM)
                    V.tensor_tensor(cut(g_meta, HR, NM), cm3[:, :, NM - 1:NM].broadcast_to([P, HR, NM]), cm3, ALU.subtract)
                    V.tensor_tensor(ex.rearrange("p (n s) -> p n s", s=P), c3[:, :, P - 1:P].broadcast_to([P, HR * NB, P]),
                                    c3, ALU.subtract).then_inc(d_done, 1)
                if n == 1:
                    dve.wait_ge(ex_done, LEVELS + 1)
                    V.tensor_tensor(rec_k_meta[:, 0:HR * NM], rec_k_meta[:, 0:HR * NM], g_meta, ALU.mult)
                    V.tensor_tensor(rec_k, rec_k, ex, ALU.mult).then_inc(kd_ready, 1)
                if n == 2:
                    V.tensor_tensor(rec_q, rec_q, x0, ALU.mult).then_inc(kd_ready, 1)
                if n in STATE_JOBS:
                    take_state(STATE_AT[n])
            for k, (rows, end) in enumerate(((o_att, "o33"), (o_rec, "ro3"))):
                dve.wait_ge(a_free, A_END[end])
                flat = (o_att, o_rec)[k].rearrange("p b n -> p (b n)")
                step(V.tensor_tensor(cum, flat, flat, ALU.mult))
                step(V.tensor_reduce(ss[:, 0:16], cut(cum, 16, P), AXX, ALU.add))
                mean_root(2 + k, slice(0, 16), P)
                if k == 0:
                    step(V.tensor_scalar(rs[:, 0:16], rs[:, 0:16], 1.0 - LAM0, None, ALU.mult))
                last = V.tensor_tensor(cut(flat, 16, P), cut(flat, 16, P), rs[:, 0:16].unsqueeze(2).broadcast_to([P, 16, P]),
                                       ALU.mult)
                if k == 1:
                    dve.wait_ge(rg_done, 1)
                    step(last)
                    last = V.tensor_tensor(o_rec, o_rec, rec_gate, ALU.mult)
                last.then_inc(mixrows, 1)
                dve.wait_ge(mixrows, k + 1)
            for k in range(2):
                for b in range(NB):
                    ps = cut(bank()[:, :], 4, P)
                    wgt = recw.unsqueeze(2).broadcast_to([P, 4, P]) if k else sublnw.unsqueeze(2).broadcast_to([P, 4, P])
                    emptied(V.tensor_tensor(mixT[:, 4 * k:4 * k + 4, P * b:P * (b + 1)], ps, wgt, ALU.mult))
            for b in range(NB):
                for j in range(2):
                    emptied(V.tensor_tensor(h[:, b, W * j:W * (j + 1)], h[:, b, W * j:W * (j + 1)], bank()[:, :], ALU.add))
                dve.wait_ge(sq_done, 2 + b)
                mean_root(4 + b, slice(b, b + 1), D)
                if b == 0:
                    dve.wait_ge(ld_p, LOADED_P)
                V.scalar_tensor_tensor(xn[:, b, :], h[:, b, :], rs[:, b:b + 1], ffnw, ALU.mult, ALU.mult)\
                    .then_inc(xn_done, 1)
            dve.wait_ge(xn_done, NB)

            def best_keys(it, g):
                step(V.tensor_copy(rows2.rearrange("p a k -> p (a k)"),
                                   sc_flat[:, bass.ds(it * (2 * NK) + g * 2 * NK, 2 * NK)]), it)
                V.max(sv[:, 0, 0:8], rows2[:, 0, :])
                step(V.max(sv[:, 1, 0:8], rows2[:, 1, :]), it)
                for a in range(2):
                    V.max_index(si[:, a, 0:8], sv[:, a, 0:8], rows2[:, a, :])
                    last = V.match_replace(s2[:, a, :], sv[:, a, 0:8], rows2[:, a, :], FMIN)
                step(last, it)
                V.max(sv[:, 0, 8:16], s2[:, 0, :])
                step(V.max(sv[:, 1, 8:16], s2[:, 1, :]), it)
                V.max_index(si[:, 0, 8:16], sv[:, 0, 8:16], s2[:, 0, :])
                step(V.max_index(si[:, 1, 8:16], sv[:, 1, 8:16], s2[:, 1, :]), it)

            def best_sums(it, g):
                V.tensor_copy(sif, si)
                step(V.tensor_tensor(cut(cand, TOP, TOP), sv[:, 0, :].unsqueeze(2).broadcast_to([P, TOP, TOP]),
                                     sv[:, 1, :].unsqueeze(1).broadcast_to([P, TOP, TOP]), ALU.add), it)
                step(V.max(top_s[:, 0:8], cand), it)
                V.max_index(pos[:, 0:8], top_s[:, 0:8], cand)
                step(V.match_replace(c2, top_s[:, 0:8], cand, FMIN), it)
                step(V.max(top_s[:, 8:16], c2), it)
                step(V.max_index(pos[:, 8:16], top_s[:, 8:16], c2), it)
                V.tensor_scalar(gate[:, bass.ds(it * TOP + g * TOP, TOP)], top_s, top_s[:, 0:1], None,
                                ALU.subtract).then_inc(gmax, 1)
                dve.wait_ge(gmax, it + (g + 1))
                V.nop(nofuse=True)

            def experts(it, g):
                V.tensor_scalar(pi[:, 0, :], pos, 4, None, ALU.logical_shift_right)
                step(V.tensor_scalar(pi[:, 1, :], pos, TOP - 1, None, ALU.bitwise_and), it)
                dims = [P, 2, TOP, TOP]
                step(V.tensor_tensor(oh, pi.unsqueeze(3).broadcast_to(dims),
                                     iota.unsqueeze(1).unsqueeze(1).broadcast_to(dims), ALU.is_equal), it)
                step(V.tensor_tensor(oh, oh, sif.unsqueeze(2).broadcast_to(dims), ALU.mult), it)
                step(V.tensor_reduce(e01, oh, AXX, ALU.add), it)
                V.scalar_tensor_tensor(expert_ids[:, bass.ds(it * TOP + g * TOP, TOP)], e01[:, 0, :],
                                       float(NK), e01[:, 1, :], ALU.mult, ALU.add).then_inc(idx_ready, 1)
                dve.wait_ge(idx_ready, it + (g + 1))
                V.nop(nofuse=True)

            dve.wait_ge(a_free, A_END["sc0"])
            with dve.Fori(0, LEAD) as it:
                best_keys(it, 0)
                best_sums(it, 0)
                experts(it, 0)
            own[0] += HEAD_STEPS * (LEAD - 1)
            V.memset(zero, 0.0).then_inc(v_free, 2 * RING)
            V.memset(d8, 0.0).then_inc(u_free, RING)
            dve.wait_ge(u_free, RING)

            def expert_heads(b, first, count, u=True, v=True):
                g = b * HP + first
                ahead = u and g + LEAD < HEADS
                with dve.Fori(0, count) as it:
                    if v:
                        gates = gate[:, bass.ds(it * TOP + (g - LAG) * TOP, TOP)]
                        weight = dots[:, bass.ds(it * TOP + (g - LAG) * TOP, TOP)]
                        dve.wait_ge(gexp, it + (g - LAG + 1))
                        V.tensor_reduce(gsum[:, 0:1], gates, AXX, ALU.add).then_inc(hid_done, 1)
                        dve.wait_ge(hid_done, it * 3 + (3 * (g - LAG) + 1))
                        V.reciprocal(gsum[:, 1:2], gsum[:, 0:1]).then_inc(hid_done, 1)
                        dve.wait_ge(hid_done, it * 3 + (3 * (g - LAG) + 2))
                        V.nop(nofuse=True)
                        dve.wait_ge(hid_ready, it + (g - LAG + 1))
                        V.scalar_tensor_tensor(weight, weight, gsum[:, 1:2], gates, ALU.mult, ALU.mult)\
                            .then_inc(hid_done, 1)
                        dve.wait_ge(hid_done, it * 3 + (3 * (g - LAG) + 3))
                    for turn in range(2):
                        if v:
                            dve.wait_ge(v_free, it * (2 * RING) + (RING + (g - LAG) * TOP + turn * RING))
                            V.tensor_tensor(dg[:, turn, :, :], ident.unsqueeze(1).broadcast_to([P, RING, P]),
                                            dots[:, bass.ds(it * TOP + (g - LAG) * TOP + turn * RING, RING)].unsqueeze(2)
                                            .broadcast_to([P, RING, P]), ALU.mult).then_inc(dg_ready, 1)
                        for s in range(RING if u else 0):
                            dve.wait_ge(u_full[s], it * 32 + (32 * g + 16 * turn + 16))
                            V.tensor_tensor_reduce(u_rows[:, s, :], u_rows[:, s, :], xn[:, b, :], 1.0, 0.0, ALU.mult, ALU.add,
                                                   d8[:, s:s + 1]).then_inc(u_free, 1)
                            if ahead and (turn, s) == (0, 5):
                                best_keys(it, g + LEAD)
                            elif ahead and (turn, s) == (1, 2):
                                best_sums(it, g + LEAD)
                            elif ahead and (turn, s) == (1, 6):
                                experts(it, g + LEAD)
                        if u:
                            dve.wait_ge(u_free, it * (2 * RING) + (RING + g * TOP + (turn + 1) * RING))
                            V.tensor_copy(dots[:, bass.ds(it * TOP + g * TOP + turn * RING, RING)], d8)\
                                .then_inc(dots_ready, 1)
                            dve.wait_ge(dots_ready, it * 2 + (2 * g + turn + 1))
                if ahead:
                    own[0] += HEAD_STEPS * (count - 1)

            def take_sums(b):
                dve.wait_ge(y_full, b + 1)
                y = psum_a if b % 2 else psum_c
                for c in range(2):
                    last = V.tensor_copy(h[:, b, W * c:W * (c + 1)], y[c][:, :])
                last.then_inc(y_free, 1)

            def first_norm(b):
                dve.wait_ge(sq_done, 6 + 2 * b)
                mean_root(8 + 2 * b, slice(b, b + 1), D)
                if b == 0:
                    dve.wait_ge(ld_p, LOADED_P + 16)
                V.scalar_tensor_tensor(h[:, b, :], h[:, b, :], rs[:, b:b + 1], finw1, ALU.mult, ALU.mult)\
                    .then_inc(h1_done, 1)

            def second_norm(b):
                dve.wait_ge(sq_done, 7 + 2 * b)
                mean_root(9 + 2 * b, slice(4 + b, 5 + b), D)

            def transposed_rows(jobs):
                for job in jobs:
                    b, g = job // 2, job % 2
                    emptied(V.tensor_tensor(hT[:, 4 * g:4 * g + 4, P * b:P * (b + 1)], cut(bank()[:, :], 4, P),
                                            normg2[:, 4 * g:4 * g + 4].unsqueeze(2).broadcast_to([P, 4, P]), ALU.mult))

            dve.wait_ge(a_free, A_END["sc1"])
            expert_heads(0, 0, 1, v=False)
            dve.wait_ge(a_free, A_END["sc3"])
            expert_heads(0, 1, LAG - 1, v=False)
            dve.wait_ge(a_free, A_END["sr3"])
            expert_heads(0, LAG, HP - LAG)
            for b in range(1, NB):
                expert_heads(b, 0, HP if b < NB - 1 else HP - LEAD)
                if b == NB - 1:
                    expert_heads(b, HP - LEAD, LEAD)
                take_sums(b - 1)
                first_norm(b - 1)
                second_norm(b - 1)
            expert_heads(NB, 0, LAG, u=False)
            take_sums(NB - 1)
            transposed_rows(range(0, 3))
            first_norm(NB - 1)
            transposed_rows(range(3, 6))
            second_norm(NB - 1)
            transposed_rows(range(6, 8))
            dve.wait_ge(ld_q, LOADED_Q)
            V.memset(wsT[GC:P, :, 0:GC], 0.0)
            step(V.memset(ones, 1.0))
            vflat = vb.rearrange("p b n -> p (b n)")
            NGB = NB * NG
            v3 = cut(vflat, NGB, GC)
            c3 = cut(vc, NGB, GC)

            def layer_norm(part):
                if part == 0:
                    dve.wait_ge(fn_done, 1)
                    step(V.tensor_reduce(gst[:, 0, :], v3, AXX, ALU.add))
                    step(V.tensor_scalar(gst[:, 0, :], gst[:, 0, :], 1.0 / GC, None, ALU.mult))
                    step(V.tensor_tensor(c3, v3, gst[:, 0, :].unsqueeze(2).broadcast_to([P, NGB, GC]), ALU.subtract))
                elif part == 1:
                    step(V.tensor_tensor(vq, vc, vc, ALU.mult))
                    step(V.tensor_reduce(gst[:, 1, :], cut(vq, NGB, GC), AXX, ALU.add))
                    V.tensor_scalar(gst[:, 1, :], gst[:, 1, :], 1.0 / GC, EPS, ALU.mult, ALU.add).then_inc(ln_r, 1)
                elif part == 2:
                    dve.wait_ge(ln_rt, 1)
                    step(V.reciprocal(gst[:, 3, :], gst[:, 2, :]))
                    step(V.tensor_tensor(c3, c3, gst[:, 3, :].unsqueeze(2).broadcast_to([P, NGB, GC]), ALU.mult))
                else:
                    step(V.tensor_tensor(cut(vc, NB, W), cut(vc, NB, W), lng.unsqueeze(1).broadcast_to([P, NB, W]),
                                         ALU.mult))
                    V.tensor_tensor(vb, cut(vc, NB, W), lnb.unsqueeze(1).broadcast_to([P, NB, W]), ALU.add)\
                        .then_inc(ln_v, 1)

            def spatial_rows(b):
                ps = bank()
                step(V.tensor_tensor(cut(up_t, NG, GC), cut(ps[:, :], NG, GC), bs.unsqueeze(2).broadcast_to([P, NG, GC]),
                                     ALU.add))
                step(V.tensor_tensor(up_t, up_t, ub[:, b, :], ALU.mult))
                emptied(V.tensor_tensor(vb[:, b, :], up_t, zb[:, b, :], ALU.mult))

            def take_z(n):
                b = UNITS2[n][0]
                z = zs[:, n % 2, :]
                ps = bank()
                if n >= 2:
                    dve.wait_ge(w_ready, n - 1)
                if b:
                    V.tensor_copy(z[:, 0:P * b], ps[:, 0:P * b])
                emptied(V.tensor_tensor(z[:, P * b:P * (b + 1)], ps[:, P * b:P * (b + 1)], stri, ALU.add))
                V.tensor_copy(softplus[:, n % 2, 0:1], z[:, 0:1]).then_inc(zs_ready, 1)

            def log_weights(n):
                nk = P * (UNITS2[n][0] + 1)
                z, soft = zs[:, n % 2, 0:nk], softplus[:, n % 2, 0:nk]
                dve.wait_ge(l_ready, n + 1)
                step(V.scalar_tensor_tensor(soft, z, 0.0, ae[:, n % 2, 0:nk], ALU.max, ALU.add))
                step(V.tensor_tensor_scan(rcs[:, 0:nk][:, ::-1], ones[:, 0:nk], soft[:, ::-1], 0.0, ALU.mult, ALU.add))
                V.tensor_tensor(z, z, rcs[:, 0:nk], ALU.subtract).then_inc(wl_ready, 1)

            take_z(0)
            for n in range(len(UNITS2)):
                log_weights(n)
                if n + 1 < len(UNITS2):
                    take_z(n + 1)
                if 2 * NB <= n < 2 * NB + 2:
                    layer_norm(n - 2 * NB)
                if 2 * NB + 3 <= n < 2 * NB + 5:
                    layer_norm(n - 2 * NB - 1)
                if n in SGU_AT:
                    if SGU_AT[n] == 0:
                        dve.wait_ge(fn_done, 2)
                    spatial_rows(SGU_AT[n])
                if n == len(UNITS2) - 3:
                    dve.wait_ge(a_free, A_END[f"o2_{3 * H2 - 1}"])
                    V.tensor_tensor(o2[:, 0:3, :], o2[:, 0:3, :], za[:, 0:3, :], ALU.mult).then_inc(y_ready, 1)
            dve.wait_ge(a_free, A_END[f"o2_{len(UNITS2) - 1}"])
            V.tensor_tensor(o2[:, 3, :], o2[:, 3, :], za[:, 3, :], ALU.mult).then_inc(y_ready, 1)
            dve.wait_ge(y_ready, 2)
            dve.wait_ge(fn_done, 3)
            for j in range(2):
                for b in range(NB):
                    gg, gh = ga[:, b, W * j:W * (j + 1)], gb[:, b, W * j:W * (j + 1)]
                    emptied(V.tensor_tensor(gg, gg, bank()[:, :], ALU.mult))
                    step(V.tensor_tensor(gh, gh, bank()[:, :], ALU.mult))
                    emptied(V.tensor_tensor(gg, gg, gh, ALU.add))
            for j in range(2):
                for b in range(NB):
                    emptied(V.tensor_tensor(h[:, b, W * j:W * (j + 1)], h[:, b, W * j:W * (j + 1)], bank()[:, :], ALU.add))
            dve.wait_ge(sq_done, 14)
            mean_root(16, slice(0, NB), D)
            for b in range(NB):
                V.scalar_tensor_tensor(h[:, b, :], h[:, b, :], rs[:, b:b + 1], finw, ALU.mult, ALU.mult)\
                    .then_inc(fin_ready, 1)

        @block.gpsimd
        def _(pool):
            steps = [0]

            def gather_heads(count, u, v):
                per = (u is not None) + (v is not None)
                with pool.Fori(0, count) as it:
                    if u is not None:
                        pool.wait_ge(idx_ready, it + (u + 1))
                        nc.gpsimd.nop(nofuse=True)
                    for turn in range(2):
                        at = it * TOP + turn * RING
                        if u is not None:
                            nc.gpsimd.tensor_copy(u_ids[:, turn, :], expert_ids[:, bass.ds(at + u * TOP, RING)])\
                                .then_inc(pool_s, 1)
                        if v is not None:
                            nc.gpsimd.tensor_copy(v_ids[:, turn, :], expert_ids[:, bass.ds(at + v * TOP, RING)])\
                                .then_inc(pool_s, 1)
                        pool.wait_ge(pool_s, it * (2 * per) + (steps[0] + per * (turn + 1)))
                        nc.gpsimd.nop(nofuse=True)
                        for s in range(RING):
                            if u is not None:
                                pool.wait_ge(u_free, it * TOP + (u * TOP + turn * RING + s + 1))
                                nc.gpsimd.nop(nofuse=True)
                                nc.gpsimd.indirect_dma_start(u_rows[:, s, :], None, t["peer_u"], bass.IndirectOffsetOnAxis(
                                    ap=u_ids[:, turn, s:s + 1].bitcast(U32), axis=0)).then_inc(u_full[s], 16)
                            if v is not None:
                                pool.wait_ge(v_free, it * TOP + (RING + v * TOP + turn * RING + s + 1))
                                nc.gpsimd.nop(nofuse=True)
                                nc.gpsimd.indirect_dma_start(v_rows[:, s, :], None, t["peer_v"], bass.IndirectOffsetOnAxis(
                                    ap=v_ids[:, turn, s:s + 1].bitcast(U32), axis=0)).then_inc(v_full[s], 16)
                steps[0] += 2 * per * count

            gather_heads(LAG, 0, None)
            gather_heads(HEADS - LAG, LAG, 0)
            gather_heads(LAG, None, HEADS - LAG)


def word(ap):
    return ap.offset


def shape_constants():
    d = 2 * (np.arange(DH // 2, dtype=np.float32))
    inv = (np.float32(10000.0) ** (-d / np.float32(DH))).astype(np.float32)
    ang = np.arange(T, dtype=np.float32)[:, None] * inv[None, :]
    ang = np.concatenate([ang, ang], axis=-1)
    cos, sin = np.cos(ang).T.astype(np.float32), np.sin(ang).T.astype(np.float32)
    rot = np.zeros((P, P), np.float32)
    half = DH // 2
    for part in range(2):
        for i in range(half):
            rot[DH * part + half + i, DH * part + i] = -1.0
            rot[DH * part + i, DH * part + half + i] = 1.0
    s, q = np.arange(P)[:, None], np.arange(P)[None, :]
    masks = []
    for l in range(LEVELS):
        hf = (P // 2) >> l
        masks.append((s // (2 * hf) == q // (2 * hf)) & (s % (2 * hf) < hf) & (q % (2 * hf) >= hf))
    masks.append(s == q)
    return {
        "ident": np.eye(P, dtype=np.float32),
        "cosT": np.concatenate([cos, cos], 0), "sinT": np.concatenate([sin, sin], 0), "rotm": rot,
        "masks": np.ascontiguousarray(np.stack(masks, 1).astype(np.int32)),
        "tri": np.where(q <= s, 0.0, NEG).astype(np.float32),
        "stri": np.where(q < s, 0.0, NEG).astype(np.float32),
        "iota": np.ascontiguousarray(np.broadcast_to(np.arange(TOP, dtype=np.float32), (P, TOP))),
    }


def kernel(**inputs):
    import numpy as _np
    import concourse.bacc as _bacc
    from concourse.bass_utils import run_bass_kernel_spmd as _run

    i = {k: _np.asarray(v) for k, v in inputs.items()}
    c = _np.ascontiguousarray
    rep = lambda a: c(_np.broadcast_to(a, (P,) + a.shape))
    arrays = {
        "x": i["x"][0], "meta": i["meta_tokens"], "w_in": i["w_in"][0], "w_out": i["w_out"][0],
        "wq": i["peer_w_query"][0], "peer_u": i["peer_u"][0], "peer_v": i["peer_v"][0],
        "w_in_2": i["w_in_2"][0], "w_up_a": i["w_up_a_2"][0], "w_up_b": i["w_up_b_2"][0], "w_out_2": i["w_out_2"][0],
        "normw": c(i["mix_norm_w"].reshape(KT, P).T), "normg2": c(i["norm_g_2"].reshape(KT, P).T),
        "sublnw": c(i["diff_subln_w"].reshape(P, 1)), "recw": c(i["rec_norm_w"].reshape(HR, P).T),
        "lam_in": rep(_np.stack([i["diff_lambda_q1"][0], i["diff_lambda_k1"][0],
                                 i["diff_lambda_q2"][0], i["diff_lambda_k2"][0]])),
        "lblog": c(i["rec_lb_logits"].reshape(2, HR, P).transpose(2, 0, 1)),
        "skT": c(i["peer_subkeys"].reshape(2 * HP, NK, P).transpose(2, 0, 1)),
        "ffnw": i["ffn_norm_w"], "finw": i["final_norm_g_2"].reshape(1, D),
        "lng": i["sgu_ln_g_2"].reshape(1, W), "lnb": i["sgu_ln_b_2"].reshape(1, W),
        "wsT": c(i["w_spatial_2"][0].transpose(2, 0, 1)), "bs": c(i["b_spatial_2"][0].T),
    }
    arrays.update(shape_constants())
    arrays["finw1"] = i["final_norm_w"].reshape(1, D)
    nc = _bacc.Bacc("TRN2", target_bir_lowering=False, num_devices=1)
    t, feed = {}, {}
    for name, a in arrays.items():
        a = c(a)
        feed[f"in_{name}"] = a
        t[name] = nc.dram_tensor(f"in_{name}", a.shape, mybir.dt.from_np(a.dtype), kind="ExternalInput").ap()
    out = nc.dram_tensor("out_0", (SEQ, D), F32, kind="ExternalOutput").ap()
    build(nc, t, out)
    r = _run(nc, [feed], core_ids=[0])
    return r.results[0]["out_0"].reshape(1, SEQ, D)
```
